# Optimizing a Trainium2 kernel written in Bass

```python
import math
import jax
import jax.numpy as jnp
from jax import lax
import numpy as np
import jax, jax.numpy as jnp

D_MODEL = 2048
BATCH = 1
SEQ = 256
DEPTH = 1

N_MIXERS = 2
N_META = 16
CONV_WIDTH = 31
HEAD_DIM = 64
N_HEADS = D_MODEL // HEAD_DIM
N_KV_HEADS = N_HEADS // 8
GROUP = N_HEADS // N_KV_HEADS
WINDOW = 128
BLOCK = 128
N_BUCKETS = 32
MAX_DISTANCE = 128
D_FF = ((8 * D_MODEL + 3 * 256 - 1) // (3 * 256)) * 256
QKV_WIDTH = (N_HEADS + 2 * N_KV_HEADS) * HEAD_DIM
RMS_EPS = 1e-6
LN_EPS = 1e-5
NEG_INF = -1e30


def rms_norm(x, g):
    xf = x.astype(jnp.float32)
    y = xf * lax.rsqrt(jnp.mean(xf * xf, axis=-1, keepdims=True) + RMS_EPS)
    return (y * g.astype(jnp.float32)).astype(x.dtype)

def layer_norm(x, g, b):
    xf = x.astype(jnp.float32)
    mu = jnp.mean(xf, axis=-1, keepdims=True)
    var = jnp.mean(jnp.square(xf - mu), axis=-1, keepdims=True)
    y = (xf - mu) * lax.rsqrt(var + LN_EPS)
    return (y * g.astype(jnp.float32) + b.astype(jnp.float32)).astype(x.dtype)

def t5_bucket(dist):
    max_exact = N_BUCKETS // 2
    d = jnp.maximum(dist, max_exact).astype(jnp.float32)
    large = max_exact + (jnp.log(d / max_exact) / math.log(MAX_DISTANCE / max_exact)
                         * (N_BUCKETS - max_exact)).astype(jnp.int32)
    return jnp.where(dist < max_exact, dist, jnp.minimum(large, N_BUCKETS - 1))

def rel_bias_lookup(rel_bias, dist):
    b = rel_bias.astype(jnp.float32)[t5_bucket(dist)]
    b = jnp.moveaxis(b, -1, -3)
    return b.reshape(b.shape[:-3] + (N_KV_HEADS, GROUP) + b.shape[-2:])

def sink_softmax(scores, sinks):
    sink = jnp.broadcast_to(sinks[None, :, :, None, None], scores.shape[:-1] + (1,))
    p = jax.nn.softmax(jnp.concatenate([scores, sink], axis=-1), axis=-1)
    return p[..., :-1]

def conformer_conv(h, w_in, b_in, w_dw, b_dw, ln_g, ln_b, w_out, b_out):
    u = h @ w_in + b_in
    a, g = jnp.split(u, 2, axis=-1)
    u = a * jax.nn.sigmoid(g)
    u = jnp.pad(u, ((0, 0), (CONV_WIDTH - 1, 0), (0, 0)))
    u = lax.conv_general_dilated(
        u, w_dw[:, None, :].astype(u.dtype), window_strides=(1,), padding='VALID',
        dimension_numbers=('NWC', 'WIO', 'NWC'), feature_group_count=D_MODEL) + b_dw
    u = layer_norm(u, ln_g, ln_b)
    u = jax.nn.silu(u)
    return u @ w_out + b_out

def sliding_window_sink_attention(h, w_qkv, b_qkv, sinks, w_o, b_o, rel_bias):
    B, L, _ = h.shape
    S = L - N_META
    n_blk = S // BLOCK
    qkv = h @ w_qkv + b_qkv
    q, k, v = jnp.split(qkv, [N_HEADS * HEAD_DIM, (N_HEADS + N_KV_HEADS) * HEAD_DIM], axis=-1)
    q = q.reshape(B, L, N_KV_HEADS, GROUP, HEAD_DIM) * (HEAD_DIM ** -0.5)
    k = k.reshape(B, L, N_KV_HEADS, HEAD_DIM)
    v = v.reshape(B, L, N_KV_HEADS, HEAD_DIM)
    sink_logits = sinks.astype(jnp.float32).reshape(N_KV_HEADS, GROUP)
    q_m, q_r = q[:, :N_META], q[:, N_META:]
    k_m, k_r = k[:, :N_META], k[:, N_META:]
    v_m, v_r = v[:, :N_META], v[:, N_META:]

    d_mm = jnp.arange(N_META)[:, None] - jnp.arange(N_META)[None, :]
    s_mm = (jnp.einsum('bqhgd,bkhd->bhgqk', q_m, k_m).astype(jnp.float32)
            + rel_bias_lookup(rel_bias, jnp.maximum(d_mm, 0)))
    s_mm = jnp.where(d_mm >= 0, s_mm, NEG_INF)
    p_mm = sink_softmax(s_mm, sink_logits).astype(v.dtype)
    o_m = jnp.einsum('bhgqk,bkhd->bqhgd', p_mm, v_m)

    pad = ((0, 0), (BLOCK, 0), (0, 0), (0, 0))
    k_p = jnp.pad(k_r, pad).reshape(B, n_blk + 1, BLOCK, N_KV_HEADS, HEAD_DIM)
    v_p = jnp.pad(v_r, pad).reshape(B, n_blk + 1, BLOCK, N_KV_HEADS, HEAD_DIM)
    k_band = jnp.concatenate([k_p[:, :-1], k_p[:, 1:]], axis=2)
    v_band = jnp.concatenate([v_p[:, :-1], v_p[:, 1:]], axis=2)
    q_blk = q_r.reshape(B, n_blk, BLOCK, N_KV_HEADS, GROUP, HEAD_DIM)

    qpos = jnp.arange(BLOCK)[:, None]
    kpos = jnp.arange(2 * BLOCK)[None, :]
    mpos = jnp.arange(N_META)[None, :]
    d_band = BLOCK + qpos - kpos
    in_window = (d_band >= 0) & (d_band < WINDOW)
    bias_band = rel_bias_lookup(rel_bias, jnp.maximum(d_band, 0))

    def block_fn(args):
        n, q_n, k_n, v_n = args
        valid = in_window & (n * BLOCK + kpos >= BLOCK)
        d_meta = N_META + n * BLOCK + qpos - mpos
        s_meta = (jnp.einsum('bqhgd,bmhd->bhgqm', q_n, k_m).astype(jnp.float32)
                  + rel_bias_lookup(rel_bias, d_meta))
        s_band = jnp.einsum('bqhgd,bjhd->bhgqj', q_n, k_n).astype(jnp.float32) + bias_band
        s_band = jnp.where(valid, s_band, NEG_INF)
        p = sink_softmax(jnp.concatenate([s_meta, s_band], axis=-1), sink_logits).astype(v_n.dtype)
        return (jnp.einsum('bhgqm,bmhd->bqhgd', p[..., :N_META], v_m)
                + jnp.einsum('bhgqj,bjhd->bqhgd', p[..., N_META:], v_n))

    xs = (jnp.arange(n_blk, dtype=jnp.int32), jnp.moveaxis(q_blk, 1, 0),
          jnp.moveaxis(k_band, 1, 0), jnp.moveaxis(v_band, 1, 0))
    o_r = lax.map(block_fn, xs)
    o_r = jnp.moveaxis(o_r, 0, 1).reshape(B, S, N_HEADS * HEAD_DIM)
    o = jnp.concatenate([o_m.reshape(B, N_META, N_HEADS * HEAD_DIM), o_r], axis=1)
    return o @ w_o + b_o

def swiglu(h, w_gate, w_up, w_down):
    return (jax.nn.silu(h @ w_gate) * (h @ w_up)) @ w_down

def first_inputs(seed: int = 0) -> dict:
    key = jax.random.key(seed)
    ks = list(jax.random.split(key, 24))
    n_conv = len(range(0, DEPTH, N_MIXERS))
    n_attn = len(range(1, DEPTH, N_MIXERS))
    D, F, H = D_MODEL, D_FF, N_HEADS * HEAD_DIM

    def nrm(k, shape, scale):
        return jax.random.normal(k, shape, jnp.float32) * scale

    def gain(k, shape):
        return 1.0 + nrm(k, shape, 0.02)

    return {
        'x': nrm(ks[0], (BATCH, SEQ, D), 1.0),
        'meta_tokens': nrm(ks[1], (N_META, D), 1.0),
        'rel_bias': nrm(ks[2], (N_BUCKETS, N_HEADS), 0.5),
        'conv_w_in': nrm(ks[3], (n_conv, D, 2 * D), D ** -0.5),
        'conv_b_in': nrm(ks[4], (n_conv, 2 * D), 0.02),
        'conv_w_dw': nrm(ks[5], (n_conv, CONV_WIDTH, D), CONV_WIDTH ** -0.5),
        'conv_b_dw': nrm(ks[6], (n_conv, D), 0.02),
        'conv_ln_g': gain(ks[7], (n_conv, D)),
        'conv_ln_b': nrm(ks[8], (n_conv, D), 0.02),
        'conv_w_out': nrm(ks[9], (n_conv, D, D), D ** -0.5),
        'conv_b_out': nrm(ks[10], (n_conv, D), 0.02),
        'attn_w_qkv': nrm(ks[11], (n_attn, D, QKV_WIDTH), D ** -0.5),
        'attn_b_qkv': nrm(ks[12], (n_attn, QKV_WIDTH), 0.02),
        'attn_sinks': nrm(ks[13], (n_attn, N_HEADS), 0.5),
        'attn_w_o': nrm(ks[14], (n_attn, H, D), H ** -0.5),
        'attn_b_o': nrm(ks[15], (n_attn, D), 0.02),
        'norm_mix_pre': gain(ks[16], (DEPTH, D)),
        'norm_mix_post': gain(ks[17], (DEPTH, D)),
        'norm_ffn_pre': gain(ks[18], (DEPTH, D)),
        'norm_ffn_post': gain(ks[19], (DEPTH, D)),
        'ffn_w_gate': nrm(ks[20], (DEPTH, D, F), D ** -0.5),
        'ffn_w_up': nrm(ks[21], (DEPTH, D, F), D ** -0.5),
        'ffn_w_down': nrm(ks[22], (DEPTH, F, D), F ** -0.5),
    }

def first_block(x, meta_tokens, rel_bias, conv_w_in, conv_b_in, conv_w_dw, conv_b_dw,
              conv_ln_g, conv_ln_b, conv_w_out, conv_b_out, attn_w_qkv, attn_b_qkv,
              attn_sinks, attn_w_o, attn_b_o, norm_mix_pre, norm_mix_post,
              norm_ffn_pre, norm_ffn_post, ffn_w_gate, ffn_w_up, ffn_w_down):
    B = x.shape[0]
    meta = jnp.broadcast_to(meta_tokens.astype(x.dtype)[None], (B, N_META, D_MODEL))
    h = jnp.concatenate([meta, x], axis=1)
    for i in range(DEPTH):
        j = i // N_MIXERS
        u = rms_norm(h, norm_mix_pre[i])
        if i % N_MIXERS == 0:
            u = conformer_conv(u, conv_w_in[j], conv_b_in[j], conv_w_dw[j], conv_b_dw[j],
                               conv_ln_g[j], conv_ln_b[j], conv_w_out[j], conv_b_out[j])
        else:
            u = sliding_window_sink_attention(u, attn_w_qkv[j], attn_b_qkv[j], attn_sinks[j],
                                              attn_w_o[j], attn_b_o[j], rel_bias)
        h = h + rms_norm(u, norm_mix_post[i])
        u = swiglu(rms_norm(h, norm_ffn_pre[i]), ffn_w_gate[i], ffn_w_up[i], ffn_w_down[i])
        h = h + rms_norm(u, norm_ffn_post[i])
    return h[:, N_META:]


CHUNK = 64

FOX_HEADS = 8
FOX_HEAD_DIM = 128
FOX_WIDTH = FOX_HEADS * FOX_HEAD_DIM
Q_BLOCK = 128
FORGET_BIAS_INIT = 3.0

POOL_WINDOWS = (2, 4, 8, 16)
POOL_GROUPS = len(POOL_WINDOWS)
POOL_WIDTH = 1024
POOL_GROUP_DIM = POOL_WIDTH // POOL_GROUPS

N_BRANCHES = 2
IN_SPLITS = (
    FOX_WIDTH,
    2 * FOX_WIDTH,
    3 * FOX_WIDTH,
    3 * FOX_WIDTH + FOX_HEADS,
    3 * FOX_WIDTH + FOX_HEADS + POOL_WIDTH,
)
IN_COLS = 3 * FOX_WIDTH + FOX_HEADS + POOL_WIDTH + N_BRANCHES * D_MODEL

PEER_HEADS = 8
PEER_KEYS = 128
PEER_EXPERTS = PEER_KEYS * PEER_KEYS
PEER_QUERY_DIM = 256
PEER_HALF = PEER_QUERY_DIM // 2
PEER_TOPK = 16
PEER_TOKEN_BLOCK = 128


def rms_norm_2(x, g):
    xf = x.astype(jnp.float32)
    y = xf * lax.rsqrt(jnp.mean(xf * xf, axis=-1, keepdims=True) + RMS_EPS)
    return (y * g.astype(jnp.float32)).astype(x.dtype)

def forgetting_attention(q, k, v, log_f):
    seq = q.shape[2]
    c = jnp.cumsum(log_f, axis=-1)
    scale = FOX_HEAD_DIM ** -0.5
    outs = []
    for blk in range(seq // Q_BLOCK):
        q0 = blk * Q_BLOCK
        q1 = q0 + Q_BLOCK
        qb = q[:, :, q0:q1]
        kb = k[:, :, :q1]
        vb = v[:, :, :q1]
        logits = jnp.einsum('bhqd,bhkd->bhqk', qb, kb,
                            preferred_element_type=jnp.float32) * scale
        logits = logits + (c[:, :, q0:q1, None] - c[:, :, None, :q1])
        causal = jnp.arange(q0, q1)[:, None] >= jnp.arange(q1)[None, :]
        logits = jnp.where(causal, logits, -jnp.inf)
        p = jax.nn.softmax(logits, axis=-1)
        outs.append(jnp.einsum('bhqk,bhkd->bhqd', p.astype(v.dtype), vb))
    return jnp.concatenate(outs, axis=2)

def multiscale_pool(p, w_groups, scale):
    b, s, _ = p.shape
    pg = p.reshape(b, s, POOL_GROUPS, POOL_GROUP_DIM).astype(jnp.float32)
    csum = jnp.cumsum(pg, axis=1)
    pos = jnp.arange(s)
    outs = []
    for gi, w in enumerate(POOL_WINDOWS):
        cs = csum[:, :, gi]
        lagged = jnp.pad(cs, ((0, 0), (w, 0), (0, 0)))[:, :s]
        count = jnp.minimum(pos + 1, w).astype(jnp.float32)[None, :, None]
        outs.append((cs - lagged) / count - pg[:, :, gi])
    mixed = jnp.stack(outs, axis=2).astype(p.dtype)
    mixed = jnp.einsum('bsgc,gcd->bsgd', mixed, w_groups)
    return mixed.reshape(b, s, POOL_WIDTH) * scale

def peer(xn, w_query, sub_keys_1, sub_keys_2, expert_u, expert_v):
    b, s, d = xn.shape
    t = b * s
    xt = xn.reshape(t, d)
    q = (xt @ w_query).reshape(t, PEER_HEADS, PEER_QUERY_DIM).astype(jnp.float32)
    q1, q2 = q[..., :PEER_HALF], q[..., PEER_HALF:]
    s1 = jnp.einsum('thd,hkd->thk', q1, sub_keys_1.astype(jnp.float32))
    s2 = jnp.einsum('thd,hkd->thk', q2, sub_keys_2.astype(jnp.float32))
    v1, i1 = lax.top_k(s1, PEER_TOPK)
    v2, i2 = lax.top_k(s2, PEER_TOPK)
    cand = (v1[..., :, None] + v2[..., None, :]).reshape(t, PEER_HEADS, PEER_TOPK * PEER_TOPK)
    cand_idx = (i1[..., :, None] * PEER_KEYS + i2[..., None, :]).reshape(
        t, PEER_HEADS, PEER_TOPK * PEER_TOPK)
    top_s, top_pos = lax.top_k(cand, PEER_TOPK)
    expert_idx = jnp.take_along_axis(cand_idx, top_pos, axis=-1)
    gates = jax.nn.softmax(top_s, axis=-1).astype(xn.dtype)

    def token_block(args):
        xb, idx, g = args
        u = jnp.take(expert_u, idx, axis=0)
        a = jnp.einsum('thkd,td->thk', u, xb)
        hid = jax.nn.gelu(a) * g
        vsel = jnp.take(expert_v, idx, axis=0)
        return jnp.einsum('thk,thkd->td', hid, vsel)

    nb = t // PEER_TOKEN_BLOCK
    out = lax.map(token_block, (
        xt.reshape(nb, PEER_TOKEN_BLOCK, d),
        expert_idx.reshape(nb, PEER_TOKEN_BLOCK, PEER_HEADS, PEER_TOPK),
        gates.reshape(nb, PEER_TOKEN_BLOCK, PEER_HEADS, PEER_TOPK),
    ))
    return out.reshape(b, s, d)

def second_inputs(seed: int = 0) -> dict:
    key = jax.random.key(seed)
    ks = jax.random.split(key, 20)
    f32 = jnp.float32

    def nrm(k, shape, std):
        return jax.random.normal(k, shape, f32) * std

    return {
        "x": nrm(ks[0], (BATCH, SEQ, D_MODEL), 1.0),
        "norm1_g": 1.0 + nrm(ks[1], (DEPTH, D_MODEL), 0.02),
        "w_in": nrm(ks[2], (DEPTH, D_MODEL, IN_COLS), D_MODEL ** -0.5),
        "forget_bias": FORGET_BIAS_INIT + nrm(ks[3], (DEPTH, FOX_HEADS), 0.5),
        "q_norm_g": 1.0 + nrm(ks[4], (DEPTH, FOX_HEAD_DIM), 0.02),
        "k_norm_g": 1.0 + nrm(ks[5], (DEPTH, FOX_HEAD_DIM), 0.02),
        "pool_group_w": nrm(ks[6], (DEPTH, POOL_GROUPS, POOL_GROUP_DIM, POOL_GROUP_DIM),
                            POOL_GROUP_DIM ** -0.5),
        "pool_scale": 1.0 + nrm(ks[7], (DEPTH, POOL_WIDTH), 0.02),
        "w_branch_attn": nrm(ks[8], (DEPTH, FOX_WIDTH, D_MODEL), FOX_WIDTH ** -0.5),
        "w_branch_pool": nrm(ks[9], (DEPTH, POOL_WIDTH, D_MODEL), POOL_WIDTH ** -0.5),
        "w_out": nrm(ks[10], (DEPTH, D_MODEL, D_MODEL), D_MODEL ** -0.5),
        "norm2_g": 1.0 + nrm(ks[11], (DEPTH, D_MODEL), 0.02),
        "peer_w_query": nrm(ks[12], (DEPTH, D_MODEL, PEER_HEADS * PEER_QUERY_DIM), D_MODEL ** -0.5),
        "peer_sub_keys_1": nrm(ks[13], (DEPTH, PEER_HEADS, PEER_KEYS, PEER_HALF), PEER_HALF ** -0.5),
        "peer_sub_keys_2": nrm(ks[14], (DEPTH, PEER_HEADS, PEER_KEYS, PEER_HALF), PEER_HALF ** -0.5),
        "peer_expert_u": nrm(ks[15], (DEPTH, PEER_EXPERTS, D_MODEL), D_MODEL ** -0.5),
        "peer_expert_v": nrm(ks[16], (DEPTH, PEER_EXPERTS, D_MODEL), PEER_HEADS ** -0.5),
    }

def second_block(x, norm1_g, w_in, forget_bias, q_norm_g, k_norm_g, pool_group_w, pool_scale,
              w_branch_attn, w_branch_pool, w_out, norm2_g, peer_w_query, peer_sub_keys_1,
              peer_sub_keys_2, peer_expert_u, peer_expert_v):
    b, s, _ = x.shape
    for l in range(DEPTH):
        h = rms_norm_2(x, norm1_g[l])
        proj = h @ w_in[l]
        q, k, v, fl, pin, gl = jnp.split(proj, IN_SPLITS, axis=-1)

        q = rms_norm_2(q.reshape(b, s, FOX_HEADS, FOX_HEAD_DIM), q_norm_g[l]).transpose(0, 2, 1, 3)
        k = rms_norm_2(k.reshape(b, s, FOX_HEADS, FOX_HEAD_DIM), k_norm_g[l]).transpose(0, 2, 1, 3)
        v = v.reshape(b, s, FOX_HEADS, FOX_HEAD_DIM).transpose(0, 2, 1, 3)
        log_f = jax.nn.log_sigmoid(fl.astype(jnp.float32)
                                   + forget_bias[l].astype(jnp.float32)).transpose(0, 2, 1)
        attn = forgetting_attention(q, k, v, log_f)
        y_attn = attn.transpose(0, 2, 1, 3).reshape(b, s, FOX_WIDTH) @ w_branch_attn[l]

        y_pool = multiscale_pool(pin, pool_group_w[l], pool_scale[l]) @ w_branch_pool[l]

        gates = jax.nn.sigmoid(gl.astype(jnp.float32)).astype(x.dtype).reshape(
            b, s, N_BRANCHES, D_MODEL)
        merged = gates[:, :, 0] * y_attn + gates[:, :, 1] * y_pool
        x = x + merged @ w_out[l]

        x = x + peer(rms_norm_2(x, norm2_g[l]), peer_w_query[l], peer_sub_keys_1[l],
                     peer_sub_keys_2[l], peer_expert_u[l], peer_expert_v[l])
    return x


def setup_inputs(seed=0):
    out = dict(first_inputs(seed))
    for name, value in second_inputs(seed + 1).items():
        if name != "x":
            out[name + "_2"] = value
    return out


def reference(
    x, meta_tokens, rel_bias, conv_w_in, conv_b_in, conv_w_dw, conv_b_dw, conv_ln_g, conv_ln_b,
    conv_w_out, conv_b_out, attn_w_qkv, attn_b_qkv, attn_sinks, attn_w_o, attn_b_o,
    norm_mix_pre, norm_mix_post, norm_ffn_pre, norm_ffn_post, ffn_w_gate, ffn_w_up, ffn_w_down,
    norm1_g_2, w_in_2, forget_bias_2, q_norm_g_2, k_norm_g_2, pool_group_w_2, pool_scale_2,
    w_branch_attn_2, w_branch_pool_2, w_out_2, norm2_g_2, peer_w_query_2, peer_sub_keys_1_2,
    peer_sub_keys_2_2, peer_expert_u_2, peer_expert_v_2,
):
    x = first_block(
        x, meta_tokens, rel_bias, conv_w_in, conv_b_in, conv_w_dw, conv_b_dw, conv_ln_g,
        conv_ln_b, conv_w_out, conv_b_out, attn_w_qkv, attn_b_qkv, attn_sinks, attn_w_o,
        attn_b_o, norm_mix_pre, norm_mix_post, norm_ffn_pre, norm_ffn_post, ffn_w_gate,
        ffn_w_up, ffn_w_down,
    )
    return second_block(
        x, norm1_g_2, w_in_2, forget_bias_2, q_norm_g_2, k_norm_g_2, pool_group_w_2,
        pool_scale_2, w_branch_attn_2, w_branch_pool_2, w_out_2, norm2_g_2, peer_w_query_2,
        peer_sub_keys_1_2, peer_sub_keys_2_2, peer_expert_u_2, peer_expert_v_2,
    )


_drawn_inputs = setup_inputs


def setup_inputs(seed=0):
    import zlib

    import numpy as np

    out = dict(_drawn_inputs(seed))
    spreads = {}
    factors = {'norm_ffn_post': 3.568,
     'norm1_g_2': 5.072,
     'q_norm_g_2': 8.0,
     'k_norm_g_2': 22.011,
     'pool_scale_2': 17.574,
     'norm2_g_2': 30.344}
    for name, (base, spread) in spreads.items():
        noise = np.random.default_rng([zlib.crc32(name.encode()), seed]).standard_normal(out[name].shape)
        drawn = base * np.exp(spread * noise) if base else spread * noise
        out[name] = jnp.asarray(drawn.astype(out[name].dtype))
    for name, factor in factors.items():
        out[name] = (out[name] * factor).astype(out[name].dtype)
    return out
```

```python
from contextlib import ExitStack, contextmanager

import numpy as np
import concourse.bass as bass
from concourse import mybir

D = 2048
T, META = 256, 16
TT = T // 128
KT = D // 128
L = META + T
FF = 5632
TAPS = 31
HEADS, HD = 8, 128
POOL_W = 1024
POOL_WINDOWS = (2, 4, 8, 16)
PADP = 16
PH, TOPK, NKEYS = 8, 16, 128
SLOTS = PH * TOPK
RMS_EPS, LN_EPS = 1e-6, 1e-5
LOWEST = -3.0e38
MASKED = -1.0e30

PANELS = [("w_in", 32), ("w_out", 16), ("ffn", 132), ("qk", 16), ("v", 8), ("pin", 8),
          ("merge", 48), ("w_out_2", 16), ("query", 16)]
NPANELS = sum(n for _, n in PANELS)

COLUMNS = [("g_mix", KT), ("b_a", KT), ("b_g", KT), ("w_dw", KT * TAPS), ("b_dw", KT), ("ln_g", KT),
           ("ln_b", KT), ("g_ffn", KT), ("g_norm1", KT), ("g_q", 1), ("g_k", 1), ("pool_scale", 8)]
COL = {}
for _name, _n in COLUMNS:
    COL[_name] = sum(n for _, n in COLUMNS[:len(COL)])
NCOLS = sum(n for _, n in COLUMNS)


PER_ROUTE = 31

BANKS8 = range(8)


def per_round(**signals):
    full, empty = signals.pop("full", {}), signals.pop("empty", {})
    out = dict(signals)
    out.update({f"full{b}": k for b, k in full.items()})
    out.update({f"empty{b}": k for b, k in empty.items()})
    if "used" in out:
        out["split"] = out["hi"] = out["used"]
        out["quad"] = out["used"] // 4
    return out


def each(banks, k=1):
    return {b: k for b in banks}


PER_ROUND = {
    "norm0": dict(per_round(ssq=1, ms=1, root=1, rstd=1, xs=TT + 1, evac=9, full=each(BANKS8),
                            empty={**each(BANKS8), 0: 2}), used=1, hi=1, split=1),
    "w_in": per_round(used=8, full=each((0, 1, 2, 4, 5, 6)), empty=each(BANKS8)),
    "ln": per_round(dev=4, dev_sq=4, root=1, ln=4, silu=KT // 4, silu_hi=4, act=4, full=each((0, 1)), empty=each((0, 1))),
    "w_out": per_round(used=4, full={0: 1}, empty=each((0, 1))),
    "post": per_round(ssq=2, ms=2, root=2, rstd=1, xs=TT, res=TT, evac=8, full=each(BANKS8), empty=each(BANKS8)),
    "ffn": per_round(used=12, hhi=4, hlo=4, full={0: 4, 1: 2, 2: 4, 3: 2, 4: 2, 5: 2, 6: 2},
                     empty={**each(range(4), 4), **each(range(4, 8), 2)}),
    "qk": per_round(used=4, full=each((0, 1, 2)), empty=each(range(4))),
    "forget": per_round(wf_hi=1, wf_lo=1, z_step=2, z_ln=1, logf=1, full=each((6, 7)), empty=each((6, 7))),
    "qknorm": per_round(qsq=1, root=1, qkn=1, full=each((4, 5)), empty=each((4, 5))),
    "v": per_round(used=4, full={4: 1}, empty=each((4, 5))),
    "cum": per_round(lfb=1, full={6: 1}, empty={6: 1}),
    "score": per_round(full=each(range(4)), empty=each(range(4))),
    "softmax": per_round(negmax=1, exp=1, prob=2),
    "pin": per_round(used=4, full=each((0, 1, 2)), empty=each(range(4))),
    "pool": per_round(mixed=4, evac=8, full=each(range(4, 8), 2), empty=each(range(4, 8), 2)),
    "heads": per_round(evac=2, full=each(range(4)), empty=each(range(4))),
    "merge": per_round(used=12, part=4, full=each((0, 1, 2, 4, 5, 6), 2), empty=each(BANKS8, 2)),
    "merged": per_round(merged_hi=4, act=4),
    "w_out_2": per_round(used=4, full={0: 1}, empty=each((0, 1))),
    "post_2": per_round(ssq=1, ms=1, root=1, rstd=1, xs=TT, evac=8, xn=TT, full=each(BANKS8), empty=each(BANKS8)),
    "query": per_round(used=4, full=each((0, 1, 2)), empty=each(range(4))),
    "keys": per_round(full=each(BANKS8), empty=each(BANKS8)),
    "route": per_round(expert=1, gate_max=1, gate_exp=1),
    "pair": per_round(expert=2, gate_max=2, gate_exp=2, dot=2 * TOPK, gelu=8, hid=8, diag=2 * TOPK, v_used=2 * TOPK,
                      u_rows=8, v_rows=4),
}


class Counts:

    def __init__(self):
        self.base, self.low = {}, {}

    def after(self, key, k):
        base = self.base.get(key, 0)
        assert isinstance(base, int) or self.low.get(key, 0) + k > 0, (key, k)
        return base + k

    @contextmanager
    def rounds(self, engine, stage, times=1, **own):
        per = {**PER_ROUND[stage], **own}
        start = dict(self.base)
        self.low = start
        if times == 1:
            yield 0
            start = self.base
        else:
            with engine.Fori(0, times) as i:
                self.base = {**start, **{key: start.get(key, 0) + i * k for key, k in per.items()}}
                yield i
        self.base = {**start, **{key: start.get(key, 0) + times * k for key, k in per.items()}}
        self.low = dict(self.base)


def wait(engine, semaphore, value):
    if not (isinstance(value, int) and value <= 0):
        engine.wait_ge(semaphore, value)


def wait_apart(engine, semaphore, value, passed):
    if not (isinstance(value, int) and value <= 0):
        engine.wait_ge(semaphore, value)
        if not isinstance(value, int):
            engine.sem_inc(passed, 1)


def two_layers(nc, stream, columns, x, meta, b_out, g_mix_post, g_ffn_post, g_norm2, w_forget,
               forget_bias, group_w, keys, expert_u, expert_v, out):
    f32, f32r, u32 = mybir.dt.float32, mybir.dt.float32r, mybir.dt.uint32
    ACT, ALU, AX = mybir.ActivationFunctionType, mybir.AluOpType, mybir.AxisListType

    K = 1024
    at = (nc.sbuf_base + 63) // 64 * 64
    names = set()

    def place(name, shape, offset, dt=f32):
        assert name not in names
        names.add(name)
        return nc.alloc_sbuf_tensor_at(name, shape, dt, offset=offset)

    def keep(name, shape, dt=f32):
        nonlocal at
        t = place(name, shape, at, dt)
        at += (int(np.prod(shape[1:])) * 4 + 63) // 64 * 64
        return t

    cols = keep("s_cols", [128, NCOLS])
    ident = keep("s_ident", [128, 128])
    ones = keep("s_ones", [128, 128])
    tri_ones = keep("s_tri_ones", [128, 2 * 128])
    causal = keep("s_causal", [128, 128])
    group_sb = keep("s_group_w", [128, 4, 2, 256])
    wf_raw = keep("s_wf_raw", [128, KT, HEADS])
    wf_hi = keep("s_wf_hi", [128, KT, HEADS], f32r)
    wf_lo = keep("s_wf_lo", [128, KT, HEADS], f32r)
    fb = keep("s_forget_bias", [128, HEADS])
    stat = keep("s_stat", [128, 8])
    fg = keep("s_forget", [128, 6, TT * HEADS])
    cq = keep("s_cq", [128, TT * HEADS])
    negmax = keep("s_negmax", [128, TT * HEADS])
    den = keep("s_den", [128, TT * HEADS])
    inv_count = keep("s_inv_count", [128, 16])
    inv_count_i = keep("s_inv_count_i", [128, 16], mybir.dt.int32)
    xres = keep("s_xres", [128, TT, D])
    ring0 = at
    raw = [keep(f"s_raw{i}", [128, 2048]) for i in range(4)]
    w_hi = [keep(f"s_w_hi{i}", [128, 2048], f32r) for i in range(2)]
    w_lo = [keep(f"s_w_lo{i}", [128, 2048], f32r) for i in range(2)]
    a_hi = keep("s_a_hi", [128, KT, L], f32r)
    a_lo = keep("s_a_lo", [128, KT, L], f32r)
    S = at
    xs = place("s_xs", [128, TT, D], S + 16 * K)
    xs0 = place("s_xs0", [128, TT, D], S + 0)
    meta_sb = place("s_meta", [META, D], S + 16 * K)
    cvg = place("s_cvg", [128, 4, TAPS - 1 + L], S + 0)
    cacc = place("s_cacc", [128, 4, T], S + 5 * K)
    sig = place("s_sig", [128, 4, L], S + 9 * K)
    cvo = place("s_cvo", [128, KT, T], S + 16 * K)
    sq = place("s_sq", [128, KT, T], S + 32 * K)
    mean = place("s_mean", [128, T], S + 48 * K)
    rstd = place("s_rstd", [128, T], S + 49 * K)
    bout_row = place("s_bout_row", [128, D], S + 50 * K)
    gmix_row = place("s_gmix_row", [128, D], S + 58 * K)
    gffn_row = place("s_gffn_row", [128, D], S + 66 * K)
    yrow = place("s_yrow", [128, TT, D], S + 0)
    sg = place("s_sg", [128, 2, T], S + 32 * K)
    hf = place("s_hf", [128, 2, T], S + 34 * K)
    h_hi = place("s_h_hi", [128, 2, T], S + 36 * K, f32r)
    h_lo = place("s_h_lo", [128, 2, T], S + 38 * K, f32r)
    qk = place("s_qk", [128, 2 * HEADS, T], S + 0)
    vrow = place("s_vrow", [128, TT, HEADS * HD], S + 16 * K)
    pin = place("s_pin", [128, 8, PADP + T], S + 24 * K)
    mixed = place("s_mixed", [128, 8, T], S + 33 * K)
    qsq = place("s_qsq", [128, 4, T], S + 41 * K)
    qrs = place("s_qrs", [128, 4, T], S + 45 * K)
    lg0 = place("s_lg0", [128, HEADS, 128], S + 41 * K)
    lg1 = place("s_lg1", [128, HEADS, 256], S + 45 * K)
    lfb = place("s_lfb", [128, TT, HEADS, 128], S + 53 * K)
    at_hi = place("s_at_hi", [128, HEADS, T], S + 61 * K, f32r)
    at_lo = place("s_at_lo", [128, HEADS, T], S + 69 * K, f32r)
    bias_t = place("s_bias_t", [128, 2, 384], S + 61 * K)
    win_a = place("s_win_a", [128, 2, PADP + T], S + 65 * K)
    win_b = place("s_win_b", [128, 2, PADP + T], S + 69 * K)
    po_hi = place("s_po_hi", [128, 8, T], S + 24 * K, f32r)
    po_lo = place("s_po_lo", [128, 8, T], S + 53 * K, f32r)
    pts = place("s_pts", [128, 2, 384], S + 33 * K)
    merged = place("s_merged", [128, KT, T], S + 0)
    gate0 = place("s_gate0", [128, 4, T], S + 16 * K)
    gate1 = place("s_gate1", [128, 4, T], S + 20 * K)
    part0 = place("s_part0", [128, 4, T], S + 33 * K)
    part1 = place("s_part1", [128, 4, T], S + 37 * K)
    xn = place("s_xn", [128, TT, D], S + 0)
    g2_row = place("s_g2_row", [128, D], S + 33 * K)
    keys_sb = place("s_keys", [128, 2 * PH, NKEYS], S + 41 * K)
    qp = place("s_qp", [128, 2 * PH, T], S + 49 * K)
    score = place("s_score", [128, TT * PH, 2 * NKEYS], S + 16 * K)
    NU, NV, NDIAG, BATCH = 4, 8, 4, 4
    u_slot = [place(f"s_u{i}", [128, D], ring0 + i * 8 * K) for i in range(NU)]
    v_slot = [place(f"s_v{i}", [128, D], ring0 + (NU + i) * 8 * K) for i in range(NV)]
    assert ring0 + (NU + NV) * 8 * K <= S
    P0 = S + 66 * K
    diag = [place(f"s_diag{i}", [128, 128], P0 + i * 512) for i in range(NDIAG)]
    P0 += NDIAG * 512

    def small(name, n, dt=f32):
        nonlocal P0
        t = place(name, [128, n], P0, dt)
        P0 += (4 * n + 63) // 64 * 64
        return t

    sc = small("s_sc", 2 * NKEYS)
    sc_rest = small("s_sc_rest", NKEYS)
    val = small("s_val", 2 * TOPK)
    ind = small("s_ind", 2 * TOPK, u32)
    indf = small("s_indf", 2 * TOPK)
    cand = small("s_cand", TOPK * TOPK)
    cand_rest = small("s_cand_rest", TOPK * TOPK)
    top = small("s_top", TOPK)
    pos = small("s_pos", TOPK, u32)
    pos1 = small("s_pos1", TOPK, u32)
    posf = small("s_posf", 2 * TOPK)
    pick = small("s_pick", TOPK * TOPK)
    chosen = small("s_chosen", 2 * TOPK)
    expert_f = small("s_expert_f", TOPK)
    expert = [small(f"s_expert{i}", TOPK, u32) for i in range(2)]
    gate = [small(f"s_pgate{i}", TOPK) for i in range(2)]
    gsum = small("s_gsum", 4)
    iota_i = small("s_iota_i", TOPK, mybir.dt.int32)
    iota_f = small("s_iota_f", TOPK)
    adot = [small(f"s_adot{i}", TOPK) for i in range(2)]
    gelu = [small(f"s_gelu{i}", TOPK) for i in range(2)]
    hid = [small(f"s_hid{i}", TOPK) for i in range(2)]
    assert P0 <= S + 78 * K, P0 - S
    zeros = place("s_zeros", [128, 128], S + 65 * K)
    out_row = place("s_out_row", [128, TT, D], S + 33 * K)

    with ExitStack() as ctx:
        bank = [ctx.enter_context(nc.psum_tensor(f"bank{b}", [128, 512], f32)) for b in range(8)]

        def sem(name):
            return ctx.enter_context(nc.semaphore(name))

        raw_loaded = [sem(f"raw_loaded{i}") for i in range(4)]
        hi_ready = sem("hi_ready")
        split_ready = sem("split_ready")
        panel_used = sem("panel_used")
        bank_full = [sem(f"bank_full{b}") for b in range(8)]
        bank_empty = [sem(f"bank_empty{b}") for b in range(8)]
        pool_passed, dve_passed = sem("pool_passed"), sem("dve_passed")
        dve_step = sem("dve_step")
        pool_step = sem("pool_step")
        x_loaded, meta_loaded, cols_loaded = sem("x_loaded"), sem("meta_loaded"), sem("cols_loaded")
        rows_loaded, small_loaded, late_loaded = sem("rows_loaded"), sem("small_loaded"), sem("late_loaded")
        const_ready, stat_clear = sem("const_ready"), sem("stat_clear")
        evac_hi = sem("evac_hi")
        ssq_ready = sem("ssq_ready")
        ms_ready = sem("ms_ready")
        root_ready = sem("root_ready")
        rstd_ready = sem("rstd_ready")
        xs_ready = sem("xs_ready")
        res_ready = sem("res_ready")
        conv_ready = sem("conv_ready")
        dev_ready = sem("dev_ready")
        dev_sq_ready = sem("dev_sq_ready")
        ln_ready = sem("ln_ready")
        silu_ready, silu_hi = sem("silu_ready"), sem("silu_hi")
        act_ready = sem("act_ready")
        hhi_ready, hlo_ready = sem("hhi_ready"), sem("hlo_ready")
        wfhi_ready, wflo_ready = sem("wfhi_ready"), sem("wflo_ready")
        z_step, z_ln, logf_ready = sem("z_step"), sem("z_ln"), sem("logf_ready")
        qsq_ready, qkn_ready = sem("qsq_ready"), sem("qkn_ready")
        lfb_ready = sem("lfb_ready")
        negmax_ready, exp_ready, prob_ready = sem("negmax_ready"), sem("exp_ready"), sem("prob_ready")
        mixed_ready, part_ready = sem("mixed_ready"), sem("part_ready")
        merged_hi, xn_ready = sem("merged_hi"), sem("xn_ready")
        zeros_ready, iota_ready = sem("zeros_ready"), sem("iota_ready")
        expert_ready = sem("expert_ready")
        gate_max, gate_exp = sem("gate_max"), sem("gate_exp")
        u_loaded = [sem(f"u_loaded{i}") for i in range(NU)]
        v_loaded = [sem(f"v_loaded{i}") for i in range(NV)]
        dot_ready, gelu_ready, hid_ready = sem("dot_ready"), sem("gelu_ready"), sem("hid_ready")
        diag_ready, v_used = sem("diag_ready"), sem("v_used")
        acc_done, out_ready, stored = sem("acc_done"), sem("out_ready"), sem("stored")

        block = ctx.enter_context(nc.Block())

        @block.sync
        def _(sp):
            sp.dma_start(xres[:, :, :], x.rearrange("(t p) d -> p t d", p=128)).then_inc(x_loaded, 16)
            sp.dma_start(meta_sb[:, :], meta).then_inc(meta_loaded, 16)
            sp.dma_start(cols[:, :], columns).then_inc(cols_loaded, 16)
            for s in range(4):
                sp.dma_start(raw[s][:, :], stream[s]).then_inc(raw_loaded[s], 16)
            panels = stream.rearrange("(q s) p n -> q s p n", s=4)
            with sp.Fori(1, NPANELS // 4) as q:
                for s in range(4):
                    sp.wait_ge(split_ready, q * 4 + (s - 3))
                    sp.dma_start(raw[s][:, :], panels[bass.ds(q, 1), s].rearrange("a p n -> (a p) n"))\
                        .then_inc(raw_loaded[s], 16)
            for t in range(TT):
                sp.wait_ge(out_ready, t + 1)
                sp.dma_start(out[t * 128:(t + 1) * 128, :], out_row[:, t, :]).then_inc(stored, 16)
            sp.wait_ge(stored, 16 * TT)

        @block.gpsimd
        def _(pool):
            n = Counts()
            pool.memset(ident[:, :], 0.0).then_inc(pool_step, 1)
            pool.memset(ones[:, :], 1.0).then_inc(pool_step, 1)
            pool.memset(tri_ones[:, :], 1.0).then_inc(pool_step, 1)
            pool.memset(causal[:, :], 0.0).then_inc(pool_step, 1)
            pool.iota(inv_count_i[:, :], pattern=[[1, 16]], base=1, channel_multiplier=0).then_inc(pool_step, 1)
            pool.wait_ge(pool_step, 5)
            pool.affine_select(out=ident[:, :], in_=ident[:, :], compare_op=ALU.not_equal, fill=1.0,
                               base=0, pattern=[[-1, 128]], channel_multiplier=1).then_inc(const_ready, 1)
            pool.affine_select(out=tri_ones[:, :], in_=tri_ones[:, :], compare_op=ALU.is_ge, fill=0.0,
                               base=0, pattern=[[1, 256]], channel_multiplier=-1).then_inc(const_ready, 1)
            pool.affine_select(out=causal[:, :], in_=causal[:, :], compare_op=ALU.is_ge, fill=MASKED,
                               base=0, pattern=[[-1, 128]], channel_multiplier=1).then_inc(const_ready, 1)
            for row, src in ((bout_row, b_out), (gmix_row, g_mix_post), (gffn_row, g_ffn_post)):
                pool.dma_start(row[:, :], src.partition_broadcast(128)).then_inc(rows_loaded, 16)
            pool.dma_start(wf_raw[:, :, :], w_forget).then_inc(small_loaded, 16)
            pool.dma_start(fb[:, :], forget_bias.partition_broadcast(128)).then_inc(small_loaded, 16)
            pool.dma_start(group_sb[:, :, :, :], group_w).then_inc(small_loaded, 16)
            pool.wait_ge(act_ready, 4 + 4)
            pool.dma_start(g2_row[:, :], g_norm2.partition_broadcast(128)).then_inc(late_loaded, 16)
            pool.dma_start(keys_sb[:, :, :], keys).then_inc(late_loaded, 16)
            pool.iota(iota_i[:, :], pattern=[[1, TOPK]], base=0, channel_multiplier=0).then_inc(iota_ready, 1)
            pool.memset(zeros[:, :], 0.0).then_inc(zeros_ready, 1)

            with n.rounds(pool, "route"):
                pass

            def gathers():
                for e in range(2):
                    wait_apart(pool, expert_ready, n.after("expert", e), pool_passed)
                    for s in range(TOPK):
                        index = bass.IndirectOffsetOnAxis(ap=expert[e][:, s:s + 1], axis=0)
                        wait_apart(pool, dot_ready, n.after("dot", e * TOPK + s + 1 - NU), pool_passed)
                        pool.indirect_dma_start(u_slot[s % NU][:, :], None, expert_u, index)\
                            .then_inc(u_loaded[s % NU], 16)
                        wait_apart(pool, v_used, n.after("v_used", e * TOPK + s + 1 - NV), pool_passed)
                        pool.indirect_dma_start(v_slot[s % NV][:, :], None, expert_v, index)\
                            .then_inc(v_loaded[s % NV], 16)

            with n.rounds(pool, "pair"):
                gathers()
            with n.rounds(pool, "pair", TT * PH // 2 - 1):
                gathers()

        @block.scalar
        def _(act):
            n = Counts()

            def col(name, k):
                return cols[:, COL[name] + k:COL[name] + k + 1]

            def split_hi(c):
                s = (c + 1) % 4
                act.wait_ge(raw_loaded[s], n.after("quad", (c + 1) // 4 + 1) * 16)
                act.wait_ge(panel_used, n.after("used", c))
                act.activation(w_hi[s % 2][:, :], raw[s][:, :], ACT.Copy).then_inc(hi_ready, 1)

            def sums_of_squares(src, junk, ready=None):
                for t in range(TT):
                    if ready:
                        act.wait_ge(ready[0], n.after(ready[1], t + 1))
                    ins = act.activation(junk[:, t, :], src[:, t, :], ACT.Square, accum_out=stat[:, t:t + 1])
                ins.then_inc(ssq_ready, 1)

            def root(k, width=TT):
                act.wait_ge(ms_ready, n.after("ms", k))
                act.activation(stat[:, 4:4 + width], stat[:, 4:4 + width], ACT.Sqrt).then_inc(root_ready, 1)

            def transposed_hi(gain, offset):
                for t in range(TT):
                    for b in range(4):
                        act.wait_ge(bank_full[4 * t + b], n.after(f"full{4 * t + b}", 1))
                        for q in range(4):
                            k = 4 * b + q
                            ins = act.activation(a_hi[:, k, offset + t * 128:offset + (t + 1) * 128],
                                                 bank[4 * t + b][:, q * 128:(q + 1) * 128], ACT.Copy,
                                                 scale=col(gain, k) if gain else 1.0)
                        ins.then_inc(evac_hi, 1)

            act.wait_ge(raw_loaded[0], 16)
            act.activation(w_hi[0][:, :], raw[0][:, :], ACT.Copy).then_inc(hi_ready, 1)
            with n.rounds(act, "norm0"):
                act.wait_ge(x_loaded, 16)
                act.wait_ge(stat_clear, 1)
                for t in range(TT):
                    act.activation(xs0[:, t, :], xres[:, t, :], ACT.Square, accum_out=stat[:, t:t + 1])
                act.wait_ge(meta_loaded, 16)
                act.activation(sq[0:META, 0:8, :].rearrange("p a t -> p (a t)"), meta_sb[:, :], ACT.Square,
                               accum_out=stat[0:META, 2:3]).then_inc(ssq_ready, 1)
                root(1, 3)
                act.wait_ge(rstd_ready, n.after("rstd", 1))
                for t in range(TT):
                    act.activation(xs0[:, t, :], xres[:, t, :], ACT.Copy, scale=stat[:, 4 + t:5 + t])\
                        .then_inc(xs_ready, 1)
                act.activation(meta_sb[:, :], meta_sb[:, :], ACT.Copy, scale=stat[0:META, 6:7]).then_inc(xs_ready, 1)
                act.wait_ge(cols_loaded, 16)
                transposed_hi("g_mix", META)
                act.wait_ge(panel_used, n.after("used", 1))
                for k in range(KT):
                    ins = act.activation(a_hi[:, k, 0:META], bank[0][:, k * META:(k + 1) * META], ACT.Copy,
                                         scale=col("g_mix", k))
                ins.then_inc(evac_hi, 1)

            with n.rounds(act, "w_in", 4) as i:
                for c in range(8):
                    split_hi(c)
                for j in range(4):
                    act.wait_ge(bank_empty[j], n.after(f"empty{j}", 0))
                    if j < 3:
                        act.wait_ge(bank_full[4 + j], n.after(f"full{4 + j}", 1))
                    else:
                        act.wait_ge(panel_used, n.after("used", 8))
                    act.activation(sig[:, j, :], bank[4 + j][:, 0:L], ACT.Sigmoid,
                                   bias=cols[:, bass.ds(i * 4 + (COL["b_g"] + j), 1)]).then_inc(bank_empty[4 + j], 1)

            with n.rounds(act, "ln"):
                for g in range(4):
                    act.wait_ge(dev_ready, n.after("dev", g + 1))
                    act.activation(sq[:, 4 * g:4 * g + 4, :], cvo[:, 4 * g:4 * g + 4, :], ACT.Square)\
                        .then_inc(dev_sq_ready, 1)
                act.wait_ge(bank_empty[1], n.after("empty1", 1))
                act.activation(rstd[:, :], rstd[:, :], ACT.Sqrt).then_inc(root_ready, 1)
                for g in range(4):
                    act.wait_ge(ln_ready, n.after("ln", g + 1))
                    for k in range(4 * g, 4 * g + 4):
                        ins = act.activation(sq[:, k, :], cvo[:, k, :], ACT.Silu, scale=col("ln_g", k), bias=col("ln_b", k))
                    ins.then_inc(silu_ready, 1)
                    act.wait_ge(silu_ready, n.after("silu", g + 1))
                    act.activation(a_hi[:, 4 * g:4 * g + 4, 0:T], sq[:, 4 * g:4 * g + 4, :], ACT.Copy).then_inc(silu_hi, 1)

            with n.rounds(act, "w_out", 4):
                for c in range(4):
                    split_hi(c)

            def post(last_bank, gain):
                act.wait_ge(bank_empty[last_bank], n.after(f"empty{last_bank}", 0))
                sums_of_squares(yrow, xs)
                root(1)
                sums_of_squares(xres, xs, (res_ready, "res"))
                root(2)
                act.wait_ge(rstd_ready, n.after("rstd", 1))
                for t in range(TT):
                    act.activation(xs[:, t, :], xres[:, t, :], ACT.Copy, scale=stat[:, 4 + t:5 + t])\
                        .then_inc(xs_ready, 1)
                transposed_hi(gain, 0)

            with n.rounds(act, "post"):
                post(1, "g_ffn")

            with n.rounds(act, "ffn", FF // 512):
                for blk in range(2):
                    c0 = 6 * blk
                    split_hi(c0)
                    split_hi(c0 + 1)
                    for j in range(2):
                        act.wait_ge(bank_empty[2 + j], n.after(f"empty{2 + j}", 2 * blk))
                        if j == 0:
                            act.wait_ge(bank_full[0], n.after("full0", 2 * blk + 1))
                        else:
                            act.wait_ge(panel_used, n.after("used", c0 + 2))
                        act.activation(sg[:, j, :], bank[j][:, 0:T], ACT.Silu).then_inc(bank_empty[j], 1)
                    split_hi(c0 + 2)
                    split_hi(c0 + 3)
                    for j in range(2):
                        act.wait_ge(bank_empty[2 + j], n.after(f"empty{2 + j}", 2 * blk + 1))
                        act.activation(h_hi[:, j, :], hf[:, j, :], ACT.Copy).then_inc(hhi_ready, 1)
                    split_hi(c0 + 4)
                    split_hi(c0 + 5)

            with n.rounds(act, "post"):
                post(7, "g_norm1")

            def copies_out(i, dst, offset):
                for j in range(4):
                    if j < 3:
                        act.wait_ge(bank_full[j], n.after(f"full{j}", 1))
                    else:
                        act.wait_ge(panel_used, n.after("used", 4))
                    act.activation(dst[:, bass.ds(i * 4 + j, 1), offset:offset + T].rearrange("p a t -> p (a t)"),
                                   bank[j][:, 0:T], ACT.Copy).then_inc(bank_empty[j], 1)

            with n.rounds(act, "qk", 4) as i:
                for c in range(4):
                    split_hi(c)
                copies_out(i, qk, 0)
            with n.rounds(act, "forget"):
                act.wait_ge(small_loaded, 48)
                act.activation(wf_hi[:, :, :], wf_raw[:, :, :], ACT.Copy).then_inc(wfhi_ready, 1)
                act.wait_ge(bank_empty[7], n.after("empty7", 1))
                act.activation(fg[:, 1, :], fg[:, 0, :], ACT.Abs).then_inc(z_step, 1)
                act.wait_ge(z_step, n.after("z_step", 1))
                act.activation(fg[:, 1, :], fg[:, 1, :], ACT.Exp, scale=-1.0).then_inc(z_step, 1)
                act.wait_ge(z_step, n.after("z_step", 2))
                act.activation(fg[:, 2, :], fg[:, 1, :], ACT.Ln, bias=1.0).then_inc(z_ln, 1)
            for g in range(4):
                with n.rounds(act, "qknorm"):
                    act.wait_ge(bank_empty[3], n.after("empty3", 0))
                    wait(act, qkn_ready, n.after("qkn", 0))
                    act.activation(qsq[:, :, :], qk[:, 4 * g:4 * g + 4, :], ACT.Square).then_inc(qsq_ready, 1)
                    act.wait_ge(bank_empty[5], n.after("empty5", 1))
                    act.activation(qrs[:, :, :], qrs[:, :, :], ACT.Sqrt).then_inc(root_ready, 1)
            with n.rounds(act, "v", 2) as i:
                for c in range(4):
                    split_hi(c)
                for t in range(TT):
                    if t == 0:
                        act.wait_ge(bank_full[4], n.after("full4", 1))
                    else:
                        act.wait_ge(panel_used, n.after("used", 4))
                    act.activation(vrow[:, t, bass.ds(i * 512, 512)], bank[4 + t][:, :], ACT.Copy)\
                        .then_inc(bank_empty[4 + t], 1)
            with n.rounds(act, "cum"):
                pass
            for r in range(HEADS // 2):
                with n.rounds(act, "score"):
                    pass
            with n.rounds(act, "softmax"):
                act.wait_ge(negmax_ready, n.after("negmax", 1))
                for h in range(HEADS):
                    act.activation(lg0[:, h, :], lg0[:, h, :], ACT.Exp, bias=negmax[:, h:h + 1],
                                   accum_out=den[:, h:h + 1])
                    ins = act.activation(lg1[:, h, :], lg1[:, h, :], ACT.Exp, bias=negmax[:, HEADS + h:HEADS + h + 1],
                                         accum_out=den[:, HEADS + h:HEADS + h + 1])
                ins.then_inc(exp_ready, 1)
            with n.rounds(act, "pin", 2) as i:
                for c in range(4):
                    split_hi(c)
                copies_out(i, pin, PADP)
            with n.rounds(act, "pool"):
                for j in range(8):
                    b = 4 + j % 4
                    act.wait_ge(bank_full[b], n.after(f"full{b}", j // 4 + 1))
                    act.activation(po_hi[:, j, :], bank[b][:, 0:T], ACT.Copy, scale=col("pool_scale", j)).then_inc(evac_hi, 1)
            for r in range(HEADS // 2):
                with n.rounds(act, "heads"):
                    for e in range(2):
                        act.wait_ge(bank_full[e], n.after(f"full{e}", 1))
                        act.activation(pts[:, e, :], bank[e][:, 0:384], ACT.Copy).then_inc(bank_empty[e], 1)
                    for e in range(2):
                        act.wait_ge(bank_full[2 + e], n.after(f"full{2 + e}", 1))
                        act.activation(at_hi[:, 2 * r + e, :], bank[2 + e][:, 0:T], ACT.Copy).then_inc(evac_hi, 1)
            with n.rounds(act, "merge", 4):
                for half, gates in enumerate((gate0, gate1)):
                    for c in range(4):
                        split_hi(4 * half + c)
                    for j in range(4):
                        b = 4 * half + j
                        if j < 3:
                            act.wait_ge(bank_full[b], n.after(f"full{b}", 1))
                        else:
                            act.wait_ge(panel_used, n.after("used", 4 * half + 4))
                        act.activation(gates[:, j, :], bank[b][:, 0:T], ACT.Sigmoid).then_inc(bank_empty[b], 1)
                for c in range(8, 12):
                    split_hi(c)
            with n.rounds(act, "merged"):
                act.wait_ge(part_ready, n.after("part", 0))
                for g in range(4):
                    act.activation(a_hi[:, 4 * g:4 * g + 4, 0:T], merged[:, 4 * g:4 * g + 4, :], ACT.Copy).then_inc(merged_hi, 1)
            with n.rounds(act, "w_out_2", 4):
                for c in range(4):
                    split_hi(c)
            with n.rounds(act, "post_2"):
                act.wait_ge(bank_empty[1], n.after("empty1", 0))
                sums_of_squares(xres, xs)
                root(1)
                act.wait_ge(rstd_ready, n.after("rstd", 1))
                for t in range(TT):
                    act.activation(xs[:, t, :], xres[:, t, :], ACT.Copy, scale=stat[:, 4 + t:5 + t]).then_inc(xs_ready, 1)
                transposed_hi(None, 0)
            with n.rounds(act, "query", 3) as i:
                for c in range(4):
                    split_hi(c)
                copies_out(i, qp, 0)
            with n.rounds(act, "query"):
                for c in range(3):
                    split_hi(c)
                copies_out(3, qp, 0)
            with n.rounds(act, "keys"):
                for t in range(TT):
                    for b in range(4):
                        act.wait_ge(bank_full[4 * t + b], n.after(f"full{4 * t + b}", 1))
                        act.activation(score[:, t * PH + 2 * b:t * PH + 2 * b + 2, :].rearrange("p h k -> p (h k)"),
                                       bank[4 * t + b][:, :], ACT.Copy).then_inc(bank_empty[4 * t + b], 1)

            def gate_exps(parity, k):
                act.wait_ge(gate_max, n.after("gate_max", k))
                act.activation(gate[parity][:, :], top[:, :], ACT.Exp, bias=gsum[:, 0:1], accum_out=gsum[:, 1:2])\
                    .then_inc(gate_exp, 1)

            def heads(more=True):
                for e in range(2):
                    for q in range(TOPK // BATCH):
                        if q == 2 and (more or e == 0):
                            gate_exps(1 - e, e + 1)
                        part = slice(q * BATCH, (q + 1) * BATCH)
                        act.wait_ge(dot_ready, n.after("dot", e * TOPK + (q + 1) * BATCH))
                        act.activation(gelu[e][:, part], adot[e][:, part], ACT.Gelu_apprx_tanh).then_inc(gelu_ready, 1)
                        act.wait_ge(hid_ready, n.after("hid", e * TOPK // BATCH + q + 1))
                        for s in range(q * BATCH, (q + 1) * BATCH):
                            wait(act, v_used, n.after("v_used", e * TOPK + s + 1 - NDIAG))
                            act.activation(diag[s % NDIAG][:, :], ident[:, :], ACT.Copy, scale=hid[e][:, s:s + 1])\
                                .then_inc(diag_ready, 1)

            with n.rounds(act, "route"):
                gate_exps(0, 1)
            with n.rounds(act, "pair"):
                heads()
            with n.rounds(act, "pair", TT * PH // 2 - 2):
                heads()
            with n.rounds(act, "pair"):
                heads(more=False)

        @block.vector
        def _(dve):
            n = Counts()

            def col(name, k):
                return cols[:, COL[name] + k:COL[name] + k + 1]

            def step(ins):
                ins.then_inc(dve_step, 1)
                n.base["dve_step"] = n.base.get("dve_step", 0) + 1

            def settled(back=0):
                dve.wait_ge(dve_step, n.base["dve_step"] - back)

            def link(ins):
                step(ins)
                settled()

            def split_lo(c):
                s = (c + 1) % 4
                dve.wait_ge(hi_ready, n.after("hi", c + 1))
                dve.tensor_tensor(w_lo[s % 2][:, :], raw[s][:, :], w_hi[s % 2][:, :].bitcast(f32), ALU.subtract)\
                    .then_inc(split_ready, 1)

            def mean_square(k, width=TT):
                dve.wait_ge(ssq_ready, n.after("ssq", k))
                dve.tensor_scalar(stat[:, 4:4 + width], stat[:, 0:width], 1.0 / D, RMS_EPS, ALU.mult, ALU.add)\
                    .then_inc(ms_ready, 1)

            def inverse(k, width=TT):
                dve.wait_ge(root_ready, n.after("root", k))
                dve.reciprocal(stat[:, 4:4 + width], stat[:, 4:4 + width]).then_inc(rstd_ready, 1)

            def transposed_lo(gain, offset):
                for t in range(TT):
                    for b in range(4):
                        dve.wait_ge(evac_hi, n.after("evac", 4 * t + b + 1))
                        for q in range(4):
                            k = 4 * b + q
                            where = slice(offset + t * 128, offset + (t + 1) * 128)
                            ins = dve.scalar_tensor_tensor(
                                a_lo[:, k, where], bank[4 * t + b][:, q * 128:(q + 1) * 128],
                                col(gain, k) if gain else 1.0, a_hi[:, k, where].bitcast(f32), ALU.mult, ALU.subtract)
                        ins.then_inc(bank_empty[4 * t + b], 1)

            dve.memset(stat[:, :], 1.0).then_inc(stat_clear, 1)
            dve.wait_ge(hi_ready, 1)
            dve.tensor_tensor(w_lo[0][:, :], raw[0][:, :], w_hi[0][:, :].bitcast(f32), ALU.subtract).then_inc(split_ready, 1)
            with n.rounds(dve, "norm0"):
                mean_square(1, 3)
                inverse(1, 3)
                dve.wait_ge(cols_loaded, 16)
                transposed_lo("g_mix", META)
                dve.wait_ge(evac_hi, n.after("evac", 9))
                for k in range(KT):
                    ins = dve.scalar_tensor_tensor(a_lo[:, k, 0:META], bank[0][:, k * META:(k + 1) * META], col("g_mix", k),
                                                   a_hi[:, k, 0:META].bitcast(f32), ALU.mult, ALU.subtract)
                ins.then_inc(bank_empty[0], 1)
                link(dve.memset(cvg[:, :, 0:TAPS - 1], 0.0))

            def glu(i):
                for j in range(4):
                    if j < 3:
                        dve.wait_ge(bank_full[j], n.after(f"full{j}", 1))
                    else:
                        dve.wait_ge(panel_used, n.after("used", 4))
                    dve.wait_ge(bank_empty[4 + j], n.after(f"empty{4 + j}", 1))
                    dve.scalar_tensor_tensor(cvg[:, j, TAPS - 1:], bank[j][:, 0:L],
                                             cols[:, bass.ds(i * 4 + (COL["b_a"] + j), 1)], sig[:, j, :],
                                             ALU.add, ALU.mult).then_inc(bank_empty[j], 1)

            def conv(i, taps, own):
                for tap in taps:
                    for j in range(4):
                        w = cols[:, bass.ds(i * (4 * TAPS) + (COL["w_dw"] + j * TAPS + tap), 1)]
                        u = cvg[:, j, META + tap:META + tap + T]
                        if tap == 0:
                            dve.wait_ge(bank_empty[j], n.after(f"empty{j}", own))
                            b = cols[:, bass.ds(i * 4 + (COL["b_dw"] + j), 1)]
                            step(dve.tensor_scalar(cacc[:, j, :], u, w, b, ALU.mult, ALU.add))
                            continue
                        settled(3)
                        if tap < TAPS - 1:
                            step(dve.scalar_tensor_tensor(cacc[:, j, :], u, w, cacc[:, j, :], ALU.mult, ALU.add))
                        else:
                            step(dve.scalar_tensor_tensor(
                                cvo[:, bass.ds(i * 4 + j, 1), :].rearrange("p a t -> p (a t)"), u, w, cacc[:, j, :],
                                ALU.mult, ALU.add))

            with n.rounds(dve, "w_in"):
                for c in range(8):
                    split_lo(c)
                glu(0)
            with n.rounds(dve, "w_in", 3, dve_step=4 * TAPS) as i:
                for c in range(8):
                    split_lo(c)
                    conv(i, range(c * TAPS // 8, (c + 1) * TAPS // 8), 0)
                settled()
                glu(i + 1)
            conv(3, range(TAPS), 0)
            settled()
            dve.memset(stat[:, 7:8], 1.0).then_inc(conv_ready, 1)

            with n.rounds(dve, "ln"):
                dve.wait_ge(bank_full[0], n.after("full0", 1))
                dve.tensor_scalar(mean[:, :], bank[0][:, 0:T], 1.0 / D, None, ALU.mult).then_inc(bank_empty[0], 1)
                dve.wait_ge(bank_empty[0], n.after("empty0", 1))
                for g in range(4):
                    four = cvo[:, 4 * g:4 * g + 4, :]
                    dve.tensor_tensor(four, four, mean[:, :].unsqueeze(1).to_broadcast([128, 4, T]), ALU.subtract)\
                        .then_inc(dev_ready, 1)
                dve.wait_ge(bank_full[1], n.after("full1", 1))
                dve.tensor_scalar(rstd[:, :], bank[1][:, 0:T], 1.0 / D, LN_EPS, ALU.mult, ALU.add).then_inc(bank_empty[1], 1)
                dve.wait_ge(root_ready, n.after("root", 1))
                link(dve.reciprocal(rstd[:, :], rstd[:, :]))
                for g in range(4):
                    four = cvo[:, 4 * g:4 * g + 4, :]
                    dve.tensor_tensor(four, four, rstd[:, :].unsqueeze(1).to_broadcast([128, 4, T]), ALU.mult)\
                        .then_inc(ln_ready, 1)
                for g in range(4):
                    dve.wait_ge(silu_hi, n.after("silu_hi", g + 1))
                    dve.tensor_tensor(a_lo[:, 4 * g:4 * g + 4, 0:T], sq[:, 4 * g:4 * g + 4, :],
                                      a_hi[:, 4 * g:4 * g + 4, 0:T].bitcast(f32), ALU.subtract).then_inc(act_ready, 1)

            dve.wait_ge(rows_loaded, 48)
            with n.rounds(dve, "w_out", 4) as i:
                for c in range(4):
                    split_lo(c)
                for t in range(TT):
                    if t == 0:
                        dve.wait_ge(bank_full[0], n.after("full0", 1))
                    else:
                        dve.wait_ge(panel_used, n.after("used", 4))
                    dve.tensor_tensor(yrow[:, t, bass.ds(i * 512, 512)], bank[t][:, :], bout_row[:, bass.ds(i * 512, 512)],
                                      ALU.add).then_inc(bank_empty[t], 1)

            def post(row, gain):
                mean_square(1)
                dve.wait_ge(root_ready, n.after("root", 1))
                link(dve.reciprocal(stat[:, 4:4 + TT], stat[:, 4:4 + TT]))
                for t in range(TT):
                    step(dve.scalar_tensor_tensor(yrow[:, t, :], yrow[:, t, :], stat[:, 4 + t:5 + t], row[:, :],
                                                  ALU.mult, ALU.mult))
                for t in range(TT):
                    settled(TT - 1 - t)
                    dve.tensor_tensor(xres[:, t, :], xres[:, t, :], yrow[:, t, :], ALU.add).then_inc(res_ready, 1)
                mean_square(2)
                inverse(2)
                transposed_lo(gain, 0)

            with n.rounds(dve, "post"):
                post(gmix_row, "g_ffn")
            for t in range(TT):
                link(dve.memset(yrow[:, t, :], 0.0))

            with n.rounds(dve, "ffn", FF // 512):
                for blk in range(2):
                    c0 = 6 * blk
                    for c in range(4):
                        split_lo(c0 + c)
                    for j in range(2):
                        dve.wait_ge(bank_empty[j], n.after(f"empty{j}", 2 * blk + 1))
                        if j == 0:
                            dve.wait_ge(bank_full[2], n.after("full2", 2 * blk + 1))
                        else:
                            dve.wait_ge(panel_used, n.after("used", c0 + 4))
                        dve.tensor_tensor(hf[:, j, :], sg[:, j, :], bank[2 + j][:, 0:T], ALU.mult).then_inc(bank_empty[2 + j], 1)
                        dve.wait_ge(hhi_ready, n.after("hhi", 2 * blk + j + 1))
                        dve.tensor_tensor(h_lo[:, j, :], hf[:, j, :], h_hi[:, j, :].bitcast(f32), ALU.subtract).then_inc(hlo_ready, 1)
                    split_lo(c0 + 4)
                    split_lo(c0 + 5)
                    for b in range(8):
                        t, c = (1, b) if b < 4 else (0, b - 4)
                        if b == 7:
                            dve.wait_ge(panel_used, n.after("used", c0 + 6))
                        else:
                            k = 2 * blk + 2 if b in (0, 2) else blk + 1
                            dve.wait_ge(bank_full[b], n.after(f"full{b}", k))
                        dst = yrow[:, t, c * 512:(c + 1) * 512]
                        dve.tensor_tensor(dst, dst, bank[b][:, :], ALU.add).then_inc(bank_empty[b], 1)

            with n.rounds(dve, "post"):
                post(gffn_row, "g_norm1")

            with n.rounds(dve, "qk", 4):
                for c in range(4):
                    split_lo(c)
            with n.rounds(dve, "forget"):
                dve.wait_ge(wfhi_ready, n.after("wf_hi", 1))
                dve.tensor_tensor(wf_lo[:, :, :], wf_raw[:, :, :], wf_hi[:, :, :].bitcast(f32), ALU.subtract).then_inc(wflo_ready, 1)
                for t in range(TT):
                    dve.wait_ge(bank_full[6 + t], n.after(f"full{6 + t}", 1))
                    dve.tensor_tensor(fg[:, 0, t * HEADS:(t + 1) * HEADS], bank[6 + t][:, 0:HEADS], fb[:, :], ALU.add)\
                        .then_inc(bank_empty[6 + t], 1)
                dve.wait_ge(z_ln, n.after("z_ln", 1))
                link(dve.tensor_scalar(fg[:, 3, :], fg[:, 1, :], 1.0, None, ALU.add))
                step(dve.reciprocal(fg[:, 4, :], fg[:, 3, :]))
                link(dve.tensor_scalar(fg[:, 5, :], fg[:, 3, :], -1.0, None, ALU.add))
                link(dve.tensor_tensor(fg[:, 5, :], fg[:, 1, :], fg[:, 5, :], ALU.subtract))
                link(dve.tensor_tensor(fg[:, 5, :], fg[:, 5, :], fg[:, 4, :], ALU.mult))
                link(dve.tensor_tensor(fg[:, 2, :], fg[:, 2, :], fg[:, 5, :], ALU.add))
                link(dve.tensor_scalar(fg[:, 3, :], fg[:, 0, :], 0.0, None, ALU.min))
                dve.tensor_tensor(fg[:, 5, :], fg[:, 3, :], fg[:, 2, :], ALU.subtract).then_inc(logf_ready, 1)
            for g in range(4):
                with n.rounds(dve, "qknorm"):
                    wait(dve, qkn_ready, n.after("qkn", 0))
                    for p in range(2):
                        dve.wait_ge(bank_full[4 + p], n.after(f"full{4 + p}", 1))
                        dve.tensor_scalar(qrs[:, 2 * p:2 * p + 2, :].rearrange("p a t -> p (a t)"), bank[4 + p][:, :],
                                          1.0 / HD, RMS_EPS, ALU.mult, ALU.add).then_inc(bank_empty[4 + p], 1)
                    dve.wait_ge(root_ready, n.after("root", 1))
                    link(dve.reciprocal(qrs[:, :, :], qrs[:, :, :]))
                    four = qk[:, 4 * g:4 * g + 4, :]
                    link(dve.tensor_tensor(four, four, qrs[:, :, :], ALU.mult))
                    dve.tensor_scalar(four, four, col("g_q" if g < 2 else "g_k", 0), None, ALU.mult).then_inc(qkn_ready, 1)
            with n.rounds(dve, "v", 2):
                for c in range(4):
                    split_lo(c)
            with n.rounds(dve, "cum"):
                dve.wait_ge(const_ready, 3)
                for t in range(TT):
                    for h in range(HEADS):
                        ins = dve.tensor_scalar(lfb[:, t, h, :], ones[:, :], fg[:, 5, t * HEADS + h:t * HEADS + h + 1], None, ALU.mult)
                ins.then_inc(lfb_ready, 1)
                dve.wait_ge(bank_full[6], n.after("full6", 1))
                dve.tensor_copy(cq[:, :], bank[6][:, 0:TT * HEADS]).then_inc(bank_empty[6], 1)
                dve.wait_ge(bank_empty[6], n.after("empty6", 1))
            for r in range(HEADS // 2):
                with n.rounds(dve, "score"):
                    for e in range(2):
                        h = 2 * r + e
                        dve.wait_ge(bank_full[e], n.after(f"full{e}", 1))
                        dve.wait_ge(bank_empty[2 + e], n.after(f"empty{2 + e}", 0))
                        dve.tensor_scalar(bias_t[:, e, 0:128], bank[e][:, 0:128], -1.0, cq[:, h:h + 1], ALU.mult, ALU.add)
                        dve.tensor_scalar(bias_t[:, e, 128:384], bank[e][:, 0:256], -1.0, cq[:, HEADS + h:HEADS + h + 1],
                                          ALU.mult, ALU.add).then_inc(bank_empty[e], 1)
                        dve.wait_ge(bank_empty[e], n.after(f"empty{e}", 1))
                        dve.wait_ge(bank_full[2 + e], n.after(f"full{2 + e}", 1))
                        dve.scalar_tensor_tensor(lg0[:, h, :], bank[2 + e][:, 0:128], HD ** -0.5, bias_t[:, e, 0:128],
                                                 ALU.mult, ALU.add)
                        dve.scalar_tensor_tensor(lg1[:, h, :], bank[2 + e][:, 128:384], HD ** -0.5, bias_t[:, e, 128:384],
                                                 ALU.mult, ALU.add).then_inc(bank_empty[2 + e], 1)
            with n.rounds(dve, "softmax"):
                dve.wait_ge(bank_empty[3], n.after("empty3", 0))
                mask = causal[:, :].unsqueeze(1).to_broadcast([128, HEADS, 128])
                step(dve.tensor_tensor(lg0[:, :, :], lg0[:, :, :], mask, ALU.add))
                link(dve.tensor_tensor(lg1[:, :, 128:256], lg1[:, :, 128:256], mask, ALU.add))
                step(dve.tensor_reduce(negmax[:, 0:HEADS], lg0[:, :, :], AX.X, ALU.max))
                link(dve.tensor_reduce(negmax[:, HEADS:2 * HEADS], lg1[:, :, :], AX.X, ALU.max))
                dve.tensor_scalar(negmax[:, :], negmax[:, :], -1.0, None, ALU.mult).then_inc(negmax_ready, 1)
                dve.wait_ge(exp_ready, n.after("exp", 1))
                link(dve.reciprocal(den[:, :], den[:, :]))
                dve.tensor_tensor(lg0[:, :, :], lg0[:, :, :], den[:, 0:HEADS].unsqueeze(2).to_broadcast([128, HEADS, 128]),
                                  ALU.mult).then_inc(prob_ready, 1)
                dve.tensor_tensor(lg1[:, :, :], lg1[:, :, :], den[:, HEADS:2 * HEADS].unsqueeze(2).to_broadcast([128, HEADS, 256]),
                                  ALU.mult).then_inc(prob_ready, 1)
            with n.rounds(dve, "pin", 2):
                for c in range(4):
                    split_lo(c)
            link(dve.tensor_copy(inv_count[:, :], inv_count_i[:, :]))
            link(dve.reciprocal(inv_count[:, :], inv_count[:, :]))
            link(dve.memset(pin[:, :, 0:PADP], 0.0))
            with n.rounds(dve, "pool"):
                dve.wait_ge(bank_empty[3], n.after("empty3", 0))
                for g, w in enumerate(POOL_WINDOWS):
                    src, s = pin[:, 2 * g:2 * g + 2, :], 1
                    own = src
                    for k in range(g + 1):
                        dst = (win_a, win_b)[k % 2][:, :, :]
                        low = 2 * s - 1
                        link(dve.tensor_tensor(dst[:, :, low:], src[:, :, low:], src[:, :, low - s:PADP + T - s], ALU.add))
                        src, s = dst, 2 * s
                    early = slice(PADP, PADP + w - 1)
                    late = slice(PADP + w - 1, PADP + T)
                    step(dve.scalar_tensor_tensor(mixed[:, 2 * g:2 * g + 2, w - 1:], src[:, :, late], 1.0 / w, own[:, :, late],
                                                  ALU.mult, ALU.subtract))
                    part = mixed[:, 2 * g:2 * g + 2, 0:w - 1]
                    link(dve.tensor_tensor(part, src[:, :, early], inv_count[:, 0:w - 1].unsqueeze(1).to_broadcast([128, 2, w - 1]),
                                           ALU.mult))
                    dve.tensor_tensor(part, part, own[:, :, early], ALU.subtract).then_inc(mixed_ready, 1)
                for j in range(8):
                    b = 4 + j % 4
                    dve.wait_ge(evac_hi, n.after("evac", j + 1))
                    dve.scalar_tensor_tensor(po_lo[:, j, :], bank[b][:, 0:T], col("pool_scale", j), po_hi[:, j, :].bitcast(f32),
                                             ALU.mult, ALU.subtract).then_inc(bank_empty[b], 1)
            for r in range(HEADS // 2):
                with n.rounds(dve, "heads"):
                    for e in range(2):
                        dve.wait_ge(evac_hi, n.after("evac", e + 1))
                        dve.tensor_tensor(at_lo[:, 2 * r + e, :], bank[2 + e][:, 0:T], at_hi[:, 2 * r + e, :].bitcast(f32),
                                          ALU.subtract).then_inc(bank_empty[2 + e], 1)
            with n.rounds(dve, "merge", 4) as i:
                for c in range(10):
                    split_lo(c)
                for j in range(4):
                    dve.wait_ge(bank_empty[j], n.after(f"empty{j}", 1))
                    if j < 3:
                        dve.wait_ge(bank_full[j], n.after(f"full{j}", 2))
                    else:
                        dve.wait_ge(panel_used, n.after("used", 10))
                    dve.tensor_tensor(part0[:, j, :], gate0[:, j, :], bank[j][:, 0:T], ALU.mult).then_inc(bank_empty[j], 1)
                split_lo(10)
                split_lo(11)
                for j in range(4):
                    dve.wait_ge(bank_empty[4 + j], n.after(f"empty{4 + j}", 1))
                    if j < 3:
                        dve.wait_ge(bank_full[4 + j], n.after(f"full{4 + j}", 2))
                    else:
                        dve.wait_ge(panel_used, n.after("used", 12))
                    dve.tensor_tensor(part1[:, j, :], gate1[:, j, :], bank[4 + j][:, 0:T], ALU.mult).then_inc(bank_empty[4 + j], 1)
                for j in range(4):
                    dve.wait_ge(bank_empty[4 + j], n.after(f"empty{4 + j}", 2))
                    dve.tensor_tensor(merged[:, bass.ds(i * 4 + j, 1), :].rearrange("p a t -> p (a t)"), part0[:, j, :],
                                      part1[:, j, :], ALU.add).then_inc(part_ready, 1)
                dve.wait_ge(part_ready, n.after("part", 4))
            with n.rounds(dve, "merged"):
                for g in range(4):
                    dve.wait_ge(merged_hi, n.after("merged_hi", g + 1))
                    dve.tensor_tensor(a_lo[:, 4 * g:4 * g + 4, 0:T], merged[:, 4 * g:4 * g + 4, :],
                                      a_hi[:, 4 * g:4 * g + 4, 0:T].bitcast(f32), ALU.subtract).then_inc(act_ready, 1)
            with n.rounds(dve, "w_out_2", 4) as i:
                for c in range(4):
                    split_lo(c)
                for t in range(TT):
                    if t == 0:
                        dve.wait_ge(bank_full[0], n.after("full0", 1))
                    else:
                        dve.wait_ge(panel_used, n.after("used", 4))
                    dst = xres[:, t, bass.ds(i * 512, 512)]
                    dve.tensor_tensor(dst, dst, bank[t][:, :], ALU.add).then_inc(bank_empty[t], 1)
            with n.rounds(dve, "post_2"):
                mean_square(1)
                inverse(1)
                dve.wait_ge(late_loaded, 32)
                for t in range(TT):
                    dve.wait_ge(xs_ready, n.after("xs", t + 1))
                    dve.tensor_tensor(xn[:, t, :], xs[:, t, :], g2_row[:, :], ALU.mult).then_inc(xn_ready, 1)
                transposed_lo(None, 0)
            with n.rounds(dve, "query", 3):
                for c in range(4):
                    split_lo(c)
            with n.rounds(dve, "query"):
                for c in range(3):
                    split_lo(c)
            with n.rounds(dve, "keys"):
                pass

            def apart():
                dve.sem_inc(dve_passed, 1)

            def sixteen(values, indices, src, rest):
                apart()
                link(dve.max(values[:, 0:8], src))
                apart()
                step(dve.max_index(indices[:, 0:8], values[:, 0:8], src))
                link(dve.match_replace(rest, values[:, 0:8], src, LOWEST))
                apart()
                link(dve.max(values[:, 8:16], rest))
                apart()
                link(dve.max_index(indices[:, 8:16], values[:, 8:16], rest))

            def route(th, parity, k, free):
                square = [128, TOPK, TOPK]
                link(dve.tensor_copy(sc[:, :], score[:, bass.ds(th, 1), :].rearrange("p a k -> p (a k)")))
                for half in range(2):
                    sixteen(val[:, half * TOPK:(half + 1) * TOPK], ind[:, half * TOPK:(half + 1) * TOPK],
                            sc[:, half * NKEYS:(half + 1) * NKEYS], sc_rest[:, :])
                step(dve.tensor_copy(indf[:, :], ind[:, :]))
                grid = cand[:, :].rearrange("p (a b) -> p a b", a=TOPK)
                link(dve.tensor_tensor(grid, val[:, 0:TOPK].unsqueeze(2).to_broadcast(square),
                                       val[:, TOPK:].unsqueeze(1).to_broadcast(square), ALU.add))
                sixteen(top[:, :], pos[:, :], cand[:, :], cand_rest[:, :])
                dve.tensor_scalar(gsum[:, 0:1], top[:, 0:1], -1.0, None, ALU.mult).then_inc(gate_max, 1)
                link(dve.tensor_scalar(pos1[:, :], pos[:, :], 4, None, ALU.logical_shift_right))
                step(dve.tensor_copy(posf[:, 0:TOPK], pos1[:, :]))
                link(dve.tensor_scalar(pos[:, :], pos[:, :], TOPK - 1, None, ALU.bitwise_and))
                link(dve.tensor_copy(posf[:, TOPK:], pos[:, :]))
                picks = pick[:, :].rearrange("p (k a) -> p k a", a=TOPK)
                for half in range(2):
                    part = slice(half * TOPK, (half + 1) * TOPK)
                    link(dve.tensor_tensor(picks, iota_f[:, :].unsqueeze(1).to_broadcast(square),
                                           posf[:, part].unsqueeze(2).to_broadcast(square), ALU.is_equal))
                    link(dve.tensor_tensor(picks, picks, indf[:, part].unsqueeze(1).to_broadcast(square), ALU.mult))
                    link(dve.tensor_reduce(chosen[:, part], picks, AX.X, ALU.add))
                link(dve.scalar_tensor_tensor(expert_f[:, :], chosen[:, 0:TOPK], float(NKEYS), chosen[:, TOPK:], ALU.mult, ALU.add))
                wait(dve, v_used, free)
                dve.tensor_copy(expert[parity][:, :], expert_f[:, :]).then_inc(expert_ready, 1)
                dve.wait_ge(gate_exp, n.after("gate_exp", k))
                link(dve.reciprocal(gsum[:, 2:3], gsum[:, 1:2]))
                link(dve.tensor_scalar(gate[parity][:, :], gate[parity][:, :], gsum[:, 2:3], None, ALU.mult))

            def heads(th, t, more=True):
                for e in range(2):
                    for q in range(TOPK // BATCH):
                        if q == 2 and (more or e == 0):
                            route(th + (e + 1), 1 - e, e + 1, n.after("v_used", e * TOPK))
                        for s in range(q * BATCH, (q + 1) * BATCH):
                            dve.wait_ge(u_loaded[s % NU], n.after("u_rows", e * 4 + s // NU + 1) * 16)
                            dve.tensor_tensor_reduce(out=u_slot[s % NU][:, :], in0=u_slot[s % NU][:, :], in1=xn[:, t, :],
                                                     scale=1.0, scalar=0.0, op0=ALU.mult, op1=ALU.add,
                                                     accum_out=adot[e][:, s:s + 1]).then_inc(dot_ready, 1)
                        part = slice(q * BATCH, (q + 1) * BATCH)
                        dve.wait_ge(gelu_ready, n.after("gelu", e * 4 + q + 1))
                        dve.tensor_tensor(hid[e][:, part], gelu[e][:, part], gate[e][:, part], ALU.mult).then_inc(hid_ready, 1)

            dve.wait_ge(iota_ready, 1)
            link(dve.tensor_copy(iota_f[:, :], iota_i[:, :]))
            dve.wait_ge(bank_empty[7], n.after("empty7", 0))
            with n.rounds(dve, "route"):
                route(0, 0, 1, 0)
            links = 2 * PER_ROUTE
            with n.rounds(dve, "pair"):
                heads(0, 0)
            with n.rounds(dve, "pair", 3, dve_step=links) as i:
                heads(i * 2 + 2, 0)
            with n.rounds(dve, "pair", 3, dve_step=links) as i:
                heads(i * 2 + 8, 1)
            with n.rounds(dve, "pair"):
                heads(14, 1, more=False)
            dve.wait_ge(acc_done, 1)
            for t in range(TT):
                for c in range(4):
                    part = slice(c * 512, (c + 1) * 512)
                    ins = dve.tensor_tensor(out_row[:, t, part], xres[:, t, part], bank[4 * t + c][:, :], ALU.add)
                ins.then_inc(out_ready, 1)

        @block.tensor
        def _(pe):
            n = Counts()

            def into(b, k):
                wait(pe, bank_empty[b], n.after(f"empty{b}", k))

            def panel(c):
                pe.wait_ge(split_ready, n.after("split", c))
                return c % 2

            def product(dst, left, right, start, stop):
                pe.matmul(dst, left[0], right[0], start=start, stop=False)
                pe.matmul(dst, left[0], right[1], start=False, stop=False)
                return pe.matmul(dst, left[1], right[0], start=False, stop=stop)

            def transposes(src, ready, key):
                for t in range(TT):
                    pe.wait_ge(ready, n.after(key, t + 1))
                    for b in range(4):
                        into(4 * t + b, 0)
                        for q in range(4):
                            k = 4 * b + q
                            ins = pe.transpose(bank[4 * t + b][:, q * 128:(q + 1) * 128], src[:, t, k * 128:(k + 1) * 128], ident[:, :])
                        ins.then_inc(bank_full[4 * t + b], 1)

            def feature_major(banks, tokens, c0, panels, kper, k):
                width = len(banks) * 128
                for c in range(panels):
                    s = panel(c0 + c)
                    for j, b in enumerate(banks):
                        for kk in range(kper):
                            kt = c * kper + kk
                            if kt == 0:
                                into(b, k)
                            where = slice(kk * width + j * 128, kk * width + (j + 1) * 128)
                            right = tokens(kt)
                            ins = product(bank[b][:, 0:right[0].shape[-1]], (w_hi[s][:, where], w_lo[s][:, where]), right,
                                          kt == 0, kt == panels * kper - 1)
                        if j == len(banks) - 1:
                            ins.then_inc(panel_used, 1)
                        elif c == panels - 1:
                            ins.then_inc(bank_full[b], 1)

            def token_major(banks):
                for c in range(4):
                    s = panel(c)
                    for t, b in enumerate(banks):
                        for kk in range(4):
                            kt = c * 4 + kk
                            if kt == 0:
                                into(b, 0)
                            tile, where = slice(t * 128, (t + 1) * 128), slice(kk * 512, (kk + 1) * 512)
                            ins = product(bank[b][:, :], (a_hi[:, kt, tile], a_lo[:, kt, tile]),
                                          (w_hi[s][:, where], w_lo[s][:, where]), kt == 0, kt == KT - 1)
                        if t == TT - 1:
                            ins.then_inc(panel_used, 1)
                        elif c == 3:
                            ins.then_inc(bank_full[b], 1)

            def all_tokens(k):
                return a_hi[:, k, :], a_lo[:, k, :]

            def tokens(k):
                return a_hi[:, k, 0:T], a_lo[:, k, 0:T]

            pe.wait_ge(const_ready, 3)
            with n.rounds(pe, "norm0"):
                transposes(xs0, xs_ready, "xs")
                pe.wait_ge(xs_ready, n.after("xs", TT + 1))
                into(0, 1)
                for k in range(KT):
                    ins = pe.transpose(bank[0][:, k * META:(k + 1) * META], meta_sb[:, k * 128:(k + 1) * 128], ident[0:META, 0:META])
                ins.then_inc(panel_used, 1)
            into(0, 0)
            with n.rounds(pe, "w_in", 4):
                feature_major((0, 1, 2, 3), all_tokens, 0, 4, 4, 0)
                feature_major((4, 5, 6, 7), all_tokens, 4, 4, 4, 0)
            with n.rounds(pe, "ln"):
                pe.wait_ge(conv_ready, 1)
                into(0, 0)
                for k in range(KT):
                    ins = pe.matmul(bank[0][:, 0:T], ones[:, :], cvo[:, k, :], start=k == 0, stop=k == KT - 1)
                ins.then_inc(bank_full[0], 1)
                into(1, 0)
                for k in range(KT):
                    if k % 4 == 0:
                        pe.wait_ge(dev_sq_ready, n.after("dev_sq", k // 4 + 1))
                    ins = pe.matmul(bank[1][:, 0:T], ones[:, :], sq[:, k, :], start=k == 0, stop=k == KT - 1)
                ins.then_inc(bank_full[1], 1)
                pe.wait_ge(act_ready, n.after("act", 4))
            with n.rounds(pe, "w_out", 4):
                token_major((0, 1))
            with n.rounds(pe, "post"):
                transposes(xs, xs_ready, "xs")
            into(7, 0)
            with n.rounds(pe, "ffn", FF // 512):
                for blk in range(2):
                    c0 = 6 * blk
                    feature_major((0, 1), tokens, c0, 2, 8, 2 * blk)
                    feature_major((2, 3), tokens, c0 + 2, 2, 8, 2 * blk)
                    for f in range(2):
                        s = panel(c0 + 4 + f)
                        pe.wait_ge(hlo_ready, n.after("hlo", 2 * blk + f + 1))
                        for t in ((0, 1), (1, 0))[f]:
                            for c in range(4):
                                b = c if t else 4 + c
                                if f == 0:
                                    into(b, 2 * blk + 1 if t else blk)
                                tile, where = slice(t * 128, (t + 1) * 128), slice(c * 512, (c + 1) * 512)
                                ins = product(bank[b][:, :], (h_hi[:, f, tile], h_lo[:, f, tile]),
                                              (w_hi[s][:, where], w_lo[s][:, where]), f == 0, f == 1)
                                if f == 1 and b < 7:
                                    ins.then_inc(bank_full[b], 1)
                        ins.then_inc(panel_used, 1)
            with n.rounds(pe, "post"):
                transposes(xs, xs_ready, "xs")
            into(7, 0)
            with n.rounds(pe, "qk", 4):
                feature_major((0, 1, 2, 3), tokens, 0, 4, 4, 0)
            with n.rounds(pe, "forget"):
                pe.wait_ge(wflo_ready, n.after("wf_lo", 1))
                for t in range(TT):
                    into(6 + t, 0)
                    for k in range(KT):
                        tile = slice(t * 128, (t + 1) * 128)
                        ins = product(bank[6 + t][:, 0:HEADS], (a_hi[:, k, tile], a_lo[:, k, tile]),
                                      (wf_hi[:, k, :], wf_lo[:, k, :]), k == 0, k == KT - 1)
                    ins.then_inc(bank_full[6 + t], 1)
            for g in range(4):
                with n.rounds(pe, "qknorm"):
                    pe.wait_ge(qsq_ready, n.after("qsq", 1))
                    for p in range(2):
                        into(4 + p, 0)
                        pe.matmul(bank[4 + p][:, :], ones[:, :], qsq[:, 2 * p:2 * p + 2, :], start=True, stop=True)\
                            .then_inc(bank_full[4 + p], 1)
            with n.rounds(pe, "v", 2):
                token_major((4, 5))
            with n.rounds(pe, "cum"):
                pe.wait_ge(logf_ready, n.after("logf", 0))
                into(6, 0)
                first, second = fg[:, 5, 0:HEADS], fg[:, 5, HEADS:2 * HEADS]
                pe.matmul(bank[6][:, 0:HEADS], tri_ones[:, 0:128], first, start=True, stop=True)
                pe.matmul(bank[6][:, HEADS:2 * HEADS], ones[:, :], first, start=True, stop=False)
                pe.matmul(bank[6][:, HEADS:2 * HEADS], tri_ones[:, 0:128], second, start=False, stop=True).then_inc(bank_full[6], 1)
                pe.wait_ge(lfb_ready, n.after("lfb", 1))
                pe.wait_ge(qkn_ready, n.after("qkn", 0))
            for r in range(HEADS // 2):
                with n.rounds(pe, "score"):
                    for e in range(2):
                        h = 2 * r + e
                        into(e, 0)
                        pe.matmul(bank[e][:, 0:256], lfb[:, 0, h, :], tri_ones[:, :], start=True, stop=False)
                        pe.matmul(bank[e][:, 128:256], lfb[:, 1, h, :], tri_ones[:, 0:128], start=False, stop=True).then_inc(bank_full[e], 1)
                        into(2 + e, 0)
                        pe.matmul(bank[2 + e][:, 0:128], qk[:, h, 0:128], qk[:, HEADS + h, 0:128], start=True, stop=True)
                        pe.matmul(bank[2 + e][:, 128:384], qk[:, h, 128:256], qk[:, HEADS + h, :], start=True, stop=True)\
                            .then_inc(bank_full[2 + e], 1)
            with n.rounds(pe, "softmax"):
                pass
            with n.rounds(pe, "pin", 2):
                feature_major((0, 1, 2, 3), tokens, 0, 4, 4, 0)
            with n.rounds(pe, "pool"):
                for j in range(8):
                    b, g = 4 + j % 4, j // 2
                    pe.wait_ge(mixed_ready, n.after("mixed", g + 1))
                    into(b, j // 4)
                    for ci in range(2):
                        ins = pe.matmul(bank[b][:, 0:T], group_sb[:, g, ci, (j % 2) * 128:(j % 2 + 1) * 128], mixed[:, 2 * g + ci, :],
                                        start=ci == 0, stop=ci == 1)
                    ins.then_inc(bank_full[b], 1)
            pe.wait_ge(prob_ready, 2)
            for r in range(HEADS // 2):
                with n.rounds(pe, "heads"):
                    for e in range(2):
                        h = 2 * r + e
                        into(e, 0)
                        pe.transpose(bank[e][:, 0:128], lg0[:, h, :], ident[:, :])
                        pe.transpose(bank[e][:, 128:256], lg1[:, h, 0:128], ident[:, :])
                        pe.transpose(bank[e][:, 256:384], lg1[:, h, 128:256], ident[:, :]).then_inc(bank_full[e], 1)
                    for e in range(2):
                        h = 2 * r + e
                        head = slice(h * HD, (h + 1) * HD)
                        into(e, 1)
                        into(2 + e, 0)
                        pe.matmul(bank[2 + e][:, 0:T], vrow[:, 0, head], pts[:, e, 0:256], start=True, stop=False)
                        pe.matmul(bank[2 + e][:, 128:256], vrow[:, 1, head], pts[:, e, 256:384], start=False, stop=True)\
                            .then_inc(bank_full[2 + e], 1)
            into(3, 0)
            into(7, 0)
            with n.rounds(pe, "merge", 4):
                feature_major((0, 1, 2, 3), tokens, 0, 4, 4, 0)
                feature_major((4, 5, 6, 7), tokens, 4, 4, 4, 0)
                feature_major((0, 1, 2, 3), lambda k: (at_hi[:, k, :], at_lo[:, k, :]), 8, 2, 4, 1)
                feature_major((4, 5, 6, 7), lambda k: (po_hi[:, k, :], po_lo[:, k, :]), 10, 2, 4, 1)
            with n.rounds(pe, "merged"):
                pe.wait_ge(act_ready, n.after("act", 4))
            with n.rounds(pe, "w_out_2", 4):
                token_major((0, 1))
            with n.rounds(pe, "post_2"):
                transposes(xn, xn_ready, "xn")
            into(7, 0)
            with n.rounds(pe, "query", 4):
                feature_major((0, 1, 2, 3), tokens, 0, 4, 4, 0)
            into(3, 0)
            pe.wait_ge(late_loaded, 32)
            with n.rounds(pe, "keys"):
                for t in range(TT):
                    for b in range(4):
                        into(4 * t + b, 0)
                        for q in range(4):
                            hh = 4 * b + q
                            ins = pe.matmul(bank[4 * t + b][:, q * 128:(q + 1) * 128], qp[:, hh, t * 128:(t + 1) * 128],
                                            keys_sb[:, hh, :], start=True, stop=True)
                        ins.then_inc(bank_full[4 * t + b], 1)

            def nothing(t, start):
                for c in range(4):
                    ins = pe.matmul(bank[4 * t + c][:, :], zeros[:, :], xn[:, 0, 0:512], start=start, stop=not start)
                return ins

            def adds(t):
                for e in range(2):
                    for s in range(TOPK):
                        pe.wait_ge(diag_ready, n.after("diag", e * TOPK + s + 1))
                        pe.wait_ge(v_loaded[s % NV], n.after("v_rows", e * 2 + s // NV + 1) * 16)
                        for c in range(4):
                            ins = pe.matmul(bank[4 * t + c][:, :], diag[s % NDIAG][:, :], v_slot[s % NV][:, c * 512:(c + 1) * 512],
                                            start=False, stop=False)
                        ins.then_inc(v_used, 1)

            pe.wait_ge(zeros_ready, 1)
            for b in range(8):
                into(b, 0)
            for t in range(TT):
                nothing(t, True)
                with n.rounds(pe, "pair"):
                    adds(t)
                with n.rounds(pe, "pair", PH // 2 - 1):
                    adds(t)
            nothing(0, False)
            nothing(1, False).then_inc(acc_done, 1)


INPUTS = ("stream", "columns", "x", "meta", "b_out", "g_mix_post", "g_ffn_post", "g_norm2", "w_forget",
          "forget_bias", "group_w", "keys", "expert_u", "expert_v")


def laid_out(a):
    def wide(w):
        k, m = w.shape
        return w.reshape(k // 512, 4, 128, m // 512, 512).transpose(3, 0, 2, 1, 4).reshape(m // 512, k // 512, 128, 2048)

    def narrow(w):
        return w.reshape(2, 8, 128, FF // 256, 256).transpose(3, 0, 2, 1, 4).reshape(FF // 256, 2, 128, 2048)

    def column(v):
        return v.reshape(-1, 128).T

    w_in = wide(a["conv_w_in"][0])
    first = np.concatenate([w_in[0:4], w_in[4:8]], 1).reshape(-1, 128, 2048)
    ffn = np.concatenate([narrow(a["ffn_w_gate"][0]), narrow(a["ffn_w_up"][0]),
                          a["ffn_w_down"][0].reshape(FF // 256, 2, 128, 2048)], 1).reshape(-1, 128, 2048)
    fox, w2 = HEADS * HD, a["w_in_2"][0]
    edges = [2 * fox, 3 * fox, 3 * fox + HEADS, 3 * fox + HEADS + POOL_W]
    w_qk, w_v, w_f, w_p, w_g = (w2[:, i:j] for i, j in zip([0] + edges, edges + [w2.shape[1]]))
    gates = wide(w_g)
    merge = np.concatenate([gates[0:4], gates[4:8], wide(a["w_branch_attn_2"][0]), wide(a["w_branch_pool_2"][0])], 1)
    flat = [w.reshape(-1, 128, 2048) for w in (wide(a["conv_w_out"][0]), ffn, wide(w_qk), wide(w_v), wide(w_p), merge,
                                               wide(a["w_out_2"][0]), wide(a["peer_w_query_2"][0]))]
    b_in = a["conv_b_in"][0]
    table = {"g_mix": column(a["norm_mix_pre"][0]), "b_a": column(b_in[:D]), "b_g": column(b_in[D:]),
             "w_dw": a["conv_w_dw"][0].reshape(TAPS, KT, 128).transpose(2, 1, 0).reshape(128, KT * TAPS),
             "b_dw": column(a["conv_b_dw"][0]), "ln_g": column(a["conv_ln_g"][0]), "ln_b": column(a["conv_ln_b"][0]),
             "g_ffn": column(a["norm_ffn_pre"][0]), "g_norm1": column(a["norm1_g_2"][0]),
             "g_q": column(a["q_norm_g_2"][0]), "g_k": column(a["k_norm_g_2"][0]), "pool_scale": column(a["pool_scale_2"][0])}
    keys = np.stack([a["peer_sub_keys_1_2"][0], a["peer_sub_keys_2_2"][0]], 1)
    return {
        "stream": np.concatenate([first] + flat, 0),
        "columns": np.concatenate([table[name] for name, _ in COLUMNS], 1),
        "x": a["x"][0], "meta": a["meta_tokens"], "b_out": a["conv_b_out"][0],
        "g_mix_post": a["norm_mix_post"][0], "g_ffn_post": a["norm_ffn_post"][0], "g_norm2": a["norm2_g_2"][0],
        "w_forget": w_f.reshape(KT, 128, HEADS).transpose(1, 0, 2),
        "forget_bias": a["forget_bias_2"][0],
        "group_w": a["pool_group_w_2"][0].reshape(4, 2, 128, 256).transpose(2, 0, 1, 3),
        "keys": keys.transpose(3, 0, 1, 2).reshape(128, 2 * PH, NKEYS),
        "expert_u": a["peer_expert_u_2"][0], "expert_v": a["peer_expert_v_2"][0],
    }


def kernel(**inputs):
    import concourse.bacc as bacc
    from concourse.bass_utils import run_bass_kernel_spmd

    nc = bacc.Bacc("TRN2", target_bir_lowering=False, num_devices=1)
    laid = laid_out({name: np.asarray(a) for name, a in inputs.items()})
    arrays, args = {}, []
    for name in INPUTS:
        a = np.ascontiguousarray(laid[name])
        arrays[f"in_{name}"] = a
        args.append(nc.dram_tensor(f"in_{name}", a.shape, mybir.dt.from_np(a.dtype), kind="ExternalInput").ap())
    args.append(nc.dram_tensor("out_0", (T, D), mybir.dt.float32, kind="ExternalOutput").ap())
    two_layers(nc, *args)
    r = run_bass_kernel_spmd(nc, [arrays], core_ids=[0])
    return r.results[0]["out_0"].reshape(1, T, D)
```

```python
from contextlib import ExitStack, contextmanager

import numpy as np
import concourse.bass as bass
from concourse import mybir

D = 2048
T, META = 256, 16
TT = T // 128
KT = D // 128
L = META + T
FF = 5632
TAPS = 31
HEADS, HD = 8, 128
POOL_W = 1024
POOL_WINDOWS = (2, 4, 8, 16)
PADP = 16
PH, TOPK, NKEYS = 8, 16, 128
SLOTS = PH * TOPK
RMS_EPS, LN_EPS = 1e-6, 1e-5
LOWEST = -3.0e38
MASKED = -1.0e30

PANELS = [("w_in", 32), ("w_out", 16), ("ffn", 132), ("qk", 16), ("v", 8), ("pin", 8),
          ("merge", 48), ("w_out_2", 16), ("query", 16)]
NPANELS = sum(n for _, n in PANELS)

COLUMNS = [("g_mix", KT), ("b_a", KT), ("b_g", KT), ("w_dw", KT * TAPS), ("b_dw", KT), ("ln_g", KT),
           ("ln_b", KT), ("g_ffn", KT), ("g_norm1", KT), ("g_q", 1), ("g_k", 1), ("pool_scale", 8)]
COL = {}
for _name, _n in COLUMNS:
    COL[_name] = sum(n for _, n in COLUMNS[:len(COL)])
NCOLS = sum(n for _, n in COLUMNS)


PER_ROUTE = 31

BANKS8 = range(8)


def per_round(**signals):
    full, empty = signals.pop("full", {}), signals.pop("empty", {})
    out = dict(signals)
    out.update({f"full{b}": k for b, k in full.items()})
    out.update({f"empty{b}": k for b, k in empty.items()})
    if "used" in out:
        out["split"] = out["hi"] = out["used"]
        out["quad"] = out["used"] // 4
    return out


def each(banks, k=1):
    return {b: k for b in banks}


PER_ROUND = {
    "norm0": dict(per_round(ssq=1, ms=1, root=1, rstd=1, xs=TT + 1, evac=9, full=each(BANKS8),
                            empty={**each(BANKS8), 0: 2}), used=1, hi=1),
    "w_in": dict(per_round(used=8, hi_half=8, conv_split=8, full=each((0, 2, 4, 6)), empty=each(BANKS8)), split=0),
    "ln": per_round(split=1, dev=4, dev_sq=4, root=1, ln=4, silu=KT // 4, silu_hi=4, act=4, full=each((0, 1)), empty=each((0, 1))),
    "w_out": per_round(used=4, full={0: 1}, empty=each((0, 1))),
    "post": per_round(ssq=2, ms=2, root=2, rstd=1, xs=TT, res=TT, evac=8, full=each(BANKS8), empty=each(BANKS8)),
    "ffn": per_round(used=12, hhi=4, hlo=4, full={**each((0, 2, 4, 6), 2), **each((1, 3, 5))}, empty=each(BANKS8, 2)),
    "qk": per_round(used=4, full=each((0, 1, 2)), empty=each(range(4))),
    "forget": per_round(wf_hi=1, wf_lo=1, z_step=2, z_ln=1, logf=1, full=each((6, 7)), empty=each((6, 7))),
    "qknorm": per_round(qsq=1, root=1, qkn=1, full=each((4, 5)), empty=each((4, 5))),
    "v": per_round(used=4, full={4: 1}, empty=each((4, 5))),
    "cum": per_round(lfb=1, full={6: 1}, empty={6: 1}),
    "score": per_round(full=each(range(4)), empty=each(range(4))),
    "softmax": per_round(negmax=1, exp=1, prob=2),
    "pin": per_round(used=4, full=each((0, 1, 2)), empty=each(range(4))),
    "pool": per_round(mixed=4, evac=8, full=each(range(4, 8), 2), empty=each(range(4, 8), 2)),
    "heads": per_round(evac=2, full=each(range(4)), empty=each(range(4))),
    "merge": per_round(used=12, part=4, full=each((0, 1, 2, 4, 5, 6), 2), empty=each(BANKS8, 2)),
    "merged": per_round(merged_hi=4, act=4),
    "w_out_2": per_round(used=4, full={0: 1}, empty=each((0, 1))),
    "post_2": per_round(ssq=1, ms=1, root=1, rstd=1, xs=TT, evac=8, xn=TT, full=each(BANKS8), empty=each(BANKS8)),
    "query": per_round(used=4, full=each((0, 1, 2)), empty=each(range(4))),
    "keys_0": per_round(full={4: 1}, empty={4: 1}),
    "keys": per_round(full=each(range(1, 8)), empty=each(range(1, 8))),
    "route": per_round(expert=1, gate_max=1, gate_exp=1),
    "pair": per_round(expert=2, gate_max=2, gate_exp=2, dot=2 * TOPK, gelu=8, hid=8, diag=2 * TOPK, v_used=2 * TOPK,
                      u_rows=8, v_rows=4),
}


class Counts:

    def __init__(self):
        self.base, self.low = {}, {}

    def after(self, key, k):
        base = self.base.get(key, 0)
        assert isinstance(base, int) or self.low.get(key, 0) + k > 0, (key, k)
        return base + k

    @contextmanager
    def rounds(self, engine, stage, times=1, **own):
        per = {**PER_ROUND[stage], **own}
        start = dict(self.base)
        self.low = start
        if times == 1:
            yield 0
            start = self.base
        else:
            with engine.Fori(0, times) as i:
                self.base = {**start, **{key: start.get(key, 0) + i * k for key, k in per.items()}}
                yield i
        self.base = {**start, **{key: start.get(key, 0) + times * k for key, k in per.items()}}
        self.low = dict(self.base)


def wait(engine, semaphore, value):
    if not (isinstance(value, int) and value <= 0):
        engine.wait_ge(semaphore, value)


def wait_apart(engine, semaphore, value, passed):
    if not (isinstance(value, int) and value <= 0):
        engine.wait_ge(semaphore, value)
        if not isinstance(value, int):
            engine.sem_inc(passed, 1)


def two_layers(nc, stream, columns, x, meta, b_out, g_mix_post, g_ffn_post, g_norm2, w_forget,
               forget_bias, group_w, keys, expert_u, expert_v, out):
    f32, f32r, u32 = mybir.dt.float32, mybir.dt.float32r, mybir.dt.uint32
    ACT, ALU, AX = mybir.ActivationFunctionType, mybir.AluOpType, mybir.AxisListType

    K = 1024
    at = (nc.sbuf_base + 63) // 64 * 64
    names = set()

    def place(name, shape, offset, dt=f32):
        assert name not in names
        names.add(name)
        return nc.alloc_sbuf_tensor_at(name, shape, dt, offset=offset)

    def keep(name, shape, dt=f32):
        nonlocal at
        t = place(name, shape, at, dt)
        at += (int(np.prod(shape[1:])) * 4 + 63) // 64 * 64
        return t

    cols = keep("s_cols", [128, NCOLS])
    ident = keep("s_ident", [128, 128])
    ones = keep("s_ones", [128, 128])
    tri_ones = keep("s_tri_ones", [128, 2 * 128])
    causal = keep("s_causal", [128, 128])
    group_sb = keep("s_group_w", [128, 4, 2, 256])
    wf_raw = keep("s_wf_raw", [128, KT, HEADS])
    wf_hi = keep("s_wf_hi", [128, KT, HEADS], f32r)
    wf_lo = keep("s_wf_lo", [128, KT, HEADS], f32r)
    fb = keep("s_forget_bias", [128, HEADS])
    stat = keep("s_stat", [128, 8])
    fg = keep("s_forget", [128, 6, TT * HEADS])
    cq = keep("s_cq", [128, TT * HEADS])
    negmax = keep("s_negmax", [128, TT * HEADS])
    den = keep("s_den", [128, TT * HEADS])
    inv_count = keep("s_inv_count", [128, 16])
    inv_count_i = keep("s_inv_count_i", [128, 16], mybir.dt.int32)
    xres = keep("s_xres", [128, TT, D])
    ring0 = at
    raw = [keep(f"s_raw{i}", [128, 2048]) for i in range(4)]
    w_hi = [keep(f"s_w_hi{i}", [128, 2048], f32r) for i in range(2)]
    w_lo = [keep(f"s_w_lo{i}", [128, 2048], f32r) for i in range(2)]
    a_hi = keep("s_a_hi", [128, KT, L], f32r)
    a_lo = keep("s_a_lo", [128, KT, L], f32r)
    S = at
    xs = place("s_xs", [128, TT, D], S + 16 * K)
    xs0 = place("s_xs0", [128, TT, D], S + 0)
    meta_sb = place("s_meta", [META, D], S + 16 * K)
    cvg = place("s_cvg", [128, 4, TAPS - 1 + L], S + 0)
    cacc = place("s_cacc", [128, 4, T], S + 5 * K)
    sig = place("s_sig", [128, 4, L], S + 9 * K)
    cvo = place("s_cvo", [128, KT, T], S + 16 * K)
    sq = place("s_sq", [128, KT, T], S + 32 * K)
    mean = place("s_mean", [128, T], S + 48 * K)
    rstd = place("s_rstd", [128, T], S + 49 * K)
    bout_row = place("s_bout_row", [128, D], S + 50 * K)
    gmix_row = place("s_gmix_row", [128, D], S + 58 * K)
    gffn_row = place("s_gffn_row", [128, D], S + 66 * K)
    yrow = place("s_yrow", [128, TT, D], S + 0)
    sg = place("s_sg", [128, 2, T], S + 32 * K)
    hf = place("s_hf", [128, 4, T], S + 34 * K)
    h_hi = place("s_h_hi", [128, 4, T], S + 38 * K, f32r)
    h_lo = place("s_h_lo", [128, 4, T], S + 42 * K, f32r)
    qk = place("s_qk", [128, 2 * HEADS, T], S + 0)
    vrow = place("s_vrow", [128, TT, HEADS * HD], S + 16 * K)
    pin = place("s_pin", [128, 8, PADP + T], S + 24 * K)
    mixed = place("s_mixed", [128, 8, T], S + 33 * K)
    qsq = place("s_qsq", [128, 4, T], S + 41 * K)
    qrs = place("s_qrs", [128, 4, T], S + 45 * K)
    lg0 = place("s_lg0", [128, HEADS, 128], S + 41 * K)
    lg1 = place("s_lg1", [128, HEADS, 256], S + 45 * K)
    lfb = place("s_lfb", [128, TT, HEADS, 128], S + 53 * K)
    at_hi = place("s_at_hi", [128, HEADS, T], S + 61 * K, f32r)
    at_lo = place("s_at_lo", [128, HEADS, T], S + 69 * K, f32r)
    bias_t = place("s_bias_t", [128, 2, 384], S + 61 * K)
    win_a = place("s_win_a", [128, 2, PADP + T], S + 65 * K)
    win_b = place("s_win_b", [128, 2, PADP + T], S + 69 * K)
    po_hi = place("s_po_hi", [128, 8, T], S + 24 * K, f32r)
    po_lo = place("s_po_lo", [128, 8, T], S + 53 * K, f32r)
    pts = place("s_pts", [128, 2, 384], S + 33 * K)
    merged = place("s_merged", [128, KT, T], S + 0)
    gate0 = place("s_gate0", [128, 4, T], S + 16 * K)
    gate1 = place("s_gate1", [128, 4, T], S + 20 * K)
    part0 = place("s_part0", [128, 4, T], S + 33 * K)
    part1 = place("s_part1", [128, 4, T], S + 37 * K)
    xn = place("s_xn", [128, TT, D], S + 0)
    g2_row = place("s_g2_row", [128, D], S + 33 * K)
    keys_sb = place("s_keys", [128, 2 * PH, NKEYS], S + 41 * K)
    qp = place("s_qp", [128, 2 * PH, T], S + 49 * K)
    score = place("s_score", [128, TT * PH, 2 * NKEYS], S + 16 * K)
    NU, NV, NDIAG, BATCH, LEAD = 4, 8, 4, 4, 3
    u_slot = [place(f"s_u{i}", [128, D], ring0 + i * 8 * K) for i in range(NU)]
    v_slot = [place(f"s_v{i}", [128, D], ring0 + (NU + i) * 8 * K) for i in range(NV)]
    assert ring0 + (NU + NV) * 8 * K <= S
    P0 = S + 66 * K
    diag = [place(f"s_diag{i}", [128, 128], P0 + i * 512) for i in range(NDIAG)]
    P0 += NDIAG * 512

    def small(name, n, dt=f32):
        nonlocal P0
        t = place(name, [128, n], P0, dt)
        P0 += (4 * n + 63) // 64 * 64
        return t

    sc = small("s_sc", 2 * NKEYS)
    sc_rest = small("s_sc_rest", NKEYS)
    val = small("s_val", 2 * TOPK)
    ind = small("s_ind", 2 * TOPK, u32)
    indf = small("s_indf", 2 * TOPK)
    cand = small("s_cand", TOPK * TOPK)
    cand_rest = small("s_cand_rest", TOPK * TOPK)
    top = small("s_top", TOPK)
    pos = small("s_pos", TOPK, u32)
    pos1 = small("s_pos1", TOPK, u32)
    posf = small("s_posf", 2 * TOPK)
    pick = small("s_pick", TOPK * TOPK)
    chosen = small("s_chosen", 2 * TOPK)
    expert_f = small("s_expert_f", TOPK)
    expert = [small(f"s_expert{i}", TOPK, u32) for i in range(2)]
    gate = [small(f"s_pgate{i}", TOPK) for i in range(2)]
    gsum = small("s_gsum", 4)
    iota_i = small("s_iota_i", TOPK, mybir.dt.int32)
    iota_f = small("s_iota_f", TOPK)
    adot = [small(f"s_adot{i}", TOPK) for i in range(2)]
    gelu = [small(f"s_gelu{i}", TOPK) for i in range(2)]
    hid = [small(f"s_hid{i}", TOPK) for i in range(2)]
    assert P0 <= S + 78 * K, P0 - S
    zeros = place("s_zeros", [128, 128], S + 65 * K)
    out_row = place("s_out_row", [128, TT, D], S + 33 * K)

    with ExitStack() as ctx:
        bank = [ctx.enter_context(nc.psum_tensor(f"bank{b}", [128, 512], f32)) for b in range(8)]

        def sem(name):
            return ctx.enter_context(nc.semaphore(name))

        raw_loaded = [sem(f"raw_loaded{i}") for i in range(4)]
        hi_half = sem("hi_half")
        hi_ready = sem("hi_ready")
        split_ready = sem("split_ready")
        conv_split = sem("conv_split")
        panel_used = sem("panel_used")
        bank_full = [sem(f"bank_full{b}") for b in range(8)]
        bank_empty = [sem(f"bank_empty{b}") for b in range(8)]
        pool_passed, dve_passed = sem("pool_passed"), sem("dve_passed")
        dve_step = sem("dve_step")
        pool_step = sem("pool_step")
        x_loaded, meta_loaded, cols_loaded = sem("x_loaded"), sem("meta_loaded"), sem("cols_loaded")
        rows_loaded, small_loaded, late_loaded = sem("rows_loaded"), sem("small_loaded"), sem("late_loaded")
        const_ready, stat_clear = sem("const_ready"), sem("stat_clear")
        evac_hi = sem("evac_hi")
        ssq_ready = sem("ssq_ready")
        ms_ready = sem("ms_ready")
        root_ready = sem("root_ready")
        rstd_ready = sem("rstd_ready")
        xs_ready = sem("xs_ready")
        res_ready = sem("res_ready")
        conv_ready = sem("conv_ready")
        dev_ready = sem("dev_ready")
        dev_sq_ready = sem("dev_sq_ready")
        ln_ready = sem("ln_ready")
        silu_ready, silu_hi = sem("silu_ready"), sem("silu_hi")
        act_ready = sem("act_ready")
        hhi_ready, hlo_ready = sem("hhi_ready"), sem("hlo_ready")
        wfhi_ready, wflo_ready = sem("wfhi_ready"), sem("wflo_ready")
        z_step, z_ln, logf_ready = sem("z_step"), sem("z_ln"), sem("logf_ready")
        qsq_ready, qkn_ready = sem("qsq_ready"), sem("qkn_ready")
        lfb_ready = sem("lfb_ready")
        negmax_ready, exp_ready, prob_ready = sem("negmax_ready"), sem("exp_ready"), sem("prob_ready")
        mixed_ready, part_ready = sem("mixed_ready"), sem("part_ready")
        merged_hi, xn_ready = sem("merged_hi"), sem("xn_ready")
        zeros_ready, iota_ready = sem("zeros_ready"), sem("iota_ready")
        expert_ready = sem("expert_ready")
        gate_max, gate_exp = sem("gate_max"), sem("gate_exp")
        u_loaded = [sem(f"u_loaded{i}") for i in range(NU)]
        v_loaded = [sem(f"v_loaded{i}") for i in range(NV)]
        dot_ready, gelu_ready, hid_ready = sem("dot_ready"), sem("gelu_ready"), sem("hid_ready")
        diag_ready, v_used = sem("diag_ready"), sem("v_used")
        acc_done, out_ready, stored = sem("acc_done"), sem("out_ready"), sem("stored")

        block = ctx.enter_context(nc.Block())

        @block.sync
        def _(sp):
            sp.dma_start(xres[:, :, :], x.rearrange("(t p) d -> p t d", p=128)).then_inc(x_loaded, 16)
            sp.dma_start(meta_sb[:, :], meta).then_inc(meta_loaded, 16)
            sp.dma_start(cols[:, :], columns).then_inc(cols_loaded, 16)
            for s in range(4):
                sp.dma_start(raw[s][:, :], stream[s]).then_inc(raw_loaded[s], 16)
            panels = stream.rearrange("(q s) p n -> q s p n", s=4)
            with sp.Fori(1, NPANELS // 4) as q:
                for s in range(4):
                    sp.wait_ge(panel_used, q * 4 + (s - 4 + 1 + 1))
                    sp.dma_start(raw[s][:, :], panels[bass.ds(q, 1), s].rearrange("a p n -> (a p) n"))\
                        .then_inc(raw_loaded[s], 16)
            for t in range(TT):
                sp.wait_ge(out_ready, t + 1)
                sp.dma_start(out[t * 128:(t + 1) * 128, :], out_row[:, t, :]).then_inc(stored, 16)
            sp.wait_ge(stored, 16 * TT)

        @block.gpsimd
        def _(pool):
            n = Counts()
            pool.memset(ident[:, :], 0.0).then_inc(pool_step, 1)
            pool.memset(ones[:, :], 1.0).then_inc(pool_step, 1)
            pool.memset(tri_ones[:, :], 1.0).then_inc(pool_step, 1)
            pool.memset(causal[:, :], 0.0).then_inc(pool_step, 1)
            pool.iota(inv_count_i[:, :], pattern=[[1, 16]], base=1, channel_multiplier=0).then_inc(pool_step, 1)
            pool.wait_ge(pool_step, 5)
            pool.affine_select(out=ident[:, :], in_=ident[:, :], compare_op=ALU.not_equal, fill=1.0,
                               base=0, pattern=[[-1, 128]], channel_multiplier=1).then_inc(const_ready, 1)
            pool.affine_select(out=tri_ones[:, :], in_=tri_ones[:, :], compare_op=ALU.is_ge, fill=0.0,
                               base=0, pattern=[[1, 256]], channel_multiplier=-1).then_inc(const_ready, 1)
            pool.affine_select(out=causal[:, :], in_=causal[:, :], compare_op=ALU.is_ge, fill=MASKED,
                               base=0, pattern=[[-1, 128]], channel_multiplier=1).then_inc(const_ready, 1)
            for row, src in ((bout_row, b_out), (gmix_row, g_mix_post), (gffn_row, g_ffn_post)):
                pool.dma_start(row[:, :], src.partition_broadcast(128)).then_inc(rows_loaded, 16)
            pool.dma_start(wf_raw[:, :, :], w_forget).then_inc(small_loaded, 16)
            pool.dma_start(fb[:, :], forget_bias.partition_broadcast(128)).then_inc(small_loaded, 16)
            pool.dma_start(group_sb[:, :, :, :], group_w).then_inc(small_loaded, 16)
            with n.rounds(pool, "norm0"):
                pass
            with n.rounds(pool, "w_in", 4):
                for c in range(8):
                    s = c % 4
                    for ready, key, half in ((hi_half, "hi_half", slice(0, 1024)), (hi_ready, "hi", slice(1024, 2048))):
                        pool.wait_ge(ready, n.after(key, c if key == "hi" else c + 1))
                        ins = pool.tensor_tensor(w_lo[s % 2][:, half], raw[s][:, half], w_hi[s % 2][:, half].bitcast(f32),
                                                 ALU.subtract)
                    ins.then_inc(conv_split, 1)
            pool.wait_ge(act_ready, 4 + 4)
            pool.dma_start(g2_row[:, :], g_norm2.partition_broadcast(128)).then_inc(late_loaded, 16)
            pool.dma_start(keys_sb[:, :, :], keys).then_inc(late_loaded, 16)
            pool.iota(iota_i[:, :], pattern=[[1, TOPK]], base=0, channel_multiplier=0).then_inc(iota_ready, 1)
            pool.memset(zeros[:, :], 0.0).then_inc(zeros_ready, 1)

            with n.rounds(pool, "route"):
                pass
            pool.wait_ge(panel_used, NPANELS + 1)

            def gathers():
                for k in range(2 * TOPK + LEAD):
                    if k < 2 * TOPK:
                        e, s = divmod(k, TOPK)
                        if s == 0:
                            wait_apart(pool, expert_ready, n.after("expert", e), pool_passed)
                        index = bass.IndirectOffsetOnAxis(ap=expert[e][:, s:s + 1], axis=0)
                        wait_apart(pool, dot_ready, n.after("dot", k + 1 - NU), pool_passed)
                        pool.indirect_dma_start(u_slot[s % NU][:, :], None, expert_u, index)\
                            .then_inc(u_loaded[s % NU], 16)
                    if k >= LEAD:
                        e, s = divmod(k - LEAD, TOPK)
                        index = bass.IndirectOffsetOnAxis(ap=expert[e][:, s:s + 1], axis=0)
                        wait_apart(pool, v_used, n.after("v_used", k - LEAD + 1 - NV), pool_passed)
                        pool.indirect_dma_start(v_slot[s % NV][:, :], None, expert_v, index)\
                            .then_inc(v_loaded[s % NV], 16)

            with n.rounds(pool, "pair"):
                gathers()
            with n.rounds(pool, "pair", TT * PH // 2 - 1):
                gathers()

        @block.scalar
        def _(act):
            n = Counts()

            def col(name, k):
                return cols[:, COL[name] + k:COL[name] + k + 1]

            def split_hi(c, halves=False):
                s = (c + 1) % 4
                act.wait_ge(raw_loaded[s], n.after("quad", (c + 1) // 4 + 1) * 16)
                act.wait_ge(panel_used, n.after("used", c))
                if halves:
                    act.activation(w_hi[s % 2][:, 0:1024], raw[s][:, 0:1024], ACT.Copy).then_inc(hi_half, 1)
                    act.activation(w_hi[s % 2][:, 1024:], raw[s][:, 1024:], ACT.Copy).then_inc(hi_ready, 1)
                    return
                act.activation(w_hi[s % 2][:, :], raw[s][:, :], ACT.Copy).then_inc(hi_ready, 1)

            def sums_of_squares(src, junk, ready=None):
                for t in range(TT):
                    if ready:
                        act.wait_ge(ready[0], n.after(ready[1], t + 1))
                    ins = act.activation(junk[:, t, :], src[:, t, :], ACT.Square, accum_out=stat[:, t:t + 1])
                ins.then_inc(ssq_ready, 1)

            def root(k, width=TT):
                act.wait_ge(ms_ready, n.after("ms", k))
                act.activation(stat[:, 4:4 + width], stat[:, 4:4 + width], ACT.Sqrt).then_inc(root_ready, 1)

            def transposed_hi(gain, offset):
                for t in range(TT):
                    for b in range(4):
                        act.wait_ge(bank_full[4 * t + b], n.after(f"full{4 * t + b}", 1))
                        for q in range(4):
                            k = 4 * b + q
                            ins = act.activation(a_hi[:, k, offset + t * 128:offset + (t + 1) * 128],
                                                 bank[4 * t + b][:, q * 128:(q + 1) * 128], ACT.Copy,
                                                 scale=col(gain, k) if gain else 1.0)
                        ins.then_inc(evac_hi, 1)

            act.wait_ge(raw_loaded[0], 16)
            act.activation(w_hi[0][:, 0:1024], raw[0][:, 0:1024], ACT.Copy).then_inc(hi_half, 1)
            act.activation(w_hi[0][:, 1024:], raw[0][:, 1024:], ACT.Copy).then_inc(hi_ready, 1)
            with n.rounds(act, "norm0"):
                act.wait_ge(x_loaded, 16)
                act.wait_ge(stat_clear, 1)
                for t in range(TT):
                    act.activation(xs0[:, t, :], xres[:, t, :], ACT.Square, accum_out=stat[:, t:t + 1])
                act.wait_ge(meta_loaded, 16)
                act.activation(sq[0:META, 0:8, :].rearrange("p a t -> p (a t)"), meta_sb[:, :], ACT.Square,
                               accum_out=stat[0:META, 2:3]).then_inc(ssq_ready, 1)
                root(1, 3)
                act.wait_ge(rstd_ready, n.after("rstd", 1))
                for t in range(TT):
                    act.activation(xs0[:, t, :], xres[:, t, :], ACT.Copy, scale=stat[:, 4 + t:5 + t])\
                        .then_inc(xs_ready, 1)
                act.activation(meta_sb[:, :], meta_sb[:, :], ACT.Copy, scale=stat[0:META, 6:7]).then_inc(xs_ready, 1)
                act.wait_ge(cols_loaded, 16)
                transposed_hi("g_mix", META)
                act.wait_ge(panel_used, n.after("used", 1))
                for k in range(KT):
                    ins = act.activation(a_hi[:, k, 0:META], bank[0][:, k * META:(k + 1) * META], ACT.Copy,
                                         scale=col("g_mix", k))
                ins.then_inc(evac_hi, 1)

            with n.rounds(act, "w_in", 4) as i:
                for c in range(8):
                    split_hi(c, halves=True)
                    if c % 4 < 3:
                        continue
                    j = c // 4 * 2
                    act.wait_ge(bank_empty[j + 1], n.after(f"empty{j + 1}", 0))
                    act.wait_ge(bank_full[4 + j], n.after(f"full{4 + j}", 1))
                    act.activation(sig[:, j, :], bank[4 + j][:, 0:L], ACT.Sigmoid,
                                   bias=cols[:, bass.ds(i * 4 + (COL["b_g"] + j), 1)]).then_inc(bank_empty[4 + j], 1)
                    j += 1
                    act.wait_ge(panel_used, n.after("used", c + 1))
                    act.activation(sig[:, j, :], bank[4 + j][:, 0:L], ACT.Sigmoid,
                                   bias=cols[:, bass.ds(i * 4 + (COL["b_g"] + j), 1)]).then_inc(bank_empty[4 + j], 1)

            with n.rounds(act, "ln"):
                for g in range(4):
                    act.wait_ge(dev_ready, n.after("dev", g + 1))
                    act.activation(sq[:, 4 * g:4 * g + 4, :], cvo[:, 4 * g:4 * g + 4, :], ACT.Square)\
                        .then_inc(dev_sq_ready, 1)
                act.wait_ge(bank_empty[1], n.after("empty1", 1))
                act.activation(rstd[:, :], rstd[:, :], ACT.Sqrt).then_inc(root_ready, 1)
                for g in range(4):
                    act.wait_ge(ln_ready, n.after("ln", g + 1))
                    for k in range(4 * g, 4 * g + 4):
                        ins = act.activation(sq[:, k, :], cvo[:, k, :], ACT.Silu, scale=col("ln_g", k), bias=col("ln_b", k))
                    ins.then_inc(silu_ready, 1)
                    act.wait_ge(silu_ready, n.after("silu", g + 1))
                    act.activation(a_hi[:, 4 * g:4 * g + 4, 0:T], sq[:, 4 * g:4 * g + 4, :], ACT.Copy).then_inc(silu_hi, 1)

            with n.rounds(act, "w_out", 4):
                for c in range(4):
                    split_hi(c)

            def post(last_bank, gain):
                act.wait_ge(bank_empty[last_bank], n.after(f"empty{last_bank}", 0))
                sums_of_squares(yrow, xs)
                root(1)
                sums_of_squares(xres, xs, (res_ready, "res"))
                root(2)
                act.wait_ge(rstd_ready, n.after("rstd", 1))
                for t in range(TT):
                    act.activation(xs[:, t, :], xres[:, t, :], ACT.Copy, scale=stat[:, 4 + t:5 + t])\
                        .then_inc(xs_ready, 1)
                transposed_hi(gain, 0)

            with n.rounds(act, "post"):
                post(1, "g_ffn")

            with n.rounds(act, "ffn", FF // 512):
                for blk in range(2):
                    c0 = 4 * blk
                    split_hi(c0)
                    split_hi(c0 + 1)
                    for j in range(2):
                        b = 2 + j if blk else 6 + j
                        act.wait_ge(bank_empty[b], n.after(f"empty{b}", blk))
                        if j == 0:
                            act.wait_ge(bank_full[c0], n.after(f"full{c0}", 1))
                        else:
                            act.wait_ge(panel_used, n.after("used", c0 + 2))
                        act.activation(sg[:, j, :], bank[c0 + j][:, 0:T], ACT.Silu).then_inc(bank_empty[c0 + j], 1)
                    split_hi(c0 + 2)
                    split_hi(c0 + 3)
                    for j in range(2):
                        b = c0 + 2 + j
                        act.wait_ge(bank_empty[b], n.after(f"empty{b}", 1))
                        act.activation(h_hi[:, 2 * blk + j, :], hf[:, 2 * blk + j, :], ACT.Copy).then_inc(hhi_ready, 1)
                for c in range(8, 12):
                    split_hi(c)

            with n.rounds(act, "post"):
                post(7, "g_norm1")

            def copies_out(i, dst, offset):
                for j in range(4):
                    if j < 3:
                        act.wait_ge(bank_full[j], n.after(f"full{j}", 1))
                    else:
                        act.wait_ge(panel_used, n.after("used", 4))
                    act.activation(dst[:, bass.ds(i * 4 + j, 1), offset:offset + T].rearrange("p a t -> p (a t)"),
                                   bank[j][:, 0:T], ACT.Copy).then_inc(bank_empty[j], 1)

            with n.rounds(act, "qk", 4) as i:
                for c in range(4):
                    split_hi(c)
                copies_out(i, qk, 0)
            with n.rounds(act, "forget"):
                act.wait_ge(small_loaded, 48)
                act.activation(wf_hi[:, :, :], wf_raw[:, :, :], ACT.Copy).then_inc(wfhi_ready, 1)
                act.wait_ge(bank_empty[7], n.after("empty7", 1))
                act.activation(fg[:, 1, :], fg[:, 0, :], ACT.Abs).then_inc(z_step, 1)
                act.wait_ge(z_step, n.after("z_step", 1))
                act.activation(fg[:, 1, :], fg[:, 1, :], ACT.Exp, scale=-1.0).then_inc(z_step, 1)
                act.wait_ge(z_step, n.after("z_step", 2))
                act.activation(fg[:, 2, :], fg[:, 1, :], ACT.Ln, bias=1.0).then_inc(z_ln, 1)
            for g in range(4):
                with n.rounds(act, "qknorm"):
                    act.wait_ge(bank_empty[3], n.after("empty3", 0))
                    wait(act, qkn_ready, n.after("qkn", 0))
                    act.activation(qsq[:, :, :], qk[:, 4 * g:4 * g + 4, :], ACT.Square).then_inc(qsq_ready, 1)
                    act.wait_ge(bank_empty[5], n.after("empty5", 1))
                    act.activation(qrs[:, :, :], qrs[:, :, :], ACT.Sqrt).then_inc(root_ready, 1)
            with n.rounds(act, "v", 2) as i:
                for c in range(4):
                    split_hi(c)
                for t in range(TT):
                    if t == 0:
                        act.wait_ge(bank_full[4], n.after("full4", 1))
                    else:
                        act.wait_ge(panel_used, n.after("used", 4))
                    act.activation(vrow[:, t, bass.ds(i * 512, 512)], bank[4 + t][:, :], ACT.Copy)\
                        .then_inc(bank_empty[4 + t], 1)
            with n.rounds(act, "cum"):
                pass
            for r in range(HEADS // 2):
                with n.rounds(act, "score"):
                    pass
            with n.rounds(act, "softmax"):
                act.wait_ge(negmax_ready, n.after("negmax", 1))
                for h in range(HEADS):
                    act.activation(lg0[:, h, :], lg0[:, h, :], ACT.Exp, bias=negmax[:, h:h + 1],
                                   accum_out=den[:, h:h + 1])
                    ins = act.activation(lg1[:, h, :], lg1[:, h, :], ACT.Exp, bias=negmax[:, HEADS + h:HEADS + h + 1],
                                         accum_out=den[:, HEADS + h:HEADS + h + 1])
                ins.then_inc(exp_ready, 1)
            with n.rounds(act, "pin", 2) as i:
                for c in range(4):
                    split_hi(c)
                copies_out(i, pin, PADP)
            with n.rounds(act, "pool"):
                for j in range(8):
                    b = 4 + j % 4
                    act.wait_ge(bank_full[b], n.after(f"full{b}", j // 4 + 1))
                    act.activation(po_hi[:, j, :], bank[b][:, 0:T], ACT.Copy, scale=col("pool_scale", j)).then_inc(evac_hi, 1)
            for r in range(HEADS // 2):
                with n.rounds(act, "heads"):
                    for e in range(2):
                        act.wait_ge(bank_full[e], n.after(f"full{e}", 1))
                        act.activation(pts[:, e, :], bank[e][:, 0:384], ACT.Copy).then_inc(bank_empty[e], 1)
                    for e in range(2):
                        act.wait_ge(bank_full[2 + e], n.after(f"full{2 + e}", 1))
                        act.activation(at_hi[:, 2 * r + e, :], bank[2 + e][:, 0:T], ACT.Copy).then_inc(evac_hi, 1)
            with n.rounds(act, "merge", 4):
                for half, gates in enumerate((gate0, gate1)):
                    for c in range(4):
                        split_hi(4 * half + c)
                    for j in range(4):
                        b = 4 * half + j
                        if j < 3:
                            act.wait_ge(bank_full[b], n.after(f"full{b}", 1))
                        else:
                            act.wait_ge(panel_used, n.after("used", 4 * half + 4))
                        act.activation(gates[:, j, :], bank[b][:, 0:T], ACT.Sigmoid).then_inc(bank_empty[b], 1)
                for c in range(8, 12):
                    split_hi(c)
            with n.rounds(act, "merged"):
                act.wait_ge(part_ready, n.after("part", 0))
                for g in range(4):
                    act.activation(a_hi[:, 4 * g:4 * g + 4, 0:T], merged[:, 4 * g:4 * g + 4, :], ACT.Copy).then_inc(merged_hi, 1)
            with n.rounds(act, "w_out_2", 4):
                for c in range(4):
                    split_hi(c)
            with n.rounds(act, "post_2"):
                act.wait_ge(bank_empty[1], n.after("empty1", 0))
                sums_of_squares(xres, xs)
                root(1)
                act.wait_ge(rstd_ready, n.after("rstd", 1))
                for t in range(TT):
                    act.activation(xs[:, t, :], xres[:, t, :], ACT.Copy, scale=stat[:, 4 + t:5 + t]).then_inc(xs_ready, 1)
                transposed_hi(None, 0)
            with n.rounds(act, "query"):
                for c in range(4):
                    split_hi(c)
                copies_out(0, qp, 0)
            for r in (1, 2):
                with n.rounds(act, "query"):
                    for c in range(4):
                        split_hi(c)
                        if r == 2 and c == 0:
                            act.wait_ge(bank_full[4], n.after("full4", 0))
                            act.activation(score[:, 0:2, :].rearrange("p h k -> p (h k)"), bank[4][:, :], ACT.Copy)\
                                .then_inc(bank_empty[4], 1)
                    copies_out(r, qp, 0)
                if r == 1:
                    with n.rounds(act, "keys_0"):
                        pass
            with n.rounds(act, "query"):
                for c in range(3):
                    split_hi(c)
                copies_out(3, qp, 0)
            with n.rounds(act, "keys"):
                for t in range(TT):
                    for b in range(4):
                        if t == b == 0:
                            continue
                        act.wait_ge(bank_full[4 * t + b], n.after(f"full{4 * t + b}", 1))
                        act.activation(score[:, t * PH + 2 * b:t * PH + 2 * b + 2, :].rearrange("p h k -> p (h k)"),
                                       bank[4 * t + b][:, :], ACT.Copy).then_inc(bank_empty[4 * t + b], 1)

            def gate_exps(parity, k):
                act.wait_ge(gate_max, n.after("gate_max", k))
                act.activation(gate[parity][:, :], top[:, :], ACT.Exp, bias=gsum[:, 0:1], accum_out=gsum[:, 1:2])\
                    .then_inc(gate_exp, 1)

            def heads(more=True):
                for e in range(2):
                    for q in range(TOPK // BATCH):
                        if q == 2 and (more or e == 0):
                            gate_exps(1 - e, e + 1)
                        part = slice(q * BATCH, (q + 1) * BATCH)
                        act.wait_ge(dot_ready, n.after("dot", e * TOPK + (q + 1) * BATCH))
                        act.activation(gelu[e][:, part], adot[e][:, part], ACT.Gelu_apprx_tanh).then_inc(gelu_ready, 1)
                        act.wait_ge(hid_ready, n.after("hid", e * TOPK // BATCH + q + 1))
                        for s in range(q * BATCH, (q + 1) * BATCH):
                            wait(act, v_used, n.after("v_used", e * TOPK + s + 1 - NDIAG))
                            act.activation(diag[s % NDIAG][:, :], ident[:, :], ACT.Copy, scale=hid[e][:, s:s + 1])\
                                .then_inc(diag_ready, 1)

            with n.rounds(act, "route"):
                gate_exps(0, 1)
            with n.rounds(act, "pair"):
                heads()
            with n.rounds(act, "pair", TT * PH // 2 - 2):
                heads()
            with n.rounds(act, "pair"):
                heads(more=False)

        @block.vector
        def _(dve):
            n = Counts()

            def col(name, k):
                return cols[:, COL[name] + k:COL[name] + k + 1]

            def step(ins):
                ins.then_inc(dve_step, 1)
                n.base["dve_step"] = n.base.get("dve_step", 0) + 1

            def settled(back=0):
                dve.wait_ge(dve_step, n.base["dve_step"] - back)

            def link(ins):
                step(ins)
                settled()

            def split_lo(c):
                s = (c + 1) % 4
                dve.wait_ge(hi_ready, n.after("hi", c + 1))
                dve.tensor_tensor(w_lo[s % 2][:, :], raw[s][:, :], w_hi[s % 2][:, :].bitcast(f32), ALU.subtract)\
                    .then_inc(split_ready, 1)

            def mean_square(k, width=TT):
                dve.wait_ge(ssq_ready, n.after("ssq", k))
                dve.tensor_scalar(stat[:, 4:4 + width], stat[:, 0:width], 1.0 / D, RMS_EPS, ALU.mult, ALU.add)\
                    .then_inc(ms_ready, 1)

            def inverse(k, width=TT):
                dve.wait_ge(root_ready, n.after("root", k))
                dve.reciprocal(stat[:, 4:4 + width], stat[:, 4:4 + width]).then_inc(rstd_ready, 1)

            def transposed_lo(gain, offset):
                for t in range(TT):
                    for b in range(4):
                        dve.wait_ge(evac_hi, n.after("evac", 4 * t + b + 1))
                        for q in range(4):
                            k = 4 * b + q
                            where = slice(offset + t * 128, offset + (t + 1) * 128)
                            ins = dve.scalar_tensor_tensor(
                                a_lo[:, k, where], bank[4 * t + b][:, q * 128:(q + 1) * 128],
                                col(gain, k) if gain else 1.0, a_hi[:, k, where].bitcast(f32), ALU.mult, ALU.subtract)
                        ins.then_inc(bank_empty[4 * t + b], 1)

            dve.memset(stat[:, :], 1.0).then_inc(stat_clear, 1)
            with n.rounds(dve, "norm0"):
                mean_square(1, 3)
                inverse(1, 3)
                dve.wait_ge(cols_loaded, 16)
                transposed_lo("g_mix", META)
                dve.wait_ge(evac_hi, n.after("evac", 9))
                for k in range(KT):
                    ins = dve.scalar_tensor_tensor(a_lo[:, k, 0:META], bank[0][:, k * META:(k + 1) * META], col("g_mix", k),
                                                   a_hi[:, k, 0:META].bitcast(f32), ALU.mult, ALU.subtract)
                ins.then_inc(bank_empty[0], 1)
                link(dve.memset(cvg[:, :, 0:TAPS - 1], 0.0))

            def glu(i, half):
                for j in (2 * half, 2 * half + 1):
                    if j % 2 == 0:
                        dve.wait_ge(bank_full[j], n.after(f"full{j}", 1))
                    else:
                        dve.wait_ge(panel_used, n.after("used", 4 * half + 2))
                    dve.wait_ge(bank_empty[4 + j], n.after(f"empty{4 + j}", 1))
                    dve.scalar_tensor_tensor(cvg[:, j, TAPS - 1:], bank[j][:, 0:L],
                                             cols[:, bass.ds(i * 4 + (COL["b_a"] + j), 1)], sig[:, j, :],
                                             ALU.add, ALU.mult).then_inc(bank_empty[j], 1)

            def conv(i, half):
                for tap in range(TAPS):
                    for j in (2 * half, 2 * half + 1):
                        w = cols[:, bass.ds(i * (4 * TAPS) + (COL["w_dw"] + j * TAPS + tap), 1)]
                        u = cvg[:, j, META + tap:META + tap + T]
                        if tap == 0:
                            dve.wait_ge(bank_empty[j], n.after(f"empty{j}", 1))
                            b = cols[:, bass.ds(i * 4 + (COL["b_dw"] + j), 1)]
                            step(dve.tensor_scalar(cacc[:, j, :], u, w, b, ALU.mult, ALU.add))
                            continue
                        settled(1)
                        if tap < TAPS - 1:
                            step(dve.scalar_tensor_tensor(cacc[:, j, :], u, w, cacc[:, j, :], ALU.mult, ALU.add))
                        else:
                            step(dve.scalar_tensor_tensor(
                                cvo[:, bass.ds(i * 4 + j, 1), :].rearrange("p a t -> p (a t)"), u, w, cacc[:, j, :],
                                ALU.mult, ALU.add))
                settled()

            with n.rounds(dve, "w_in", 4, dve_step=4 * TAPS) as i:
                for half in range(2):
                    glu(i, half)
                    conv(i, half)
            dve.memset(stat[:, 7:8], 1.0).then_inc(conv_ready, 1)
            split_lo(-1)

            with n.rounds(dve, "ln"):
                dve.wait_ge(bank_full[0], n.after("full0", 1))
                dve.tensor_scalar(mean[:, :], bank[0][:, 0:T], 1.0 / D, None, ALU.mult).then_inc(bank_empty[0], 1)
                dve.wait_ge(bank_empty[0], n.after("empty0", 1))
                for g in range(4):
                    four = cvo[:, 4 * g:4 * g + 4, :]
                    dve.tensor_tensor(four, four, mean[:, :].unsqueeze(1).to_broadcast([128, 4, T]), ALU.subtract)\
                        .then_inc(dev_ready, 1)
                dve.wait_ge(bank_full[1], n.after("full1", 1))
                dve.tensor_scalar(rstd[:, :], bank[1][:, 0:T], 1.0 / D, LN_EPS, ALU.mult, ALU.add).then_inc(bank_empty[1], 1)
                dve.wait_ge(root_ready, n.after("root", 1))
                link(dve.reciprocal(rstd[:, :], rstd[:, :]))
                for g in range(4):
                    four = cvo[:, 4 * g:4 * g + 4, :]
                    dve.tensor_tensor(four, four, rstd[:, :].unsqueeze(1).to_broadcast([128, 4, T]), ALU.mult)\
                        .then_inc(ln_ready, 1)
                for g in range(4):
                    dve.wait_ge(silu_hi, n.after("silu_hi", g + 1))
                    dve.tensor_tensor(a_lo[:, 4 * g:4 * g + 4, 0:T], sq[:, 4 * g:4 * g + 4, :],
                                      a_hi[:, 4 * g:4 * g + 4, 0:T].bitcast(f32), ALU.subtract).then_inc(act_ready, 1)

            dve.wait_ge(rows_loaded, 48)
            with n.rounds(dve, "w_out", 4) as i:
                for c in range(4):
                    split_lo(c)
                for t in range(TT):
                    if t == 0:
                        dve.wait_ge(bank_full[0], n.after("full0", 1))
                    else:
                        dve.wait_ge(panel_used, n.after("used", 4))
                    dve.tensor_tensor(yrow[:, t, bass.ds(i * 512, 512)], bank[t][:, :], bout_row[:, bass.ds(i * 512, 512)],
                                      ALU.add).then_inc(bank_empty[t], 1)

            def post(row, gain):
                mean_square(1)
                dve.wait_ge(root_ready, n.after("root", 1))
                link(dve.reciprocal(stat[:, 4:4 + TT], stat[:, 4:4 + TT]))
                for t in range(TT):
                    step(dve.scalar_tensor_tensor(yrow[:, t, :], yrow[:, t, :], stat[:, 4 + t:5 + t], row[:, :],
                                                  ALU.mult, ALU.mult))
                for t in range(TT):
                    settled(TT - 1 - t)
                    dve.tensor_tensor(xres[:, t, :], xres[:, t, :], yrow[:, t, :], ALU.add).then_inc(res_ready, 1)
                mean_square(2)
                inverse(2)
                transposed_lo(gain, 0)

            with n.rounds(dve, "post"):
                post(gmix_row, "g_ffn")
            for t in range(TT):
                link(dve.memset(yrow[:, t, :], 0.0))

            with n.rounds(dve, "ffn", FF // 512):
                for blk in range(2):
                    c0 = 4 * blk
                    for c in range(4):
                        split_lo(c0 + c)
                    for j in range(2):
                        f, b = 2 * blk + j, c0 + 2 + j
                        dve.wait_ge(bank_empty[c0 + j], n.after(f"empty{c0 + j}", 1))
                        if j == 0:
                            dve.wait_ge(bank_full[b], n.after(f"full{b}", 1))
                        else:
                            dve.wait_ge(panel_used, n.after("used", c0 + 4))
                        dve.tensor_tensor(hf[:, f, :], sg[:, j, :], bank[b][:, 0:T], ALU.mult).then_inc(bank_empty[b], 1)
                        dve.wait_ge(hhi_ready, n.after("hhi", f + 1))
                        dve.tensor_tensor(h_lo[:, f, :], hf[:, f, :], h_hi[:, f, :].bitcast(f32), ALU.subtract).then_inc(hlo_ready, 1)
                for c in range(8, 12):
                    split_lo(c)
                for b in range(8):
                    t, c = (1, b) if b < 4 else (0, b - 4)
                    if b == 7:
                        dve.wait_ge(panel_used, n.after("used", 12))
                    else:
                        dve.wait_ge(bank_full[b], n.after(f"full{b}", 1 if b % 2 else 2))
                    dst = yrow[:, t, c * 512:(c + 1) * 512]
                    dve.tensor_tensor(dst, dst, bank[b][:, :], ALU.add).then_inc(bank_empty[b], 1)

            with n.rounds(dve, "post"):
                post(gffn_row, "g_norm1")

            with n.rounds(dve, "qk", 4):
                for c in range(4):
                    split_lo(c)
            with n.rounds(dve, "forget"):
                dve.wait_ge(wfhi_ready, n.after("wf_hi", 1))
                dve.tensor_tensor(wf_lo[:, :, :], wf_raw[:, :, :], wf_hi[:, :, :].bitcast(f32), ALU.subtract).then_inc(wflo_ready, 1)
                for t in range(TT):
                    dve.wait_ge(bank_full[6 + t], n.after(f"full{6 + t}", 1))
                    dve.tensor_tensor(fg[:, 0, t * HEADS:(t + 1) * HEADS], bank[6 + t][:, 0:HEADS], fb[:, :], ALU.add)\
                        .then_inc(bank_empty[6 + t], 1)
                dve.wait_ge(z_ln, n.after("z_ln", 1))
                link(dve.tensor_scalar(fg[:, 3, :], fg[:, 1, :], 1.0, None, ALU.add))
                step(dve.reciprocal(fg[:, 4, :], fg[:, 3, :]))
                link(dve.tensor_scalar(fg[:, 5, :], fg[:, 3, :], -1.0, None, ALU.add))
                link(dve.tensor_tensor(fg[:, 5, :], fg[:, 1, :], fg[:, 5, :], ALU.subtract))
                link(dve.tensor_tensor(fg[:, 5, :], fg[:, 5, :], fg[:, 4, :], ALU.mult))
                link(dve.tensor_tensor(fg[:, 2, :], fg[:, 2, :], fg[:, 5, :], ALU.add))
                link(dve.tensor_scalar(fg[:, 3, :], fg[:, 0, :], 0.0, None, ALU.min))
                dve.tensor_tensor(fg[:, 5, :], fg[:, 3, :], fg[:, 2, :], ALU.subtract).then_inc(logf_ready, 1)
            for g in range(4):
                with n.rounds(dve, "qknorm"):
                    wait(dve, qkn_ready, n.after("qkn", 0))
                    for p in range(2):
                        dve.wait_ge(bank_full[4 + p], n.after(f"full{4 + p}", 1))
                        dve.tensor_scalar(qrs[:, 2 * p:2 * p + 2, :].rearrange("p a t -> p (a t)"), bank[4 + p][:, :],
                                          1.0 / HD, RMS_EPS, ALU.mult, ALU.add).then_inc(bank_empty[4 + p], 1)
                    dve.wait_ge(root_ready, n.after("root", 1))
                    link(dve.reciprocal(qrs[:, :, :], qrs[:, :, :]))
                    four = qk[:, 4 * g:4 * g + 4, :]
                    link(dve.tensor_tensor(four, four, qrs[:, :, :], ALU.mult))
                    dve.tensor_scalar(four, four, col("g_q" if g < 2 else "g_k", 0), None, ALU.mult).then_inc(qkn_ready, 1)
            with n.rounds(dve, "v", 2):
                for c in range(4):
                    split_lo(c)
            with n.rounds(dve, "cum"):
                dve.wait_ge(const_ready, 3)
                for t in range(TT):
                    for h in range(HEADS):
                        ins = dve.tensor_scalar(lfb[:, t, h, :], ones[:, :], fg[:, 5, t * HEADS + h:t * HEADS + h + 1], None, ALU.mult)
                ins.then_inc(lfb_ready, 1)
                dve.wait_ge(bank_full[6], n.after("full6", 1))
                dve.tensor_copy(cq[:, :], bank[6][:, 0:TT * HEADS]).then_inc(bank_empty[6], 1)
                dve.wait_ge(bank_empty[6], n.after("empty6", 1))
            for r in range(HEADS // 2):
                with n.rounds(dve, "score"):
                    for e in range(2):
                        h = 2 * r + e
                        dve.wait_ge(bank_full[e], n.after(f"full{e}", 1))
                        dve.wait_ge(bank_empty[2 + e], n.after(f"empty{2 + e}", 0))
                        dve.tensor_scalar(bias_t[:, e, 0:128], bank[e][:, 0:128], -1.0, cq[:, h:h + 1], ALU.mult, ALU.add)
                        dve.tensor_scalar(bias_t[:, e, 128:384], bank[e][:, 0:256], -1.0, cq[:, HEADS + h:HEADS + h + 1],
                                          ALU.mult, ALU.add).then_inc(bank_empty[e], 1)
                        dve.wait_ge(bank_empty[e], n.after(f"empty{e}", 1))
                        dve.wait_ge(bank_full[2 + e], n.after(f"full{2 + e}", 1))
                        dve.scalar_tensor_tensor(lg0[:, h, :], bank[2 + e][:, 0:128], HD ** -0.5, bias_t[:, e, 0:128],
                                                 ALU.mult, ALU.add)
                        dve.scalar_tensor_tensor(lg1[:, h, :], bank[2 + e][:, 128:384], HD ** -0.5, bias_t[:, e, 128:384],
                                                 ALU.mult, ALU.add).then_inc(bank_empty[2 + e], 1)
            with n.rounds(dve, "softmax"):
                dve.wait_ge(bank_empty[3], n.after("empty3", 0))
                mask = causal[:, :].unsqueeze(1).to_broadcast([128, HEADS, 128])
                step(dve.tensor_tensor(lg0[:, :, :], lg0[:, :, :], mask, ALU.add))
                link(dve.tensor_tensor(lg1[:, :, 128:256], lg1[:, :, 128:256], mask, ALU.add))
                step(dve.tensor_reduce(negmax[:, 0:HEADS], lg0[:, :, :], AX.X, ALU.max))
                link(dve.tensor_reduce(negmax[:, HEADS:2 * HEADS], lg1[:, :, :], AX.X, ALU.max))
                dve.tensor_scalar(negmax[:, :], negmax[:, :], -1.0, None, ALU.mult).then_inc(negmax_ready, 1)
                dve.wait_ge(exp_ready, n.after("exp", 1))
                link(dve.reciprocal(den[:, :], den[:, :]))
                dve.tensor_tensor(lg0[:, :, :], lg0[:, :, :], den[:, 0:HEADS].unsqueeze(2).to_broadcast([128, HEADS, 128]),
                                  ALU.mult).then_inc(prob_ready, 1)
                dve.tensor_tensor(lg1[:, :, :], lg1[:, :, :], den[:, HEADS:2 * HEADS].unsqueeze(2).to_broadcast([128, HEADS, 256]),
                                  ALU.mult).then_inc(prob_ready, 1)
            with n.rounds(dve, "pin", 2):
                for c in range(4):
                    split_lo(c)
            link(dve.tensor_copy(inv_count[:, :], inv_count_i[:, :]))
            link(dve.reciprocal(inv_count[:, :], inv_count[:, :]))
            link(dve.memset(pin[:, :, 0:PADP], 0.0))
            with n.rounds(dve, "pool"):
                dve.wait_ge(bank_empty[3], n.after("empty3", 0))
                for g, w in enumerate(POOL_WINDOWS):
                    src, s = pin[:, 2 * g:2 * g + 2, :], 1
                    own = src
                    for k in range(g + 1):
                        dst = (win_a, win_b)[k % 2][:, :, :]
                        low = 2 * s - 1
                        link(dve.tensor_tensor(dst[:, :, low:], src[:, :, low:], src[:, :, low - s:PADP + T - s], ALU.add))
                        src, s = dst, 2 * s
                    early = slice(PADP, PADP + w - 1)
                    late = slice(PADP + w - 1, PADP + T)
                    step(dve.scalar_tensor_tensor(mixed[:, 2 * g:2 * g + 2, w - 1:], src[:, :, late], 1.0 / w, own[:, :, late],
                                                  ALU.mult, ALU.subtract))
                    part = mixed[:, 2 * g:2 * g + 2, 0:w - 1]
                    link(dve.tensor_tensor(part, src[:, :, early], inv_count[:, 0:w - 1].unsqueeze(1).to_broadcast([128, 2, w - 1]),
                                           ALU.mult))
                    dve.tensor_tensor(part, part, own[:, :, early], ALU.subtract).then_inc(mixed_ready, 1)
                for j in range(8):
                    b = 4 + j % 4
                    dve.wait_ge(evac_hi, n.after("evac", j + 1))
                    dve.scalar_tensor_tensor(po_lo[:, j, :], bank[b][:, 0:T], col("pool_scale", j), po_hi[:, j, :].bitcast(f32),
                                             ALU.mult, ALU.subtract).then_inc(bank_empty[b], 1)
            for r in range(HEADS // 2):
                with n.rounds(dve, "heads"):
                    for e in range(2):
                        dve.wait_ge(evac_hi, n.after("evac", e + 1))
                        dve.tensor_tensor(at_lo[:, 2 * r + e, :], bank[2 + e][:, 0:T], at_hi[:, 2 * r + e, :].bitcast(f32),
                                          ALU.subtract).then_inc(bank_empty[2 + e], 1)
            with n.rounds(dve, "merge", 4) as i:
                for c in range(10):
                    split_lo(c)
                for j in range(4):
                    dve.wait_ge(bank_empty[j], n.after(f"empty{j}", 1))
                    if j < 3:
                        dve.wait_ge(bank_full[j], n.after(f"full{j}", 2))
                    else:
                        dve.wait_ge(panel_used, n.after("used", 10))
                    dve.tensor_tensor(part0[:, j, :], gate0[:, j, :], bank[j][:, 0:T], ALU.mult).then_inc(bank_empty[j], 1)
                split_lo(10)
                split_lo(11)
                for j in range(4):
                    dve.wait_ge(bank_empty[4 + j], n.after(f"empty{4 + j}", 1))
                    if j < 3:
                        dve.wait_ge(bank_full[4 + j], n.after(f"full{4 + j}", 2))
                    else:
                        dve.wait_ge(panel_used, n.after("used", 12))
                    dve.tensor_tensor(part1[:, j, :], gate1[:, j, :], bank[4 + j][:, 0:T], ALU.mult).then_inc(bank_empty[4 + j], 1)
                for j in range(4):
                    dve.wait_ge(bank_empty[4 + j], n.after(f"empty{4 + j}", 2))
                    dve.tensor_tensor(merged[:, bass.ds(i * 4 + j, 1), :].rearrange("p a t -> p (a t)"), part0[:, j, :],
                                      part1[:, j, :], ALU.add).then_inc(part_ready, 1)
                dve.wait_ge(part_ready, n.after("part", 4))
            with n.rounds(dve, "merged"):
                for g in range(4):
                    dve.wait_ge(merged_hi, n.after("merged_hi", g + 1))
                    dve.tensor_tensor(a_lo[:, 4 * g:4 * g + 4, 0:T], merged[:, 4 * g:4 * g + 4, :],
                                      a_hi[:, 4 * g:4 * g + 4, 0:T].bitcast(f32), ALU.subtract).then_inc(act_ready, 1)
            with n.rounds(dve, "w_out_2", 4) as i:
                for c in range(4):
                    split_lo(c)
                for t in range(TT):
                    if t == 0:
                        dve.wait_ge(bank_full[0], n.after("full0", 1))
                    else:
                        dve.wait_ge(panel_used, n.after("used", 4))
                    dst = xres[:, t, bass.ds(i * 512, 512)]
                    dve.tensor_tensor(dst, dst, bank[t][:, :], ALU.add).then_inc(bank_empty[t], 1)
            with n.rounds(dve, "post_2"):
                mean_square(1)
                inverse(1)
                dve.wait_ge(late_loaded, 32)
                for t in range(TT):
                    dve.wait_ge(xs_ready, n.after("xs", t + 1))
                    dve.tensor_tensor(xn[:, t, :], xs[:, t, :], g2_row[:, :], ALU.mult).then_inc(xn_ready, 1)
                transposed_lo(None, 0)
            with n.rounds(dve, "query", 2):
                for c in range(4):
                    split_lo(c)
            def apart():
                dve.sem_inc(dve_passed, 1)

            def sixteen(values, indices, src, rest):
                apart()
                link(dve.max(values[:, 0:8], src))
                apart()
                step(dve.max_index(indices[:, 0:8], values[:, 0:8], src))
                link(dve.match_replace(rest, values[:, 0:8], src, LOWEST))
                apart()
                link(dve.max(values[:, 8:16], rest))
                apart()
                link(dve.max_index(indices[:, 8:16], values[:, 8:16], rest))

            square = [128, TOPK, TOPK]

            def best_keys(th, halves):
                if 0 in halves:
                    link(dve.tensor_copy(sc[:, :], score[:, bass.ds(th, 1), :].rearrange("p a k -> p (a k)")))
                for half in halves:
                    sixteen(val[:, half * TOPK:(half + 1) * TOPK], ind[:, half * TOPK:(half + 1) * TOPK],
                            sc[:, half * NKEYS:(half + 1) * NKEYS], sc_rest[:, :])

            def best_pairs():
                step(dve.tensor_copy(indf[:, :], ind[:, :]))
                grid = cand[:, :].rearrange("p (a b) -> p a b", a=TOPK)
                link(dve.tensor_tensor(grid, val[:, 0:TOPK].unsqueeze(2).to_broadcast(square),
                                       val[:, TOPK:].unsqueeze(1).to_broadcast(square), ALU.add))
                sixteen(top[:, :], pos[:, :], cand[:, :], cand_rest[:, :])
                dve.tensor_scalar(gsum[:, 0:1], top[:, 0:1], -1.0, None, ALU.mult).then_inc(gate_max, 1)

            def pairs_experts(parity, free):
                link(dve.tensor_scalar(pos1[:, :], pos[:, :], 4, None, ALU.logical_shift_right))
                step(dve.tensor_copy(posf[:, 0:TOPK], pos1[:, :]))
                link(dve.tensor_scalar(pos[:, :], pos[:, :], TOPK - 1, None, ALU.bitwise_and))
                link(dve.tensor_copy(posf[:, TOPK:], pos[:, :]))
                picks = pick[:, :].rearrange("p (k a) -> p k a", a=TOPK)
                for half in range(2):
                    part = slice(half * TOPK, (half + 1) * TOPK)
                    link(dve.tensor_tensor(picks, iota_f[:, :].unsqueeze(1).to_broadcast(square),
                                           posf[:, part].unsqueeze(2).to_broadcast(square), ALU.is_equal))
                    link(dve.tensor_tensor(picks, picks, indf[:, part].unsqueeze(1).to_broadcast(square), ALU.mult))
                    link(dve.tensor_reduce(chosen[:, part], picks, AX.X, ALU.add))
                link(dve.scalar_tensor_tensor(expert_f[:, :], chosen[:, 0:TOPK], float(NKEYS), chosen[:, TOPK:], ALU.mult, ALU.add))
                wait(dve, v_used, free)
                dve.tensor_copy(expert[parity][:, :], expert_f[:, :]).then_inc(expert_ready, 1)

            def gates_softmax(parity, k):
                dve.wait_ge(gate_exp, n.after("gate_exp", k))
                link(dve.reciprocal(gsum[:, 2:3], gsum[:, 1:2]))
                link(dve.tensor_scalar(gate[parity][:, :], gate[parity][:, :], gsum[:, 2:3], None, ALU.mult))

            def route(th, parity, k, free):
                best_keys(th, (0, 1))
                best_pairs()
                pairs_experts(parity, free)
                gates_softmax(parity, k)

            def heads(th, t, more=True):
                for e in range(2):
                    for q in range(TOPK // BATCH):
                        if q == 2 and (more or e == 0):
                            route(th + (e + 1), 1 - e, e + 1, n.after("v_used", e * TOPK))
                        for s in range(q * BATCH, (q + 1) * BATCH):
                            dve.wait_ge(u_loaded[s % NU], n.after("u_rows", e * 4 + s // NU + 1) * 16)
                            dve.tensor_tensor_reduce(out=u_slot[s % NU][:, :], in0=u_slot[s % NU][:, :], in1=xn[:, t, :],
                                                     scale=1.0, scalar=0.0, op0=ALU.mult, op1=ALU.add,
                                                     accum_out=adot[e][:, s:s + 1]).then_inc(dot_ready, 1)
                        part = slice(q * BATCH, (q + 1) * BATCH)
                        dve.wait_ge(gelu_ready, n.after("gelu", e * 4 + q + 1))
                        dve.tensor_tensor(hid[e][:, part], gelu[e][:, part], gate[e][:, part], ALU.mult).then_inc(hid_ready, 1)

            dve.wait_ge(iota_ready, 1)
            link(dve.tensor_copy(iota_f[:, :], iota_i[:, :]))
            with n.rounds(dve, "keys_0"):
                stored_0 = n.after("empty4", 1)
            with n.rounds(dve, "query"):
                split_lo(0)
                split_lo(1)
                dve.wait_ge(bank_empty[4], stored_0)
                best_keys(0, (0,))
                split_lo(2)
                best_keys(0, (1,))
                split_lo(3)
            with n.rounds(dve, "query"):
                split_lo(0)
                best_pairs()
                split_lo(1)
                split_lo(2)
            with n.rounds(dve, "keys"):
                stored_all = n.after("empty7", 1)
            with n.rounds(dve, "route"):
                pairs_experts(0, 0)
                gates_softmax(0, 1)
            dve.wait_ge(bank_empty[7], stored_all)
            links = 2 * PER_ROUTE
            with n.rounds(dve, "pair"):
                heads(0, 0)
            with n.rounds(dve, "pair", 3, dve_step=links) as i:
                heads(i * 2 + 2, 0)
            with n.rounds(dve, "pair", 3, dve_step=links) as i:
                heads(i * 2 + 8, 1)

            def result(t):
                dve.wait_ge(acc_done, t + 1)
                for c in range(4):
                    part = slice(c * 512, (c + 1) * 512)
                    ins = dve.tensor_tensor(out_row[:, t, part], xres[:, t, part], bank[4 * t + c][:, :], ALU.add)
                ins.then_inc(out_ready, 1)

            result(0)
            with n.rounds(dve, "pair"):
                heads(14, 1, more=False)
            result(1)

        @block.tensor
        def _(pe):
            n = Counts()

            def into(b, k):
                wait(pe, bank_empty[b], n.after(f"empty{b}", k))

            def panel(c, conv=False):
                if conv:
                    pe.wait_ge(conv_split, n.after("conv_split", c + 1))
                else:
                    pe.wait_ge(split_ready, n.after("split", c))
                return c % 2

            def product(dst, left, right, start, stop):
                pe.matmul(dst, left[0], right[0], start=start, stop=False)
                pe.matmul(dst, left[0], right[1], start=False, stop=False)
                return pe.matmul(dst, left[1], right[0], start=False, stop=stop)

            def transposes(src, ready, key):
                for t in range(TT):
                    pe.wait_ge(ready, n.after(key, t + 1))
                    for b in range(4):
                        into(4 * t + b, 0)
                        for q in range(4):
                            k = 4 * b + q
                            ins = pe.transpose(bank[4 * t + b][:, q * 128:(q + 1) * 128], src[:, t, k * 128:(k + 1) * 128], ident[:, :])
                        ins.then_inc(bank_full[4 * t + b], 1)

            def feature_major(banks, tokens, c0, panels, kper, k, conv=False):
                width = len(banks) * 128
                for c in range(panels):
                    s = panel(c0 + c, conv)
                    for j, b in enumerate(banks):
                        for kk in range(kper):
                            kt = c * kper + kk
                            if kt == 0:
                                into(b, k)
                            where = slice(kk * width + j * 128, kk * width + (j + 1) * 128)
                            right = tokens(kt)
                            ins = product(bank[b][:, 0:right[0].shape[-1]], (w_hi[s][:, where], w_lo[s][:, where]), right,
                                          kt == 0, kt == panels * kper - 1)
                        if j == len(banks) - 1:
                            ins.then_inc(panel_used, 1)
                        elif c == panels - 1:
                            ins.then_inc(bank_full[b], 1)

            def token_major(banks):
                for c in range(4):
                    s = panel(c)
                    for t, b in enumerate(banks):
                        for kk in range(4):
                            kt = c * 4 + kk
                            if kt == 0:
                                into(b, 0)
                            tile, where = slice(t * 128, (t + 1) * 128), slice(kk * 512, (kk + 1) * 512)
                            ins = product(bank[b][:, :], (a_hi[:, kt, tile], a_lo[:, kt, tile]),
                                          (w_hi[s][:, where], w_lo[s][:, where]), kt == 0, kt == KT - 1)
                        if t == TT - 1:
                            ins.then_inc(panel_used, 1)
                        elif c == 3:
                            ins.then_inc(bank_full[b], 1)

            def all_tokens(k):
                return a_hi[:, k, :], a_lo[:, k, :]

            def tokens(k):
                return a_hi[:, k, 0:T], a_lo[:, k, 0:T]

            pe.wait_ge(const_ready, 3)
            with n.rounds(pe, "norm0"):
                transposes(xs0, xs_ready, "xs")
                pe.wait_ge(xs_ready, n.after("xs", TT + 1))
                into(0, 1)
                for k in range(KT):
                    ins = pe.transpose(bank[0][:, k * META:(k + 1) * META], meta_sb[:, k * 128:(k + 1) * 128], ident[0:META, 0:META])
                ins.then_inc(panel_used, 1)
            into(0, 0)
            with n.rounds(pe, "w_in", 4):
                for half in range(2):
                    feature_major((2 * half, 2 * half + 1), all_tokens, 4 * half, 2, 8, 0, True)
                    feature_major((4 + 2 * half, 5 + 2 * half), all_tokens, 4 * half + 2, 2, 8, 0, True)
            with n.rounds(pe, "ln"):
                pe.wait_ge(conv_ready, 1)
                into(0, 0)
                for k in range(KT):
                    ins = pe.matmul(bank[0][:, 0:T], ones[:, :], cvo[:, k, :], start=k == 0, stop=k == KT - 1)
                ins.then_inc(bank_full[0], 1)
                into(1, 0)
                for k in range(KT):
                    if k % 4 == 0:
                        pe.wait_ge(dev_sq_ready, n.after("dev_sq", k // 4 + 1))
                    ins = pe.matmul(bank[1][:, 0:T], ones[:, :], sq[:, k, :], start=k == 0, stop=k == KT - 1)
                ins.then_inc(bank_full[1], 1)
                pe.wait_ge(act_ready, n.after("act", 4))
            with n.rounds(pe, "w_out", 4):
                token_major((0, 1))
            with n.rounds(pe, "post"):
                transposes(xs, xs_ready, "xs")
            into(7, 0)
            with n.rounds(pe, "ffn", FF // 512):
                for blk in range(2):
                    feature_major((4 * blk, 4 * blk + 1), tokens, 4 * blk, 2, 8, 0)
                    feature_major((4 * blk + 2, 4 * blk + 3), tokens, 4 * blk + 2, 2, 8, 0)
                for f in range(4):
                    s = panel(8 + f)
                    pe.wait_ge(hlo_ready, n.after("hlo", f + 1))
                    for t in (1, 0):
                        for c in range(4):
                            b = c if t else 4 + c
                            if f == 0:
                                into(b, 1)
                            tile, where = slice(t * 128, (t + 1) * 128), slice(c * 512, (c + 1) * 512)
                            ins = product(bank[b][:, :], (h_hi[:, f, tile], h_lo[:, f, tile]),
                                          (w_hi[s][:, where], w_lo[s][:, where]), f == 0, f == 3)
                            if f == 3 and b < 7:
                                ins.then_inc(bank_full[b], 1)
                    ins.then_inc(panel_used, 1)
            with n.rounds(pe, "post"):
                transposes(xs, xs_ready, "xs")
            into(7, 0)
            with n.rounds(pe, "qk", 4):
                feature_major((0, 1, 2, 3), tokens, 0, 4, 4, 0)
            with n.rounds(pe, "forget"):
                pe.wait_ge(wflo_ready, n.after("wf_lo", 1))
                for t in range(TT):
                    into(6 + t, 0)
                    for k in range(KT):
                        tile = slice(t * 128, (t + 1) * 128)
                        ins = product(bank[6 + t][:, 0:HEADS], (a_hi[:, k, tile], a_lo[:, k, tile]),
                                      (wf_hi[:, k, :], wf_lo[:, k, :]), k == 0, k == KT - 1)
                    ins.then_inc(bank_full[6 + t], 1)
            for g in range(4):
                with n.rounds(pe, "qknorm"):
                    pe.wait_ge(qsq_ready, n.after("qsq", 1))
                    for p in range(2):
                        into(4 + p, 0)
                        pe.matmul(bank[4 + p][:, :], ones[:, :], qsq[:, 2 * p:2 * p + 2, :], start=True, stop=True)\
                            .then_inc(bank_full[4 + p], 1)
            with n.rounds(pe, "v", 2):
                token_major((4, 5))
            with n.rounds(pe, "cum"):
                pe.wait_ge(logf_ready, n.after("logf", 0))
                into(6, 0)
                first, second = fg[:, 5, 0:HEADS], fg[:, 5, HEADS:2 * HEADS]
                pe.matmul(bank[6][:, 0:HEADS], tri_ones[:, 0:128], first, start=True, stop=True)
                pe.matmul(bank[6][:, HEADS:2 * HEADS], ones[:, :], first, start=True, stop=False)
                pe.matmul(bank[6][:, HEADS:2 * HEADS], tri_ones[:, 0:128], second, start=False, stop=True).then_inc(bank_full[6], 1)
                pe.wait_ge(lfb_ready, n.after("lfb", 1))
                pe.wait_ge(qkn_ready, n.after("qkn", 0))
            for r in range(HEADS // 2):
                with n.rounds(pe, "score"):
                    for e in range(2):
                        h = 2 * r + e
                        into(e, 0)
                        pe.matmul(bank[e][:, 0:256], lfb[:, 0, h, :], tri_ones[:, :], start=True, stop=False)
                        pe.matmul(bank[e][:, 128:256], lfb[:, 1, h, :], tri_ones[:, 0:128], start=False, stop=True).then_inc(bank_full[e], 1)
                        into(2 + e, 0)
                        pe.matmul(bank[2 + e][:, 0:128], qk[:, h, 0:128], qk[:, HEADS + h, 0:128], start=True, stop=True)
                        pe.matmul(bank[2 + e][:, 128:384], qk[:, h, 128:256], qk[:, HEADS + h, :], start=True, stop=True)\
                            .then_inc(bank_full[2 + e], 1)
            with n.rounds(pe, "softmax"):
                pass
            with n.rounds(pe, "pin", 2):
                feature_major((0, 1, 2, 3), tokens, 0, 4, 4, 0)
            with n.rounds(pe, "pool"):
                for j in range(8):
                    b, g = 4 + j % 4, j // 2
                    pe.wait_ge(mixed_ready, n.after("mixed", g + 1))
                    into(b, j // 4)
                    for ci in range(2):
                        ins = pe.matmul(bank[b][:, 0:T], group_sb[:, g, ci, (j % 2) * 128:(j % 2 + 1) * 128], mixed[:, 2 * g + ci, :],
                                        start=ci == 0, stop=ci == 1)
                    ins.then_inc(bank_full[b], 1)
            pe.wait_ge(prob_ready, 2)
            for r in range(HEADS // 2):
                with n.rounds(pe, "heads"):
                    for e in range(2):
                        h = 2 * r + e
                        into(e, 0)
                        pe.transpose(bank[e][:, 0:128], lg0[:, h, :], ident[:, :])
                        pe.transpose(bank[e][:, 128:256], lg1[:, h, 0:128], ident[:, :])
                        pe.transpose(bank[e][:, 256:384], lg1[:, h, 128:256], ident[:, :]).then_inc(bank_full[e], 1)
                    for e in range(2):
                        h = 2 * r + e
                        head = slice(h * HD, (h + 1) * HD)
                        into(e, 1)
                        into(2 + e, 0)
                        pe.matmul(bank[2 + e][:, 0:T], vrow[:, 0, head], pts[:, e, 0:256], start=True, stop=False)
                        pe.matmul(bank[2 + e][:, 128:256], vrow[:, 1, head], pts[:, e, 256:384], start=False, stop=True)\
                            .then_inc(bank_full[2 + e], 1)
            into(3, 0)
            into(7, 0)
            with n.rounds(pe, "merge", 4):
                feature_major((0, 1, 2, 3), tokens, 0, 4, 4, 0)
                feature_major((4, 5, 6, 7), tokens, 4, 4, 4, 0)
                feature_major((0, 1, 2, 3), lambda k: (at_hi[:, k, :], at_lo[:, k, :]), 8, 2, 4, 1)
                feature_major((4, 5, 6, 7), lambda k: (po_hi[:, k, :], po_lo[:, k, :]), 10, 2, 4, 1)
            with n.rounds(pe, "merged"):
                pe.wait_ge(act_ready, n.after("act", 4))
            with n.rounds(pe, "w_out_2", 4):
                token_major((0, 1))
            with n.rounds(pe, "post_2"):
                transposes(xn, xn_ready, "xn")
            into(7, 0)
            def key_scores(t, two, b):
                into(b, 0)
                for hh in range(4 * two, 4 * two + 4):
                    q = hh % 4
                    ins = pe.matmul(bank[b][:, q * 128:(q + 1) * 128], qp[:, hh, t * 128:(t + 1) * 128], keys_sb[:, hh, :],
                                    start=True, stop=True)
                ins.then_inc(bank_full[b], 1)

            pe.wait_ge(late_loaded, 32)
            with n.rounds(pe, "query", 2):
                feature_major((0, 1, 2, 3), tokens, 0, 4, 4, 0)
            with n.rounds(pe, "keys_0"):
                key_scores(0, 0, 4)
            with n.rounds(pe, "query", 2):
                feature_major((0, 1, 2, 3), tokens, 0, 4, 4, 0)
            into(3, 0)
            with n.rounds(pe, "keys"):
                for t in range(TT):
                    for two in range(4):
                        if t or two:
                            key_scores(t, two, 4 * t + two)

            def nothing(t, start):
                for c in range(4):
                    ins = pe.matmul(bank[4 * t + c][:, :], zeros[:, :], xn[:, 0, 0:512], start=start, stop=not start)
                return ins

            def adds(t):
                for e in range(2):
                    for s in range(TOPK):
                        pe.wait_ge(diag_ready, n.after("diag", e * TOPK + s + 1))
                        pe.wait_ge(v_loaded[s % NV], n.after("v_rows", e * 2 + s // NV + 1) * 16)
                        for c in range(4):
                            ins = pe.matmul(bank[4 * t + c][:, :], diag[s % NDIAG][:, :], v_slot[s % NV][:, c * 512:(c + 1) * 512],
                                            start=False, stop=False)
                        ins.then_inc(v_used, 1)

            pe.wait_ge(zeros_ready, 1)
            for b in range(8):
                into(b, 0)
            for t in range(TT):
                nothing(t, True)
                with n.rounds(pe, "pair"):
                    adds(t)
                with n.rounds(pe, "pair", PH // 2 - 1):
                    adds(t)
                nothing(t, False).then_inc(acc_done, 1)


INPUTS = ("stream", "columns", "x", "meta", "b_out", "g_mix_post", "g_ffn_post", "g_norm2", "w_forget",
          "forget_bias", "group_w", "keys", "expert_u", "expert_v")


def laid_out(a):
    def wide(w):
        k, m = w.shape
        return w.reshape(k // 512, 4, 128, m // 512, 512).transpose(3, 0, 2, 1, 4).reshape(m // 512, k // 512, 128, 2048)

    def narrow(w):
        blocks = w.shape[1] // 256
        return w.reshape(2, 8, 128, blocks, 256).transpose(3, 0, 2, 1, 4).reshape(blocks, 2, 128, 2048)

    def column(v):
        return v.reshape(-1, 128).T

    w_in = narrow(a["conv_w_in"][0])
    first = np.concatenate([w_in[0:D // 256], w_in[D // 256:]], 1).reshape(-1, 128, 2048)
    gate_up = np.stack([narrow(a["ffn_w_gate"][0]), narrow(a["ffn_w_up"][0])], 1)
    ffn = np.concatenate([gate_up.reshape(FF // 512, 8, 128, 2048), a["ffn_w_down"][0].reshape(FF // 512, 4, 128, 2048)], 1)
    fox, w2 = HEADS * HD, a["w_in_2"][0]
    edges = [2 * fox, 3 * fox, 3 * fox + HEADS, 3 * fox + HEADS + POOL_W]
    w_qk, w_v, w_f, w_p, w_g = (w2[:, i:j] for i, j in zip([0] + edges, edges + [w2.shape[1]]))
    gates = wide(w_g)
    merge = np.concatenate([gates[0:4], gates[4:8], wide(a["w_branch_attn_2"][0]), wide(a["w_branch_pool_2"][0])], 1)
    flat = [w.reshape(-1, 128, 2048) for w in (wide(a["conv_w_out"][0]), ffn, wide(w_qk), wide(w_v), wide(w_p), merge,
                                               wide(a["w_out_2"][0]), wide(a["peer_w_query_2"][0]))]
    b_in = a["conv_b_in"][0]
    table = {"g_mix": column(a["norm_mix_pre"][0]), "b_a": column(b_in[:D]), "b_g": column(b_in[D:]),
             "w_dw": a["conv_w_dw"][0].reshape(TAPS, KT, 128).transpose(2, 1, 0).reshape(128, KT * TAPS),
             "b_dw": column(a["conv_b_dw"][0]), "ln_g": column(a["conv_ln_g"][0]), "ln_b": column(a["conv_ln_b"][0]),
             "g_ffn": column(a["norm_ffn_pre"][0]), "g_norm1": column(a["norm1_g_2"][0]),
             "g_q": column(a["q_norm_g_2"][0]), "g_k": column(a["k_norm_g_2"][0]), "pool_scale": column(a["pool_scale_2"][0])}
    keys = np.stack([a["peer_sub_keys_1_2"][0], a["peer_sub_keys_2_2"][0]], 1)
    return {
        "stream": np.concatenate([first] + flat, 0),
        "columns": np.concatenate([table[name] for name, _ in COLUMNS], 1),
        "x": a["x"][0], "meta": a["meta_tokens"], "b_out": a["conv_b_out"][0],
        "g_mix_post": a["norm_mix_post"][0], "g_ffn_post": a["norm_ffn_post"][0], "g_norm2": a["norm2_g_2"][0],
        "w_forget": w_f.reshape(KT, 128, HEADS).transpose(1, 0, 2),
        "forget_bias": a["forget_bias_2"][0],
        "group_w": a["pool_group_w_2"][0].reshape(4, 2, 128, 256).transpose(2, 0, 1, 3),
        "keys": keys.transpose(3, 0, 1, 2).reshape(128, 2 * PH, NKEYS),
        "expert_u": a["peer_expert_u_2"][0], "expert_v": a["peer_expert_v_2"][0],
    }


def kernel(**inputs):
    import concourse.bacc as bacc
    from concourse.bass_utils import run_bass_kernel_spmd

    nc = bacc.Bacc("TRN2", target_bir_lowering=False, num_devices=1)
    laid = laid_out({name: np.asarray(a) for name, a in inputs.items()})
    arrays, args = {}, []
    for name in INPUTS:
        a = np.ascontiguousarray(laid[name])
        arrays[f"in_{name}"] = a
        args.append(nc.dram_tensor(f"in_{name}", a.shape, mybir.dt.from_np(a.dtype), kind="ExternalInput").ap())
    args.append(nc.dram_tensor("out_0", (T, D), mybir.dt.float32, kind="ExternalOutput").ap())
    two_layers(nc, *args)
    r = run_bass_kernel_spmd(nc, [arrays], core_ids=[0])
    return r.results[0]["out_0"].reshape(1, T, D)
```

```python
from contextlib import ExitStack, contextmanager

import numpy as np
import concourse.bass as bass
from concourse import mybir

D = 2048
T, META = 256, 16
TT = T // 128
KT = D // 128
L = META + T
FF = 5632
TAPS = 31
HEADS, HD = 8, 128
POOL_W = 1024
POOL_WINDOWS = (2, 4, 8, 16)
PADP = 16
PH, TOPK, NKEYS = 8, 16, 128
SLOTS = PH * TOPK
RMS_EPS, LN_EPS = 1e-6, 1e-5
LOWEST = -3.0e38
MASKED = -1.0e30

PANELS = [("w_in", 32), ("w_out", 16), ("ffn", 132), ("qk", 16), ("pin", 8), ("v", 8),
          ("merge", 48), ("w_out_2", 16), ("query", 16)]
NPANELS = sum(n for _, n in PANELS)

COLUMNS = [("g_mix", KT), ("b_a", KT), ("b_g", KT), ("w_dw", KT * TAPS), ("b_dw", KT), ("ln_g", KT),
           ("ln_b", KT), ("g_ffn", KT), ("g_norm1", KT), ("g_q", 1), ("g_k", 1), ("pool_scale", 8)]
COL = {}
for _name, _n in COLUMNS:
    COL[_name] = sum(n for _, n in COLUMNS[:len(COL)])
NCOLS = sum(n for _, n in COLUMNS)


PER_ROUTE = 31

BANKS8 = range(8)


def per_round(**signals):
    full, empty = signals.pop("full", {}), signals.pop("empty", {})
    out = dict(signals)
    out.update({f"full{b}": k for b, k in full.items()})
    out.update({f"empty{b}": k for b, k in empty.items()})
    if "used" in out:
        out["split"] = out["hi"] = out["used"]
        out["quad"] = out["used"] // 4
    return out


def each(banks, k=1):
    return {b: k for b in banks}


PER_ROUND = {
    "norm0": dict(per_round(ssq=1, ms=1, root=1, rstd=1, xs=TT + 1, evac=9, full=each(BANKS8),
                            empty={**each(BANKS8), 0: 2}), used=1, hi=1),
    "w_in": dict(per_round(used=8, hi_half=8, conv_split=8, full=each((0, 2, 4, 6)), empty=each(BANKS8)), split=0),
    "ln": per_round(split=1, dev=4, dev_sq=4, root=1, ln=4, silu=KT // 4, silu_hi=4, act=4, full=each((0, 1)), empty=each((0, 1))),
    "w_out": per_round(used=4, full={0: 1}, empty=each((0, 1))),
    "post": per_round(ssq=2, ms=2, root=2, rstd=1, xs=TT, res=TT, evac=8, full=each(BANKS8), empty=each(BANKS8)),
    "ffn": per_round(used=12, hhi=4, hlo=4, full={**each((0, 2, 4, 6), 2), **each((1, 3, 5))}, empty=each(BANKS8, 2)),
    "qk": per_round(used=4, full=each((0, 1, 2)), empty=each(range(4))),
    "forget": per_round(z_step=2, z_ln=1, logf=1, full=each((6, 7)), empty=each((6, 7))),
    "qknorm": per_round(qsq=1, root=1, qkn=1, full=each((6, 7)), empty=each((6, 7))),
    "v": per_round(used=4, full={4: 1}, empty=each((4, 5))),
    "cum": per_round(lfb=1, full={6: 1}, empty={6: 1}),
    "score": per_round(full=each(range(4)), empty=each(range(4))),
    "softmax": per_round(negmax=1, exp=1, prob=2),
    "pin": per_round(used=4, full=each((0, 1, 2)), empty=each(range(4))),
    "pool": per_round(mixed=4, evac=8, full=each(range(4, 8), 2), empty=each(range(4, 8), 2)),
    "heads": per_round(evac=2, full=each(range(4)), empty=each(range(4))),
    "merge": per_round(used=12, part=4, full=each((0, 1, 2, 4, 5, 6), 2), empty=each(BANKS8, 2)),
    "gates_0": per_round(used=4, full=each((0, 1, 2)), empty=each(range(4))),
    "gates_1": per_round(used=4, full=each((4, 5, 6)), empty=each(range(4, 8))),
    "branches": per_round(used=4, part=4, full=each((0, 1, 2, 4, 5, 6)), empty=each(BANKS8)),
    "merged": per_round(merged_hi=4, act=4),
    "w_out_2": per_round(used=4, full={0: 1}, empty=each((0, 1))),
    "post_2": per_round(ssq=1, ms=1, root=1, rstd=1, xs=TT, evac=8, xn=TT, full=each(BANKS8), empty=each(BANKS8)),
    "query": per_round(used=4, full=each((0, 1, 2)), empty=each(range(4))),
    "keys_0": per_round(full={4: 1}, empty={4: 1}),
    "keys": per_round(full=each(range(1, 8)), empty=each(range(1, 8))),
    "route": per_round(expert=1, gate_max=1, gate_exp=1),
    "pair": per_round(expert=2, gate_max=2, gate_exp=2, dot=2 * TOPK, gelu=8, hid=8, diag=2 * TOPK, v_used=2 * TOPK,
                      u_rows=8, v_rows=4),
}


class Counts:

    def __init__(self):
        self.base, self.low = {}, {}

    def after(self, key, k):
        base = self.base.get(key, 0)
        assert isinstance(base, int) or self.low.get(key, 0) + k > 0, (key, k)
        return base + k

    @contextmanager
    def rounds(self, engine, stage, times=1, **own):
        per = {**PER_ROUND[stage], **own}
        start, low = dict(self.base), dict(self.low)
        if times == 1:
            yield 0
            start, low = self.base, self.low
        else:
            with engine.Fori(0, times) as i:
                self.base = {**start, **{key: start.get(key, 0) + i * k for key, k in per.items()}}
                yield i
        self.base = {**start, **{key: start.get(key, 0) + times * k for key, k in per.items()}}
        self.low = {**low, **{key: low.get(key, 0) + times * k for key, k in per.items()}}

    def past(self, stage, times=1):
        for key, k in PER_ROUND[stage].items():
            self.base[key] = self.base.get(key, 0) + times * k
            self.low[key] = self.low.get(key, 0) + times * k


def wait(engine, semaphore, value):
    if not (isinstance(value, int) and value <= 0):
        engine.wait_ge(semaphore, value)


def wait_apart(engine, semaphore, value, passed):
    if not (isinstance(value, int) and value <= 0):
        engine.wait_ge(semaphore, value)
        if not isinstance(value, int):
            engine.sem_inc(passed, 1)


def two_layers(nc, stream, columns, x, meta, b_out, g_mix_post, g_ffn_post, g_norm2, w_forget,
               forget_bias, group_w, keys, expert_u, expert_v, out):
    f32, f32r, u32 = mybir.dt.float32, mybir.dt.float32r, mybir.dt.uint32
    ACT, ALU, AX = mybir.ActivationFunctionType, mybir.AluOpType, mybir.AxisListType

    K = 1024
    at = (nc.sbuf_base + 63) // 64 * 64
    names = set()

    def place(name, shape, offset, dt=f32):
        assert name not in names
        names.add(name)
        return nc.alloc_sbuf_tensor_at(name, shape, dt, offset=offset)

    def keep(name, shape, dt=f32):
        nonlocal at
        t = place(name, shape, at, dt)
        at += (int(np.prod(shape[1:])) * 4 + 63) // 64 * 64
        return t

    cols = keep("s_cols", [128, NCOLS])
    ident = keep("s_ident", [128, 128])
    ones = keep("s_ones", [128, 128])
    tri_ones = keep("s_tri_ones", [128, 2 * 128])
    causal = keep("s_causal", [128, 128])
    group_sb = keep("s_group_w", [128, 4, 2, 256])
    wf_raw = keep("s_wf_raw", [128, KT, HEADS])
    wf_hi = keep("s_wf_hi", [128, KT, HEADS], f32r)
    wf_lo = keep("s_wf_lo", [128, KT, HEADS], f32r)
    fb = keep("s_forget_bias", [128, HEADS])
    stat = keep("s_stat", [128, 8])
    fg = keep("s_forget", [128, 6, TT * HEADS])
    cq = keep("s_cq", [128, TT * HEADS])
    negmax = keep("s_negmax", [128, TT * HEADS])
    den = keep("s_den", [128, TT * HEADS])
    inv_count = keep("s_inv_count", [128, 16])
    inv_count_i = keep("s_inv_count_i", [128, 16], mybir.dt.int32)
    xres = keep("s_xres", [128, TT, D])
    ring0 = at
    raw = [keep(f"s_raw{i}", [128, 2048]) for i in range(4)]
    w_hi = [keep(f"s_w_hi{i}", [128, 2048], f32r) for i in range(2)]
    w_lo = [keep(f"s_w_lo{i}", [128, 2048], f32r) for i in range(2)]
    a_hi = keep("s_a_hi", [128, KT, L], f32r)
    a_lo = keep("s_a_lo", [128, KT, L], f32r)
    S = at
    xs = place("s_xs", [128, TT, D], S + 16 * K)
    xs0 = place("s_xs0", [128, TT, D], S + 0)
    meta_sb = place("s_meta", [META, D], S + 16 * K)
    cvg = place("s_cvg", [128, 4, TAPS - 1 + L], S + 0)
    cacc = place("s_cacc", [128, 4, T], S + 5 * K)
    sig = place("s_sig", [128, 4, L], S + 9 * K)
    cvo = place("s_cvo", [128, KT, T], S + 16 * K)
    sq = place("s_sq", [128, KT, T], S + 32 * K)
    mean = place("s_mean", [128, T], S + 48 * K)
    rstd = place("s_rstd", [128, T], S + 49 * K)
    bout_row = place("s_bout_row", [128, D], S + 50 * K)
    gmix_row = place("s_gmix_row", [128, D], S + 58 * K)
    gffn_row = place("s_gffn_row", [128, D], S + 66 * K)
    yrow = place("s_yrow", [128, TT, D], S + 0)
    gained = place("s_gained", [128, TT, D], S + 32 * K)
    sg = place("s_sg", [128, 2, T], S + 32 * K)
    hf = place("s_hf", [128, 4, T], S + 34 * K)
    h_hi = place("s_h_hi", [128, 4, T], S + 38 * K, f32r)
    h_lo = place("s_h_lo", [128, 4, T], S + 42 * K, f32r)
    qk = place("s_qk", [128, 2 * HEADS, T], S + 0)
    vrow = place("s_vrow", [128, TT, HEADS * HD], S + 16 * K)
    pin = place("s_pin", [128, 8, PADP + T], S + 24 * K)
    mixed = place("s_mixed", [128, 8, T], S + 33 * K)
    qsq = place("s_qsq", [128, 4, T], S + 41 * K)
    qrs = place("s_qrs", [128, 4, T], S + 45 * K)
    lg0 = place("s_lg0", [128, HEADS, 128], S + 41 * K)
    lg1 = place("s_lg1", [128, HEADS, 256], S + 45 * K)
    lfb = place("s_lfb", [128, TT, HEADS, 128], S + 53 * K)
    at_hi = place("s_at_hi", [128, HEADS, T], S + 61 * K, f32r)
    at_lo = place("s_at_lo", [128, HEADS, T], S + 69 * K, f32r)
    bias_t = place("s_bias_t", [128, 2, 384], S + 61 * K)
    win_a = place("s_win_a", [128, 2, PADP + T], S + 65 * K)
    win_b = place("s_win_b", [128, 2, PADP + T], S + 69 * K)
    po_hi = place("s_po_hi", [128, 8, T], S + 24 * K, f32r)
    po_lo = place("s_po_lo", [128, 8, T], S + 53 * K, f32r)
    pts = place("s_pts", [128, 2, 384], S + 37 * K)
    merged = place("s_merged", [128, KT, T], S + 0)
    gate1 = place("s_gate1", [128, 4, T], S + 33 * K)
    xn = place("s_xn", [128, TT, D], S + 0)
    g2_row = place("s_g2_row", [128, D], S + 33 * K)
    keys_sb = place("s_keys", [128, 2 * PH, NKEYS], S + 41 * K)
    qp = place("s_qp", [128, 2 * PH, T], S + 49 * K)
    score = place("s_score", [128, TT * PH, 2 * NKEYS], S + 16 * K)
    NU, NV, NDIAG, BATCH, LEAD = 4, 8, 4, 4, 3
    u_slot = [place(f"s_u{i}", [128, D], ring0 + i * 8 * K) for i in range(NU)]
    v_slot = [place(f"s_v{i}", [128, D], ring0 + (NU + i) * 8 * K) for i in range(NV)]
    assert ring0 + (NU + NV) * 8 * K <= S
    P0 = S + 66 * K
    diag = [place(f"s_diag{i}", [128, 128], P0 + i * 512) for i in range(NDIAG)]
    P0 += NDIAG * 512

    def small(name, n, dt=f32):
        nonlocal P0
        t = place(name, [128, n], P0, dt)
        P0 += (4 * n + 63) // 64 * 64
        return t

    sc = small("s_sc", 2 * NKEYS)
    sc_rest = small("s_sc_rest", NKEYS)
    val = small("s_val", 2 * TOPK)
    ind = small("s_ind", 2 * TOPK, u32)
    indf = small("s_indf", 2 * TOPK)
    cand = small("s_cand", TOPK * TOPK)
    cand_rest = small("s_cand_rest", TOPK * TOPK)
    top = small("s_top", TOPK)
    pos = small("s_pos", TOPK, u32)
    pos1 = small("s_pos1", TOPK, u32)
    posf = small("s_posf", 2 * TOPK)
    pick = small("s_pick", TOPK * TOPK)
    chosen = small("s_chosen", 2 * TOPK)
    expert_f = small("s_expert_f", TOPK)
    expert = [small(f"s_expert{i}", TOPK, u32) for i in range(2)]
    gate = [small(f"s_pgate{i}", TOPK) for i in range(2)]
    gsum = small("s_gsum", 4)
    iota_i = small("s_iota_i", TOPK, mybir.dt.int32)
    iota_f = small("s_iota_f", TOPK)
    adot = [small(f"s_adot{i}", TOPK) for i in range(2)]
    gelu = [small(f"s_gelu{i}", TOPK) for i in range(2)]
    hid = [small(f"s_hid{i}", TOPK) for i in range(2)]
    assert P0 <= S + 78 * K, P0 - S
    zeros = place("s_zeros", [128, 128], S + 65 * K)
    out_row = place("s_out_row", [128, TT, D], S + 33 * K)

    with ExitStack() as ctx:
        bank = [ctx.enter_context(nc.psum_tensor(f"bank{b}", [128, 512], f32)) for b in range(8)]

        def sem(name):
            return ctx.enter_context(nc.semaphore(name))

        raw_loaded = [sem(f"raw_loaded{i}") for i in range(4)]
        hi_half = sem("hi_half")
        hi_ready = sem("hi_ready")
        split_ready = sem("split_ready")
        conv_split = sem("conv_split")
        panel_used = sem("panel_used")
        bank_full = [sem(f"bank_full{b}") for b in range(8)]
        bank_empty = [sem(f"bank_empty{b}") for b in range(8)]
        pool_passed, dve_passed = sem("pool_passed"), sem("dve_passed")
        dve_step = sem("dve_step")
        pool_step = sem("pool_step")
        x_loaded = [sem(f"x_loaded{t}") for t in range(TT)]
        meta_loaded, cols_loaded = sem("meta_loaded"), sem("cols_loaded")
        rows_loaded, small_loaded, late_loaded = sem("rows_loaded"), sem("small_loaded"), sem("late_loaded")
        const_ready, stat_clear = sem("const_ready"), sem("stat_clear")
        evac_hi = sem("evac_hi")
        ssq_ready = sem("ssq_ready")
        ms_ready = sem("ms_ready")
        root_ready = sem("root_ready")
        rstd_ready = sem("rstd_ready")
        xs_ready = sem("xs_ready")
        res_ready = sem("res_ready")
        conv_ready = sem("conv_ready")
        dev_ready = sem("dev_ready")
        dev_sq_ready = sem("dev_sq_ready")
        ln_ready = sem("ln_ready")
        silu_ready, silu_hi = sem("silu_ready"), sem("silu_hi")
        act_ready = sem("act_ready")
        hhi_ready, hlo_ready = sem("hhi_ready"), sem("hlo_ready")
        wfhi_ready, wflo_ready = sem("wfhi_ready"), sem("wflo_ready")
        counts_ready = sem("counts_ready")
        z_step, z_ln, logf_ready = sem("z_step"), sem("z_ln"), sem("logf_ready")
        qsq_ready, qkn_ready = sem("qsq_ready"), sem("qkn_ready")
        lfb_ready = sem("lfb_ready")
        negmax_ready, exp_ready, prob_ready = sem("negmax_ready"), sem("exp_ready"), sem("prob_ready")
        mixed_ready, part_ready = sem("mixed_ready"), sem("part_ready")
        merged_hi, xn_ready = sem("merged_hi"), sem("xn_ready")
        zeros_ready, iota_ready = sem("zeros_ready"), sem("iota_ready")
        expert_ready = sem("expert_ready")
        gate_max, gate_exp = sem("gate_max"), sem("gate_exp")
        u_loaded = [sem(f"u_loaded{i}") for i in range(NU)]
        v_loaded = [sem(f"v_loaded{i}") for i in range(NV)]
        dot_ready, gelu_ready, hid_ready = sem("dot_ready"), sem("gelu_ready"), sem("hid_ready")
        diag_ready, v_used = sem("diag_ready"), sem("v_used")
        acc_done, out_ready, stored = sem("acc_done"), sem("out_ready"), sem("stored")

        def four_tiles(b):
            return bank[b][:, :].rearrange("p (a t) -> p a t", a=4)

        block = ctx.enter_context(nc.Block())

        @block.sync
        def _(sp):
            sp.dma_start(meta_sb[:, :], meta).then_inc(meta_loaded, 16)
            for t in range(TT):
                sp.dma_start(xres[:, t, :], x[t * 128:(t + 1) * 128, :]).then_inc(x_loaded[t], 16)
            sp.dma_start(cols[:, :], columns).then_inc(cols_loaded, 16)
            for s in range(4):
                sp.dma_start(raw[s][:, :], stream[s]).then_inc(raw_loaded[s], 16)
            panels = stream.rearrange("(q s) p n -> q s p n", s=4)
            with sp.Fori(1, NPANELS // 4) as q:
                for s in range(4):
                    sp.wait_ge(panel_used, q * 4 + (s - 4 + 1 + 1))
                    sp.dma_start(raw[s][:, :], panels[bass.ds(q, 1), s].rearrange("a p n -> (a p) n"))\
                        .then_inc(raw_loaded[s], 16)
            for t in range(TT):
                sp.wait_ge(out_ready, t + 1)
                sp.dma_start(out[t * 128:(t + 1) * 128, :], out_row[:, t, :]).then_inc(stored, 16)
            sp.wait_ge(stored, 16 * TT)

        @block.gpsimd
        def _(pool):
            n = Counts()
            pool.memset(ident[:, :], 0.0).then_inc(pool_step, 1)
            pool.memset(ones[:, :], 1.0).then_inc(pool_step, 1)
            pool.memset(tri_ones[:, :], 1.0).then_inc(pool_step, 1)
            pool.memset(causal[:, :], 0.0).then_inc(pool_step, 1)
            pool.iota(inv_count_i[:, :], pattern=[[1, 16]], base=1, channel_multiplier=0).then_inc(pool_step, 1)
            n.base["pool_step"] = 5
            pool.wait_ge(pool_step, n.base["pool_step"])
            pool.affine_select(out=ident[:, :], in_=ident[:, :], compare_op=ALU.not_equal, fill=1.0,
                               base=0, pattern=[[-1, 128]], channel_multiplier=1).then_inc(const_ready, 1)
            pool.affine_select(out=tri_ones[:, :], in_=tri_ones[:, :], compare_op=ALU.is_ge, fill=0.0,
                               base=0, pattern=[[1, 256]], channel_multiplier=-1).then_inc(const_ready, 1)
            pool.affine_select(out=causal[:, :], in_=causal[:, :], compare_op=ALU.is_ge, fill=MASKED,
                               base=0, pattern=[[-1, 128]], channel_multiplier=1).then_inc(const_ready, 1)
            for row, src in ((bout_row, b_out), (gmix_row, g_mix_post), (gffn_row, g_ffn_post)):
                pool.dma_start(row[:, :], src.partition_broadcast(128)).then_inc(rows_loaded, 16)
            pool.dma_start(wf_raw[:, :, :], w_forget).then_inc(small_loaded, 16)
            pool.dma_start(fb[:, :], forget_bias.partition_broadcast(128)).then_inc(small_loaded, 16)
            pool.dma_start(group_sb[:, :, :, :], group_w).then_inc(small_loaded, 16)
            with n.rounds(pool, "norm0"):
                pass
            with n.rounds(pool, "w_in", 4):
                for c in range(8):
                    s = c % 4
                    for ready, key, half in ((hi_half, "hi_half", slice(0, 1024)), (hi_ready, "hi", slice(1024, 2048))):
                        pool.wait_ge(ready, n.after(key, c if key == "hi" else c + 1))
                        ins = pool.tensor_tensor(w_lo[s % 2][:, half], raw[s][:, half], w_hi[s % 2][:, half].bitcast(f32),
                                                 ALU.subtract)
                    ins.then_inc(conv_split, 1)
            def step(ins):
                ins.then_inc(pool_step, 1)
                n.base["pool_step"] += 1

            def link(ins):
                step(ins)
                pool.wait_ge(pool_step, n.base["pool_step"])

            for stage, times in (("ln", 1), ("w_out", 4), ("post", 2), ("ffn", FF // 512), ("qk", 4), ("forget", 1), ("pin", 2)):
                n.past(stage, times)
            pool.wait_ge(counts_ready, 1)
            pool.wait_ge(bank_empty[3], n.after("empty3", 0))
            link(pool.memset(pin[:, :, 0:PADP], 0.0))
            for g, w in enumerate(POOL_WINDOWS):
                src, s = pin[:, 2 * g:2 * g + 2, :], 1
                own = src
                for k in range(g + 1):
                    dst = (win_a, win_b)[k % 2][:, :, :]
                    low = 2 * s - 1
                    link(pool.tensor_tensor(dst[:, :, low:], src[:, :, low:], src[:, :, low - s:PADP + T - s], ALU.add))
                    src, s = dst, 2 * s
                early = slice(PADP, PADP + w - 1)
                late = slice(PADP + w - 1, PADP + T)
                some = mixed[:, 2 * g:2 * g + 2, :]
                step(pool.tensor_scalar(some[:, :, w - 1:], src[:, :, late], 1.0 / w, None, ALU.mult))
                link(pool.tensor_tensor(some[:, :, 0:w - 1], src[:, :, early],
                                        inv_count[:, 0:w - 1].unsqueeze(1).to_broadcast([128, 2, w - 1]), ALU.mult))
                pool.tensor_tensor(some, some, own[:, :, PADP:], ALU.subtract).then_inc(mixed_ready, 1)
            pool.wait_ge(act_ready, 4 + 4)
            pool.dma_start(g2_row[:, :], g_norm2.partition_broadcast(128)).then_inc(late_loaded, 16)
            pool.dma_start(keys_sb[:, :, :], keys).then_inc(late_loaded, 16)
            pool.iota(iota_i[:, :], pattern=[[1, TOPK]], base=0, channel_multiplier=0).then_inc(iota_ready, 1)
            pool.memset(zeros[:, :], 0.0).then_inc(zeros_ready, 1)

            with n.rounds(pool, "route"):
                pass
            pool.wait_ge(panel_used, NPANELS + 1)

            def gathers():
                for k in range(2 * TOPK + LEAD):
                    if k < 2 * TOPK:
                        e, s = divmod(k, TOPK)
                        if s == 0:
                            wait_apart(pool, expert_ready, n.after("expert", e), pool_passed)
                        index = bass.IndirectOffsetOnAxis(ap=expert[e][:, s:s + 1], axis=0)
                        wait_apart(pool, dot_ready, n.after("dot", k + 1 - NU), pool_passed)
                        pool.indirect_dma_start(u_slot[s % NU][:, :], None, expert_u, index)\
                            .then_inc(u_loaded[s % NU], 16)
                    if k >= LEAD:
                        e, s = divmod(k - LEAD, TOPK)
                        index = bass.IndirectOffsetOnAxis(ap=expert[e][:, s:s + 1], axis=0)
                        wait_apart(pool, v_used, n.after("v_used", k - LEAD + 1 - NV), pool_passed)
                        pool.indirect_dma_start(v_slot[s % NV][:, :], None, expert_v, index)\
                            .then_inc(v_loaded[s % NV], 16)

            with n.rounds(pool, "pair"):
                gathers()
            with n.rounds(pool, "pair", TT * PH // 2 - 1):
                gathers()

        @block.scalar
        def _(act):
            n = Counts()

            def col(name, k):
                return cols[:, COL[name] + k:COL[name] + k + 1]

            def split_hi(c, halves=False):
                s = (c + 1) % 4
                act.wait_ge(raw_loaded[s], n.after("quad", (c + 1) // 4 + 1) * 16)
                act.wait_ge(panel_used, n.after("used", c))
                if halves:
                    act.activation(w_hi[s % 2][:, 0:1024], raw[s][:, 0:1024], ACT.Copy).then_inc(hi_half, 1)
                    act.activation(w_hi[s % 2][:, 1024:], raw[s][:, 1024:], ACT.Copy).then_inc(hi_ready, 1)
                    return
                act.activation(w_hi[s % 2][:, :], raw[s][:, :], ACT.Copy).then_inc(hi_ready, 1)

            def sums_of_squares(src, junk, ready=None):
                for t in range(TT):
                    if ready:
                        act.wait_ge(ready[0], n.after(ready[1], t + 1))
                    ins = act.activation(junk[:, t, :], src[:, t, :], ACT.Square, accum_out=stat[:, t:t + 1])
                ins.then_inc(ssq_ready, 1)

            def root(k, width=TT):
                act.wait_ge(ms_ready, n.after("ms", k))
                act.activation(stat[:, 4:4 + width], stat[:, 4:4 + width], ACT.Sqrt).then_inc(root_ready, 1)

            def transposed_hi(gain, offset):
                for t in range(TT):
                    for b in range(4):
                        act.wait_ge(bank_full[4 * t + b], n.after(f"full{4 * t + b}", 1))
                        if not gain:
                            act.activation(a_hi[:, 4 * b:4 * b + 4, t * 128:(t + 1) * 128], four_tiles(4 * t + b), ACT.Copy)\
                                .then_inc(evac_hi, 1)
                            continue
                        for q in range(4):
                            k = 4 * b + q
                            ins = act.activation(a_hi[:, k, offset + t * 128:offset + (t + 1) * 128],
                                                 bank[4 * t + b][:, q * 128:(q + 1) * 128], ACT.Copy, scale=col(gain, k))
                        ins.then_inc(evac_hi, 1)

            with n.rounds(act, "norm0"):
                act.wait_ge(stat_clear, 1)
                act.wait_ge(meta_loaded, 16)
                act.activation(sq[0:META, 0:8, :].rearrange("p a t -> p (a t)"), meta_sb[:, :], ACT.Square,
                               accum_out=stat[0:META, 2:3])
                for t in range(TT):
                    act.wait_ge(x_loaded[t], 16)
                    ins = act.activation(xs0[:, t, :], xres[:, t, :], ACT.Square, accum_out=stat[:, t:t + 1])
                ins.then_inc(ssq_ready, 1)
                root(1, 3)
                act.wait_ge(rstd_ready, n.after("rstd", 1))
                for t in range(TT):
                    act.activation(xs0[:, t, :], xres[:, t, :], ACT.Copy, scale=stat[:, 4 + t:5 + t])\
                        .then_inc(xs_ready, 1)
                act.activation(meta_sb[:, :], meta_sb[:, :], ACT.Copy, scale=stat[0:META, 6:7]).then_inc(xs_ready, 1)
                act.wait_ge(raw_loaded[0], 16)
                act.activation(w_hi[0][:, 0:1024], raw[0][:, 0:1024], ACT.Copy).then_inc(hi_half, 1)
                act.activation(w_hi[0][:, 1024:], raw[0][:, 1024:], ACT.Copy).then_inc(hi_ready, 1)
                act.wait_ge(cols_loaded, 16)
                transposed_hi("g_mix", META)
                act.wait_ge(panel_used, n.after("used", 1))
                for k in range(KT):
                    ins = act.activation(a_hi[:, k, 0:META], bank[0][:, k * META:(k + 1) * META], ACT.Copy,
                                         scale=col("g_mix", k))
                ins.then_inc(evac_hi, 1)

            with n.rounds(act, "w_in", 4) as i:
                for c in range(8):
                    split_hi(c, halves=True)
                    if c % 4 < 3:
                        continue
                    j = c // 4 * 2
                    act.wait_ge(bank_empty[j + 1], n.after(f"empty{j + 1}", 0))
                    act.wait_ge(bank_full[4 + j], n.after(f"full{4 + j}", 1))
                    act.activation(sig[:, j, :], bank[4 + j][:, 0:L], ACT.Sigmoid,
                                   bias=cols[:, bass.ds(i * 4 + (COL["b_g"] + j), 1)]).then_inc(bank_empty[4 + j], 1)
                    j += 1
                    act.wait_ge(panel_used, n.after("used", c + 1))
                    act.activation(sig[:, j, :], bank[4 + j][:, 0:L], ACT.Sigmoid,
                                   bias=cols[:, bass.ds(i * 4 + (COL["b_g"] + j), 1)]).then_inc(bank_empty[4 + j], 1)

            with n.rounds(act, "ln"):
                for g in range(4):
                    act.wait_ge(dev_ready, n.after("dev", g + 1))
                    act.activation(sq[:, 4 * g:4 * g + 4, :], cvo[:, 4 * g:4 * g + 4, :], ACT.Square)\
                        .then_inc(dev_sq_ready, 1)
                act.wait_ge(bank_empty[1], n.after("empty1", 1))
                act.activation(rstd[:, :], rstd[:, :], ACT.Sqrt).then_inc(root_ready, 1)
                for g in range(4):
                    act.wait_ge(ln_ready, n.after("ln", g + 1))
                    for k in range(4 * g, 4 * g + 4):
                        ins = act.activation(sq[:, k, :], cvo[:, k, :], ACT.Silu, scale=col("ln_g", k), bias=col("ln_b", k))
                    ins.then_inc(silu_ready, 1)
                    act.wait_ge(silu_ready, n.after("silu", g + 1))
                    act.activation(a_hi[:, 4 * g:4 * g + 4, 0:T], sq[:, 4 * g:4 * g + 4, :], ACT.Copy).then_inc(silu_hi, 1)

            with n.rounds(act, "w_out", 4):
                for c in range(4):
                    split_hi(c)

            def post(last_bank, gain):
                act.wait_ge(bank_empty[last_bank], n.after(f"empty{last_bank}", 0))
                sums_of_squares(yrow, xs)
                root(1)
                sums_of_squares(xres, xs, (res_ready, "res"))
                root(2)
                act.wait_ge(rstd_ready, n.after("rstd", 1))
                for t in range(TT):
                    act.activation(xs[:, t, :], xres[:, t, :], ACT.Copy, scale=stat[:, 4 + t:5 + t])\
                        .then_inc(xs_ready, 1)
                transposed_hi(gain, 0)

            with n.rounds(act, "post"):
                post(1, "g_ffn")

            with n.rounds(act, "ffn", FF // 512):
                for blk in range(2):
                    c0 = 4 * blk
                    split_hi(c0)
                    split_hi(c0 + 1)
                    for j in range(2):
                        b = 2 + j if blk else 6 + j
                        act.wait_ge(bank_empty[b], n.after(f"empty{b}", blk))
                        if j == 0:
                            act.wait_ge(bank_full[c0], n.after(f"full{c0}", 1))
                        else:
                            act.wait_ge(panel_used, n.after("used", c0 + 2))
                        act.activation(sg[:, j, :], bank[c0 + j][:, 0:T], ACT.Silu).then_inc(bank_empty[c0 + j], 1)
                    split_hi(c0 + 2)
                    split_hi(c0 + 3)
                    for j in range(2):
                        b = c0 + 2 + j
                        act.wait_ge(bank_empty[b], n.after(f"empty{b}", 1))
                        act.activation(h_hi[:, 2 * blk + j, :], hf[:, 2 * blk + j, :], ACT.Copy).then_inc(hhi_ready, 1)
                for c in range(8, 12):
                    split_hi(c)

            with n.rounds(act, "post"):
                post(7, "g_norm1")

            def copies_out(i, dst, offset):
                for j in range(4):
                    if j < 3:
                        act.wait_ge(bank_full[j], n.after(f"full{j}", 1))
                    else:
                        act.wait_ge(panel_used, n.after("used", 4))
                    act.activation(dst[:, bass.ds(i * 4 + j, 1), offset:offset + T].rearrange("p a t -> p (a t)"),
                                   bank[j][:, 0:T], ACT.Copy).then_inc(bank_empty[j], 1)

            act.wait_ge(small_loaded, 48)
            act.activation(wf_hi[:, :, :], wf_raw[:, :, :], ACT.Copy).then_inc(wfhi_ready, 1)
            with n.rounds(act, "qk", 4) as i:
                for c in range(4):
                    split_hi(c)
                copies_out(i, qk, 0)
            heads_stored = n.after("empty3", 0)

            def log_sigmoid():
                with n.rounds(act, "forget"):
                    act.wait_ge(bank_empty[7], n.after("empty7", 1))
                    act.activation(fg[:, 1, :], fg[:, 0, :], ACT.Abs).then_inc(z_step, 1)
                    act.wait_ge(z_step, n.after("z_step", 1))
                    act.activation(fg[:, 1, :], fg[:, 1, :], ACT.Exp, scale=-1.0).then_inc(z_step, 1)
                    act.wait_ge(z_step, n.after("z_step", 2))
                    act.activation(fg[:, 2, :], fg[:, 1, :], ACT.Ln, bias=1.0).then_inc(z_ln, 1)

            def head_norm(g, c):
                with n.rounds(act, "qknorm"):
                    act.wait_ge(bank_empty[3], heads_stored)
                    wait(act, qkn_ready, n.after("qkn", 0))
                    act.activation(qsq[:, :, :], qk[:, 4 * g:4 * g + 4, :], ACT.Square).then_inc(qsq_ready, 1)
                    split_hi(c)
                    act.wait_ge(bank_empty[7], n.after("empty7", 1))
                    act.activation(qrs[:, :, :], qrs[:, :, :], ACT.Sqrt).then_inc(root_ready, 1)

            for r in range(2):
                with n.rounds(act, "pin"):
                    split_hi(0)
                    if r == 0:
                        log_sigmoid()
                    head_norm(2 * r, 1)
                    split_hi(2)
                    head_norm(2 * r + 1, 3)
                    copies_out(r, pin, PADP)
            for r in range(2):
                with n.rounds(act, "v"):
                    for c in range(4):
                        split_hi(c)
                    for t in range(TT):
                        if t == 0:
                            act.wait_ge(bank_full[4], n.after("full4", 1))
                        else:
                            act.wait_ge(panel_used, n.after("used", 4))
                        act.activation(vrow[:, t, r * 512:(r + 1) * 512], bank[4 + t][:, :], ACT.Copy).then_inc(bank_empty[4 + t], 1)
            n.past("cum")
            n.past("score", HEADS // 2)

            def exponentials():
                with n.rounds(act, "softmax"):
                    act.wait_ge(negmax_ready, n.after("negmax", 1))
                    for h in range(HEADS):
                        act.activation(lg0[:, h, :], lg0[:, h, :], ACT.Exp, bias=negmax[:, h:h + 1],
                                       accum_out=den[:, h:h + 1])
                        ins = act.activation(lg1[:, h, :], lg1[:, h, :], ACT.Exp, bias=negmax[:, HEADS + h:HEADS + h + 1],
                                             accum_out=den[:, HEADS + h:HEADS + h + 1])
                    ins.then_inc(exp_ready, 1)

            def pooled(half):
                for j in range(4 * half, 4 * half + 4):
                    b = 4 + j % 4
                    act.wait_ge(bank_full[b], n.after(f"full{b}", half + 1))
                    act.activation(po_hi[:, j, :], bank[b][:, 0:T], ACT.Copy, scale=col("pool_scale", j)).then_inc(evac_hi, 1)

            def gates_0(i):
                for j in range(4):
                    if j < 3:
                        act.wait_ge(bank_full[j], n.after(f"full{j}", 1))
                    else:
                        act.wait_ge(panel_used, n.after("used", 4))
                    act.activation(merged[:, bass.ds(i * 4 + j, 1), :].rearrange("p a t -> p (a t)"), bank[j][:, 0:T], ACT.Sigmoid)\
                        .then_inc(bank_empty[j], 1)

            def gates_1():
                wait(act, part_ready, n.after("part", 0))
                for j in range(4):
                    b = 4 + j
                    if j < 3:
                        act.wait_ge(bank_full[b], n.after(f"full{b}", 1))
                    else:
                        act.wait_ge(panel_used, n.after("used", 4))
                    act.activation(gate1[:, j, :], bank[b][:, 0:T], ACT.Sigmoid).then_inc(bank_empty[b], 1)

            with n.rounds(act, "gates_0"):
                with n.rounds(act, "pool"):
                    split_hi(0)
                    split_hi(1)
                    exponentials()
                    split_hi(2)
                    pooled(0)
                    split_hi(3)
                    gates_0(0)
                    pooled(1)
            with n.rounds(act, "gates_1"):
                for r in range(HEADS // 2):
                    with n.rounds(act, "heads"):
                        for e in range(2):
                            act.wait_ge(bank_full[e], n.after(f"full{e}", 1))
                            act.activation(pts[:, e, :], bank[e][:, 0:384], ACT.Copy).then_inc(bank_empty[e], 1)
                        split_hi(r)
                        for e in range(2):
                            act.wait_ge(bank_full[2 + e], n.after(f"full{2 + e}", 1))
                            act.activation(at_hi[:, 2 * r + e, :], bank[2 + e][:, 0:T], ACT.Copy).then_inc(evac_hi, 1)
                gates_1()
            with n.rounds(act, "branches"):
                for c in range(4):
                    split_hi(c)
            with n.rounds(act, "merge", 3) as i:
                with n.rounds(act, "gates_0"):
                    for c in range(4):
                        split_hi(c)
                    gates_0(i + 1)
                with n.rounds(act, "gates_1"):
                    for c in range(4):
                        split_hi(c)
                    gates_1()
                with n.rounds(act, "branches"):
                    for c in range(4):
                        split_hi(c)
            with n.rounds(act, "merged"):
                act.wait_ge(part_ready, n.after("part", 0))
                for g in range(4):
                    act.activation(a_hi[:, 4 * g:4 * g + 4, 0:T], merged[:, 4 * g:4 * g + 4, :], ACT.Copy).then_inc(merged_hi, 1)
            with n.rounds(act, "w_out_2", 4):
                for c in range(4):
                    split_hi(c)
            with n.rounds(act, "post_2"):
                act.wait_ge(bank_empty[1], n.after("empty1", 0))
                sums_of_squares(xres, xs)
                root(1)
                act.wait_ge(rstd_ready, n.after("rstd", 1))
                for t in range(TT):
                    act.activation(xs[:, t, :], xres[:, t, :], ACT.Copy, scale=stat[:, 4 + t:5 + t]).then_inc(xs_ready, 1)
                transposed_hi(None, 0)
            with n.rounds(act, "query"):
                for c in range(4):
                    split_hi(c)
                copies_out(0, qp, 0)
            for r in (1, 2):
                with n.rounds(act, "query"):
                    for c in range(4):
                        split_hi(c)
                        if r == 2 and c == 0:
                            act.wait_ge(bank_full[4], n.after("full4", 0))
                            act.activation(score[:, 0:2, :].rearrange("p h k -> p (h k)"), bank[4][:, :], ACT.Copy)\
                                .then_inc(bank_empty[4], 1)
                    copies_out(r, qp, 0)
                if r == 1:
                    with n.rounds(act, "keys_0"):
                        pass
            with n.rounds(act, "query"):
                for c in range(3):
                    split_hi(c)
                copies_out(3, qp, 0)
            with n.rounds(act, "keys"):
                for t in range(TT):
                    for b in range(4):
                        if t == b == 0:
                            continue
                        act.wait_ge(bank_full[4 * t + b], n.after(f"full{4 * t + b}", 1))
                        act.activation(score[:, t * PH + 2 * b:t * PH + 2 * b + 2, :].rearrange("p h k -> p (h k)"),
                                       bank[4 * t + b][:, :], ACT.Copy).then_inc(bank_empty[4 * t + b], 1)

            def gate_exps(parity, k):
                act.wait_ge(gate_max, n.after("gate_max", k))
                act.activation(gate[parity][:, :], top[:, :], ACT.Exp, bias=gsum[:, 0:1], accum_out=gsum[:, 1:2])\
                    .then_inc(gate_exp, 1)

            def heads(more=True):
                for e in range(2):
                    for q in range(TOPK // BATCH):
                        if q == 2 and (more or e == 0):
                            gate_exps(1 - e, e + 1)
                        part = slice(q * BATCH, (q + 1) * BATCH)
                        act.wait_ge(dot_ready, n.after("dot", e * TOPK + (q + 1) * BATCH))
                        act.activation(gelu[e][:, part], adot[e][:, part], ACT.Gelu_apprx_tanh).then_inc(gelu_ready, 1)
                        act.wait_ge(hid_ready, n.after("hid", e * TOPK // BATCH + q + 1))
                        for s in range(q * BATCH, (q + 1) * BATCH):
                            wait(act, v_used, n.after("v_used", e * TOPK + s + 1 - NDIAG))
                            act.activation(diag[s % NDIAG][:, :], ident[:, :], ACT.Copy, scale=hid[e][:, s:s + 1])\
                                .then_inc(diag_ready, 1)

            with n.rounds(act, "route"):
                gate_exps(0, 1)
            with n.rounds(act, "pair"):
                heads()
            with n.rounds(act, "pair", TT * PH // 2 - 2):
                heads()
            with n.rounds(act, "pair"):
                heads(more=False)

        @block.vector
        def _(dve):
            n = Counts()

            def col(name, k):
                return cols[:, COL[name] + k:COL[name] + k + 1]

            def step(ins):
                ins.then_inc(dve_step, 1)
                n.base["dve_step"] = n.base.get("dve_step", 0) + 1

            def settled(back=0):
                dve.wait_ge(dve_step, n.base["dve_step"] - back)

            def link(ins):
                step(ins)
                settled()

            def split_lo(c):
                s = (c + 1) % 4
                dve.wait_ge(hi_ready, n.after("hi", c + 1))
                dve.tensor_tensor(w_lo[s % 2][:, :], raw[s][:, :], w_hi[s % 2][:, :].bitcast(f32), ALU.subtract)\
                    .then_inc(split_ready, 1)

            def mean_square(k, width=TT):
                dve.wait_ge(ssq_ready, n.after("ssq", k))
                dve.tensor_scalar(stat[:, 4:4 + width], stat[:, 0:width], 1.0 / D, RMS_EPS, ALU.mult, ALU.add)\
                    .then_inc(ms_ready, 1)

            def inverse(k, width=TT):
                dve.wait_ge(root_ready, n.after("root", k))
                dve.reciprocal(stat[:, 4:4 + width], stat[:, 4:4 + width]).then_inc(rstd_ready, 1)

            def transposed_lo(gain, offset):
                for t in range(TT):
                    for b in range(4):
                        dve.wait_ge(evac_hi, n.after("evac", 4 * t + b + 1))
                        if not gain:
                            four = slice(4 * b, 4 * b + 4), slice(t * 128, (t + 1) * 128)
                            dve.tensor_tensor(a_lo[:, *four], four_tiles(4 * t + b), a_hi[:, *four].bitcast(f32), ALU.subtract)\
                                .then_inc(bank_empty[4 * t + b], 1)
                            continue
                        for q in range(4):
                            k = 4 * b + q
                            where = slice(offset + t * 128, offset + (t + 1) * 128)
                            ins = dve.scalar_tensor_tensor(
                                a_lo[:, k, where], bank[4 * t + b][:, q * 128:(q + 1) * 128],
                                col(gain, k), a_hi[:, k, where].bitcast(f32), ALU.mult, ALU.subtract)
                        ins.then_inc(bank_empty[4 * t + b], 1)

            dve.memset(stat[:, :], 1.0).then_inc(stat_clear, 1)
            dve.wait_ge(const_ready, 3)
            link(dve.tensor_copy(inv_count[:, :], inv_count_i[:, :]))
            dve.reciprocal(inv_count[:, :], inv_count[:, :]).then_inc(counts_ready, 1)
            with n.rounds(dve, "norm0"):
                mean_square(1, 3)
                inverse(1, 3)
                dve.wait_ge(cols_loaded, 16)
                transposed_lo("g_mix", META)
                dve.wait_ge(evac_hi, n.after("evac", 9))
                for k in range(KT):
                    ins = dve.scalar_tensor_tensor(a_lo[:, k, 0:META], bank[0][:, k * META:(k + 1) * META], col("g_mix", k),
                                                   a_hi[:, k, 0:META].bitcast(f32), ALU.mult, ALU.subtract)
                ins.then_inc(bank_empty[0], 1)
                link(dve.memset(cvg[:, :, 0:TAPS - 1], 0.0))

            def glu(i, half):
                for j in (2 * half, 2 * half + 1):
                    if j % 2 == 0:
                        dve.wait_ge(bank_full[j], n.after(f"full{j}", 1))
                    else:
                        dve.wait_ge(panel_used, n.after("used", 4 * half + 2))
                    dve.wait_ge(bank_empty[4 + j], n.after(f"empty{4 + j}", 1))
                    dve.scalar_tensor_tensor(cvg[:, j, TAPS - 1:], bank[j][:, 0:L],
                                             cols[:, bass.ds(i * 4 + (COL["b_a"] + j), 1)], sig[:, j, :],
                                             ALU.add, ALU.mult).then_inc(bank_empty[j], 1)

            def conv(i, half):
                for tap in range(TAPS):
                    for j in (2 * half, 2 * half + 1):
                        w = cols[:, bass.ds(i * (4 * TAPS) + (COL["w_dw"] + j * TAPS + tap), 1)]
                        u = cvg[:, j, META + tap:META + tap + T]
                        if tap == 0:
                            dve.wait_ge(bank_empty[j], n.after(f"empty{j}", 1))
                            b = cols[:, bass.ds(i * 4 + (COL["b_dw"] + j), 1)]
                            step(dve.tensor_scalar(cacc[:, j, :], u, w, b, ALU.mult, ALU.add))
                            continue
                        settled(1)
                        if tap < TAPS - 1:
                            step(dve.scalar_tensor_tensor(cacc[:, j, :], u, w, cacc[:, j, :], ALU.mult, ALU.add))
                        else:
                            step(dve.scalar_tensor_tensor(
                                cvo[:, bass.ds(i * 4 + j, 1), :].rearrange("p a t -> p (a t)"), u, w, cacc[:, j, :],
                                ALU.mult, ALU.add))
                settled()
                dve.memset(stat[:, 7:8], 1.0).then_inc(conv_ready, 1)

            with n.rounds(dve, "w_in", 4, dve_step=4 * TAPS) as i:
                for half in range(2):
                    glu(i, half)
                    conv(i, half)
            split_lo(-1)

            with n.rounds(dve, "ln"):
                dve.wait_ge(bank_full[0], n.after("full0", 1))
                dve.tensor_scalar(mean[:, :], bank[0][:, 0:T], 1.0 / D, None, ALU.mult).then_inc(bank_empty[0], 1)
                dve.wait_ge(bank_empty[0], n.after("empty0", 1))
                for g in range(4):
                    four = cvo[:, 4 * g:4 * g + 4, :]
                    dve.tensor_tensor(four, four, mean[:, :].unsqueeze(1).to_broadcast([128, 4, T]), ALU.subtract)\
                        .then_inc(dev_ready, 1)
                dve.wait_ge(bank_full[1], n.after("full1", 1))
                dve.tensor_scalar(rstd[:, :], bank[1][:, 0:T], 1.0 / D, LN_EPS, ALU.mult, ALU.add).then_inc(bank_empty[1], 1)
                dve.wait_ge(root_ready, n.after("root", 1))
                link(dve.reciprocal(rstd[:, :], rstd[:, :]))
                for g in range(4):
                    four = cvo[:, 4 * g:4 * g + 4, :]
                    dve.tensor_tensor(four, four, rstd[:, :].unsqueeze(1).to_broadcast([128, 4, T]), ALU.mult)\
                        .then_inc(ln_ready, 1)
                for g in range(4):
                    dve.wait_ge(silu_hi, n.after("silu_hi", g + 1))
                    dve.tensor_tensor(a_lo[:, 4 * g:4 * g + 4, 0:T], sq[:, 4 * g:4 * g + 4, :],
                                      a_hi[:, 4 * g:4 * g + 4, 0:T].bitcast(f32), ALU.subtract).then_inc(act_ready, 1)

            dve.wait_ge(rows_loaded, 48)
            with n.rounds(dve, "w_out", 4) as i:
                for c in range(4):
                    split_lo(c)
                for t in range(TT):
                    if t == 0:
                        dve.wait_ge(bank_full[0], n.after("full0", 1))
                    else:
                        dve.wait_ge(panel_used, n.after("used", 4))
                    dve.tensor_tensor(yrow[:, t, bass.ds(i * 512, 512)], bank[t][:, :], bout_row[:, bass.ds(i * 512, 512)],
                                      ALU.add).then_inc(bank_empty[t], 1)

            def post(row, gain):
                mean_square(1)
                for t in range(TT):
                    step(dve.tensor_tensor(gained[:, t, :], yrow[:, t, :], row[:, :], ALU.mult))
                dve.wait_ge(root_ready, n.after("root", 1))
                link(dve.reciprocal(stat[:, 4:4 + TT], stat[:, 4:4 + TT]))
                for t in range(TT):
                    dve.scalar_tensor_tensor(xres[:, t, :], gained[:, t, :], stat[:, 4 + t:5 + t], xres[:, t, :],
                                             ALU.mult, ALU.add).then_inc(res_ready, 1)
                mean_square(2)
                inverse(2)
                transposed_lo(gain, 0)

            with n.rounds(dve, "post"):
                post(gmix_row, "g_ffn")
            for t in range(TT):
                link(dve.memset(yrow[:, t, :], 0.0))

            with n.rounds(dve, "ffn", FF // 512):
                for blk in range(2):
                    c0 = 4 * blk
                    for c in range(4):
                        split_lo(c0 + c)
                    for j in range(2):
                        f, b = 2 * blk + j, c0 + 2 + j
                        dve.wait_ge(bank_empty[c0 + j], n.after(f"empty{c0 + j}", 1))
                        if j == 0:
                            dve.wait_ge(bank_full[b], n.after(f"full{b}", 1))
                        else:
                            dve.wait_ge(panel_used, n.after("used", c0 + 4))
                        dve.tensor_tensor(hf[:, f, :], sg[:, j, :], bank[b][:, 0:T], ALU.mult).then_inc(bank_empty[b], 1)
                        dve.wait_ge(hhi_ready, n.after("hhi", f + 1))
                        dve.tensor_tensor(h_lo[:, f, :], hf[:, f, :], h_hi[:, f, :].bitcast(f32), ALU.subtract).then_inc(hlo_ready, 1)
                for c in range(8, 12):
                    split_lo(c)
                for b in range(8):
                    t, c = (1, b) if b < 4 else (0, b - 4)
                    if b == 7:
                        dve.wait_ge(panel_used, n.after("used", 12))
                    else:
                        dve.wait_ge(bank_full[b], n.after(f"full{b}", 1 if b % 2 else 2))
                    dst = yrow[:, t, c * 512:(c + 1) * 512]
                    dve.tensor_tensor(dst, dst, bank[b][:, :], ALU.add).then_inc(bank_empty[b], 1)

            with n.rounds(dve, "post"):
                post(gffn_row, "g_norm1")

            dve.wait_ge(wfhi_ready, 1)
            dve.tensor_tensor(wf_lo[:, :, :], wf_raw[:, :, :], wf_hi[:, :, :].bitcast(f32), ALU.subtract).then_inc(wflo_ready, 1)
            with n.rounds(dve, "qk", 4):
                for c in range(4):
                    split_lo(c)

            def log_sigmoid():
                with n.rounds(dve, "forget"):
                    for t in range(TT):
                        dve.wait_ge(bank_full[6 + t], n.after(f"full{6 + t}", 1))
                        dve.tensor_tensor(fg[:, 0, t * HEADS:(t + 1) * HEADS], bank[6 + t][:, 0:HEADS], fb[:, :], ALU.add)\
                            .then_inc(bank_empty[6 + t], 1)
                    dve.wait_ge(z_ln, n.after("z_ln", 1))
                    link(dve.tensor_scalar(fg[:, 3, :], fg[:, 1, :], 1.0, None, ALU.add))
                    step(dve.reciprocal(fg[:, 4, :], fg[:, 3, :]))
                    link(dve.tensor_scalar(fg[:, 5, :], fg[:, 3, :], -1.0, None, ALU.add))
                    link(dve.tensor_tensor(fg[:, 5, :], fg[:, 1, :], fg[:, 5, :], ALU.subtract))
                    link(dve.tensor_tensor(fg[:, 5, :], fg[:, 5, :], fg[:, 4, :], ALU.mult))
                    link(dve.tensor_tensor(fg[:, 2, :], fg[:, 2, :], fg[:, 5, :], ALU.add))
                    link(dve.tensor_scalar(fg[:, 3, :], fg[:, 0, :], 0.0, None, ALU.min))
                    dve.tensor_tensor(fg[:, 5, :], fg[:, 3, :], fg[:, 2, :], ALU.subtract).then_inc(logf_ready, 1)

            def head_norm(g, c):
                with n.rounds(dve, "qknorm"):
                    wait(dve, qkn_ready, n.after("qkn", 0))
                    for p in range(2):
                        dve.wait_ge(bank_full[6 + p], n.after(f"full{6 + p}", 1))
                        dve.tensor_scalar(qrs[:, 2 * p:2 * p + 2, :].rearrange("p a t -> p (a t)"), bank[6 + p][:, :],
                                          1.0 / HD, RMS_EPS, ALU.mult, ALU.add).then_inc(bank_empty[6 + p], 1)
                    split_lo(c)
                    dve.wait_ge(root_ready, n.after("root", 1))
                    link(dve.reciprocal(qrs[:, :, :], qrs[:, :, :]))
                    four = qk[:, 4 * g:4 * g + 4, :]
                    link(dve.tensor_tensor(four, four, qrs[:, :, :], ALU.mult))
                    dve.tensor_scalar(four, four, col("g_q" if g < 2 else "g_k", 0), None, ALU.mult).then_inc(qkn_ready, 1)

            for r in range(2):
                with n.rounds(dve, "pin"):
                    split_lo(0)
                    if r == 0:
                        log_sigmoid()
                    head_norm(2 * r, 1)
                    split_lo(2)
                    head_norm(2 * r + 1, 3)

            def cumulative_keys():
                for t in range(TT):
                    for h in range(HEADS):
                        ins = dve.tensor_scalar(lfb[:, t, h, :], ones[:, :], fg[:, 5, t * HEADS + h:t * HEADS + h + 1], None, ALU.mult)
                ins.then_inc(lfb_ready, 1)

            def cumulative_queries():
                dve.wait_ge(bank_full[6], n.after("full6", 1))
                dve.tensor_copy(cq[:, :], bank[6][:, 0:TT * HEADS]).then_inc(bank_empty[6], 1)
                dve.wait_ge(bank_empty[6], n.after("empty6", 1))

            def scores(r):
                with n.rounds(dve, "score"):
                    for e in range(2):
                        h = 2 * r + e
                        dve.wait_ge(bank_full[e], n.after(f"full{e}", 1))
                        dve.wait_ge(bank_empty[2 + e], n.after(f"empty{2 + e}", 0))
                        dve.tensor_scalar(bias_t[:, e, 0:128], bank[e][:, 0:128], -1.0, cq[:, h:h + 1], ALU.mult, ALU.add)
                        dve.tensor_scalar(bias_t[:, e, 128:384], bank[e][:, 0:256], -1.0, cq[:, HEADS + h:HEADS + h + 1],
                                          ALU.mult, ALU.add).then_inc(bank_empty[e], 1)
                        dve.wait_ge(bank_empty[e], n.after(f"empty{e}", 1))
                        dve.wait_ge(bank_full[2 + e], n.after(f"full{2 + e}", 1))
                        dve.scalar_tensor_tensor(lg0[:, h, :], bank[2 + e][:, 0:128], HD ** -0.5, bias_t[:, e, 0:128],
                                                 ALU.mult, ALU.add)
                        dve.scalar_tensor_tensor(lg1[:, h, :], bank[2 + e][:, 128:384], HD ** -0.5, bias_t[:, e, 128:384],
                                                 ALU.mult, ALU.add).then_inc(bank_empty[2 + e], 1)

            mask = causal[:, :].unsqueeze(1).to_broadcast([128, HEADS, 128])
            with n.rounds(dve, "v"):
                with n.rounds(dve, "cum"):
                    split_lo(0)
                    cumulative_keys()
                    split_lo(1)
                    cumulative_queries()
                split_lo(2)
                scores(0)
                split_lo(3)
                scores(1)
            with n.rounds(dve, "v"):
                split_lo(0)
                scores(2)
                split_lo(1)
                scores(3)
                split_lo(2)
                dve.wait_ge(bank_empty[3], n.after("empty3", 0))
                link(dve.tensor_tensor(lg0[:, :, :], lg0[:, :, :], mask, ALU.add))
                step(dve.tensor_reduce(negmax[:, 0:HEADS], lg0[:, :, :], AX.X, ALU.max))
                split_lo(3)
                link(dve.tensor_tensor(lg1[:, :, 128:256], lg1[:, :, 128:256], mask, ALU.add))
                link(dve.tensor_reduce(negmax[:, HEADS:2 * HEADS], lg1[:, :, :], AX.X, ALU.max))
                dve.tensor_scalar(negmax[:, :], negmax[:, :], -1.0, None, ALU.mult).then_inc(negmax_ready, 1)

            def pooled(half):
                for j in range(4 * half, 4 * half + 4):
                    b = 4 + j % 4
                    dve.wait_ge(evac_hi, n.after("evac", j + 1))
                    dve.scalar_tensor_tensor(po_lo[:, j, :], bank[b][:, 0:T], col("pool_scale", j), po_hi[:, j, :].bitcast(f32),
                                             ALU.mult, ALU.subtract).then_inc(bank_empty[b], 1)

            def branches(i):
                def merged_tile(j):
                    return merged[:, bass.ds(i * 4 + j, 1), :].rearrange("p a t -> p (a t)")

                split_lo(0)
                split_lo(1)
                for j in range(4):
                    if j < 3:
                        dve.wait_ge(bank_full[j], n.after(f"full{j}", 1))
                    else:
                        dve.wait_ge(panel_used, n.after("used", 2))
                    dve.wait_ge(bank_empty[j], n.after(f"empty{j}", 0))
                    dve.tensor_tensor(merged_tile(j), merged_tile(j), bank[j][:, 0:T], ALU.mult).then_inc(bank_empty[j], 1)
                split_lo(2)
                split_lo(3)
                for j in range(4):
                    if j < 3:
                        dve.wait_ge(bank_full[4 + j], n.after(f"full{4 + j}", 1))
                    else:
                        dve.wait_ge(panel_used, n.after("used", 4))
                    dve.wait_ge(bank_empty[4 + j], n.after(f"empty{4 + j}", 0))
                    dve.tensor_tensor(gate1[:, j, :], gate1[:, j, :], bank[4 + j][:, 0:T], ALU.mult).then_inc(bank_empty[4 + j], 1)
                for j in range(4):
                    dve.wait_ge(bank_empty[4 + j], n.after(f"empty{4 + j}", 1))
                    dve.tensor_tensor(merged_tile(j), merged_tile(j), gate1[:, j, :], ALU.add).then_inc(part_ready, 1)
                dve.wait_ge(part_ready, n.after("part", 4))

            with n.rounds(dve, "gates_0"):
                with n.rounds(dve, "pool"):
                    split_lo(0)
                    split_lo(1)
                    with n.rounds(dve, "softmax"):
                        dve.wait_ge(exp_ready, n.after("exp", 1))
                        link(dve.reciprocal(den[:, :], den[:, :]))
                        dve.tensor_tensor(lg0[:, :, :], lg0[:, :, :], den[:, 0:HEADS].unsqueeze(2).to_broadcast([128, HEADS, 128]),
                                          ALU.mult).then_inc(prob_ready, 1)
                        dve.tensor_tensor(lg1[:, :, :], lg1[:, :, :], den[:, HEADS:].unsqueeze(2).to_broadcast([128, HEADS, 256]),
                                          ALU.mult).then_inc(prob_ready, 1)
                    split_lo(2)
                    pooled(0)
                    split_lo(3)
                    pooled(1)
            with n.rounds(dve, "gates_1"):
                for r in range(HEADS // 2):
                    with n.rounds(dve, "heads"):
                        split_lo(r)
                        for e in range(2):
                            dve.wait_ge(evac_hi, n.after("evac", e + 1))
                            dve.tensor_tensor(at_lo[:, 2 * r + e, :], bank[2 + e][:, 0:T], at_hi[:, 2 * r + e, :].bitcast(f32),
                                              ALU.subtract).then_inc(bank_empty[2 + e], 1)
            with n.rounds(dve, "branches"):
                branches(0)
            with n.rounds(dve, "merge", 3) as i:
                for stage in ("gates_0", "gates_1"):
                    with n.rounds(dve, stage):
                        for c in range(4):
                            split_lo(c)
                with n.rounds(dve, "branches"):
                    branches(i + 1)
            with n.rounds(dve, "merged"):
                for g in range(4):
                    dve.wait_ge(merged_hi, n.after("merged_hi", g + 1))
                    dve.tensor_tensor(a_lo[:, 4 * g:4 * g + 4, 0:T], merged[:, 4 * g:4 * g + 4, :],
                                      a_hi[:, 4 * g:4 * g + 4, 0:T].bitcast(f32), ALU.subtract).then_inc(act_ready, 1)
            with n.rounds(dve, "w_out_2", 4) as i:
                for c in range(4):
                    split_lo(c)
                for t in range(TT):
                    if t == 0:
                        dve.wait_ge(bank_full[0], n.after("full0", 1))
                    else:
                        dve.wait_ge(panel_used, n.after("used", 4))
                    dst = xres[:, t, bass.ds(i * 512, 512)]
                    dve.tensor_tensor(dst, dst, bank[t][:, :], ALU.add).then_inc(bank_empty[t], 1)
            with n.rounds(dve, "post_2"):
                mean_square(1)
                inverse(1)
                dve.wait_ge(late_loaded, 32)
                for t in range(TT):
                    dve.wait_ge(xs_ready, n.after("xs", t + 1))
                    dve.tensor_tensor(xn[:, t, :], xs[:, t, :], g2_row[:, :], ALU.mult).then_inc(xn_ready, 1)
                transposed_lo(None, 0)
            with n.rounds(dve, "query", 2):
                for c in range(4):
                    split_lo(c)
            def apart():
                dve.sem_inc(dve_passed, 1)

            def sixteen(values, indices, src, rest):
                apart()
                link(dve.max(values[:, 0:8], src))
                apart()
                step(dve.max_index(indices[:, 0:8], values[:, 0:8], src))
                link(dve.match_replace(rest, values[:, 0:8], src, LOWEST))
                apart()
                link(dve.max(values[:, 8:16], rest))
                apart()
                link(dve.max_index(indices[:, 8:16], values[:, 8:16], rest))

            square = [128, TOPK, TOPK]

            def best_keys(th, halves):
                if 0 in halves:
                    link(dve.tensor_copy(sc[:, :], score[:, bass.ds(th, 1), :].rearrange("p a k -> p (a k)")))
                for half in halves:
                    sixteen(val[:, half * TOPK:(half + 1) * TOPK], ind[:, half * TOPK:(half + 1) * TOPK],
                            sc[:, half * NKEYS:(half + 1) * NKEYS], sc_rest[:, :])

            def best_pairs():
                step(dve.tensor_copy(indf[:, :], ind[:, :]))
                grid = cand[:, :].rearrange("p (a b) -> p a b", a=TOPK)
                link(dve.tensor_tensor(grid, val[:, 0:TOPK].unsqueeze(2).to_broadcast(square),
                                       val[:, TOPK:].unsqueeze(1).to_broadcast(square), ALU.add))
                sixteen(top[:, :], pos[:, :], cand[:, :], cand_rest[:, :])
                dve.tensor_scalar(gsum[:, 0:1], top[:, 0:1], -1.0, None, ALU.mult).then_inc(gate_max, 1)

            def pairs_experts(parity, free):
                link(dve.tensor_scalar(pos1[:, :], pos[:, :], 4, None, ALU.logical_shift_right))
                step(dve.tensor_copy(posf[:, 0:TOPK], pos1[:, :]))
                link(dve.tensor_scalar(pos[:, :], pos[:, :], TOPK - 1, None, ALU.bitwise_and))
                link(dve.tensor_copy(posf[:, TOPK:], pos[:, :]))
                picks = pick[:, :].rearrange("p (k a) -> p k a", a=TOPK)
                for half in range(2):
                    part = slice(half * TOPK, (half + 1) * TOPK)
                    link(dve.tensor_tensor(picks, iota_f[:, :].unsqueeze(1).to_broadcast(square),
                                           posf[:, part].unsqueeze(2).to_broadcast(square), ALU.is_equal))
                    link(dve.tensor_tensor(picks, picks, indf[:, part].unsqueeze(1).to_broadcast(square), ALU.mult))
                    link(dve.tensor_reduce(chosen[:, part], picks, AX.X, ALU.add))
                link(dve.scalar_tensor_tensor(expert_f[:, :], chosen[:, 0:TOPK], float(NKEYS), chosen[:, TOPK:], ALU.mult, ALU.add))
                wait(dve, v_used, free)
                dve.tensor_copy(expert[parity][:, :], expert_f[:, :]).then_inc(expert_ready, 1)

            def gates_softmax(parity, k):
                dve.wait_ge(gate_exp, n.after("gate_exp", k))
                link(dve.reciprocal(gsum[:, 2:3], gsum[:, 1:2]))
                link(dve.tensor_scalar(gate[parity][:, :], gate[parity][:, :], gsum[:, 2:3], None, ALU.mult))

            def route(th, parity, k, free):
                best_keys(th, (0, 1))
                best_pairs()
                pairs_experts(parity, free)
                gates_softmax(parity, k)

            def heads(th, t, more=True):
                for e in range(2):
                    for q in range(TOPK // BATCH):
                        if q == 2 and (more or e == 0):
                            route(th + (e + 1), 1 - e, e + 1, n.after("v_used", e * TOPK))
                        for s in range(q * BATCH, (q + 1) * BATCH):
                            dve.wait_ge(u_loaded[s % NU], n.after("u_rows", e * 4 + s // NU + 1) * 16)
                            dve.tensor_tensor_reduce(out=u_slot[s % NU][:, :], in0=u_slot[s % NU][:, :], in1=xn[:, t, :],
                                                     scale=1.0, scalar=0.0, op0=ALU.mult, op1=ALU.add,
                                                     accum_out=adot[e][:, s:s + 1]).then_inc(dot_ready, 1)
                        part = slice(q * BATCH, (q + 1) * BATCH)
                        dve.wait_ge(gelu_ready, n.after("gelu", e * 4 + q + 1))
                        dve.tensor_tensor(hid[e][:, part], gelu[e][:, part], gate[e][:, part], ALU.mult).then_inc(hid_ready, 1)

            dve.wait_ge(iota_ready, 1)
            link(dve.tensor_copy(iota_f[:, :], iota_i[:, :]))
            with n.rounds(dve, "keys_0"):
                stored_0 = n.after("empty4", 1)
            with n.rounds(dve, "query"):
                split_lo(0)
                split_lo(1)
                dve.wait_ge(bank_empty[4], stored_0)
                best_keys(0, (0,))
                split_lo(2)
                best_keys(0, (1,))
                split_lo(3)
            with n.rounds(dve, "query"):
                split_lo(0)
                best_pairs()
                split_lo(1)
                split_lo(2)
            with n.rounds(dve, "keys"):
                stored_all = n.after("empty7", 1)
            with n.rounds(dve, "route"):
                pairs_experts(0, 0)
                gates_softmax(0, 1)
            dve.wait_ge(bank_empty[7], stored_all)
            links = 2 * PER_ROUTE
            with n.rounds(dve, "pair"):
                heads(0, 0)
            with n.rounds(dve, "pair", 3, dve_step=links) as i:
                heads(i * 2 + 2, 0)
            with n.rounds(dve, "pair", 3, dve_step=links) as i:
                heads(i * 2 + 8, 1)

            def result(t):
                dve.wait_ge(acc_done, t + 1)
                for c in range(4):
                    part = slice(c * 512, (c + 1) * 512)
                    ins = dve.tensor_tensor(out_row[:, t, part], xres[:, t, part], bank[4 * t + c][:, :], ALU.add)
                ins.then_inc(out_ready, 1)

            result(0)
            with n.rounds(dve, "pair"):
                heads(14, 1, more=False)
            result(1)

        @block.tensor
        def _(pe):
            n = Counts()

            def into(b, k):
                wait(pe, bank_empty[b], n.after(f"empty{b}", k))

            def panel(c, conv=False):
                if conv:
                    pe.wait_ge(conv_split, n.after("conv_split", c + 1))
                else:
                    pe.wait_ge(split_ready, n.after("split", c))
                return c % 2

            def product(dst, left, right, start, stop):
                pe.matmul(dst, left[0], right[0], start=start, stop=False)
                pe.matmul(dst, left[0], right[1], start=False, stop=False)
                return pe.matmul(dst, left[1], right[0], start=False, stop=stop)

            def transposes(src, ready, key):
                for t in range(TT):
                    pe.wait_ge(ready, n.after(key, t + 1))
                    for b in range(4):
                        into(4 * t + b, 0)
                        for q in range(4):
                            k = 4 * b + q
                            ins = pe.transpose(bank[4 * t + b][:, q * 128:(q + 1) * 128], src[:, t, k * 128:(k + 1) * 128], ident[:, :])
                        ins.then_inc(bank_full[4 * t + b], 1)

            def feature_major(banks, tokens, c0, panels, kper, k, conv=False, only=None, ready=None):
                width = len(banks) * 128
                for c in only or range(panels):
                    s = panel(c0 + c, conv)
                    for j, b in enumerate(banks):
                        for kk in range(kper):
                            kt = c * kper + kk
                            if kt == 0:
                                into(b, k)
                            if ready and j == 0 and kt % 4 == 0:
                                pe.wait_ge(bank_empty[4 + kt // 4], ready[kt // 4])
                            where = slice(kk * width + j * 128, kk * width + (j + 1) * 128)
                            right = tokens(kt)
                            ins = product(bank[b][:, 0:right[0].shape[-1]], (w_hi[s][:, where], w_lo[s][:, where]), right,
                                          kt == 0, kt == panels * kper - 1)
                        if j == len(banks) - 1:
                            ins.then_inc(panel_used, 1)
                        elif c == panels - 1:
                            ins.then_inc(bank_full[b], 1)

            def token_major(banks, only=range(4), ready=None):
                for c in only:
                    if ready:
                        ready(c)
                    s = panel(c)
                    for t, b in enumerate(banks):
                        for kk in range(4):
                            kt = c * 4 + kk
                            if kt == 0:
                                into(b, 0)
                            tile, where = slice(t * 128, (t + 1) * 128), slice(kk * 512, (kk + 1) * 512)
                            ins = product(bank[b][:, :], (a_hi[:, kt, tile], a_lo[:, kt, tile]),
                                          (w_hi[s][:, where], w_lo[s][:, where]), kt == 0, kt == KT - 1)
                        if t == TT - 1:
                            ins.then_inc(panel_used, 1)
                        elif c == 3:
                            ins.then_inc(bank_full[b], 1)

            def all_tokens(k):
                return a_hi[:, k, :], a_lo[:, k, :]

            def tokens(k):
                return a_hi[:, k, 0:T], a_lo[:, k, 0:T]

            pe.wait_ge(const_ready, 3)
            with n.rounds(pe, "norm0"):
                transposes(xs0, xs_ready, "xs")
                pe.wait_ge(xs_ready, n.after("xs", TT + 1))
                into(0, 1)
                for k in range(KT):
                    ins = pe.transpose(bank[0][:, k * META:(k + 1) * META], meta_sb[:, k * 128:(k + 1) * 128], ident[0:META, 0:META])
                ins.then_inc(panel_used, 1)
            into(0, 0)
            with n.rounds(pe, "w_in", 4):
                for half in range(2):
                    feature_major((2 * half, 2 * half + 1), all_tokens, 4 * half, 2, 8, 0, True)
                    feature_major((4 + 2 * half, 5 + 2 * half), all_tokens, 4 * half + 2, 2, 8, 0, True)
            with n.rounds(pe, "ln"):
                into(0, 0)
                for k in range(KT):
                    if k in (0, KT - 2):
                        pe.wait_ge(conv_ready, KT // 2 - (k == 0))
                    ins = pe.matmul(bank[0][:, 0:T], ones[:, :], cvo[:, k, :], start=k == 0, stop=k == KT - 1)
                ins.then_inc(bank_full[0], 1)
                into(1, 0)
                for k in range(KT):
                    if k % 4 == 0:
                        pe.wait_ge(dev_sq_ready, n.after("dev_sq", k // 4 + 1))
                    ins = pe.matmul(bank[1][:, 0:T], ones[:, :], sq[:, k, :], start=k == 0, stop=k == KT - 1)
                ins.then_inc(bank_full[1], 1)
            with n.rounds(pe, "w_out", 4):
                token_major((0, 1), ready=lambda c: pe.wait_ge(act_ready, c + 1))
            with n.rounds(pe, "post"):
                transposes(xs, xs_ready, "xs")
            ready = [n.after(f"empty{b}", 0) for b in range(4, 8)]
            with n.rounds(pe, "ffn", FF // 512):
                for blk in range(2):
                    feature_major((4 * blk, 4 * blk + 1), tokens, 4 * blk, 2, 8, 0, ready=None if blk else ready)
                    feature_major((4 * blk + 2, 4 * blk + 3), tokens, 4 * blk + 2, 2, 8, 0)
                for f in range(4):
                    s = panel(8 + f)
                    pe.wait_ge(hlo_ready, n.after("hlo", f + 1))
                    for t in (1, 0):
                        for c in range(4):
                            b = c if t else 4 + c
                            if f == 0:
                                into(b, 1)
                            tile, where = slice(t * 128, (t + 1) * 128), slice(c * 512, (c + 1) * 512)
                            ins = product(bank[b][:, :], (h_hi[:, f, tile], h_lo[:, f, tile]),
                                          (w_hi[s][:, where], w_lo[s][:, where]), f == 0, f == 3)
                            if f == 3 and b < 7:
                                ins.then_inc(bank_full[b], 1)
                    ins.then_inc(panel_used, 1)
            with n.rounds(pe, "post"):
                transposes(xs, xs_ready, "xs")
            ready = [n.after(f"empty{b}", 0) for b in range(4, 8)]
            with n.rounds(pe, "qk", 4):
                feature_major((0, 1, 2, 3), tokens, 0, 4, 4, 0, ready=ready)
            with n.rounds(pe, "forget"):
                pe.wait_ge(wflo_ready, 1)
                for t in range(TT):
                    into(6 + t, 0)
                    for k in range(KT):
                        tile = slice(t * 128, (t + 1) * 128)
                        ins = product(bank[6 + t][:, 0:HEADS], (a_hi[:, k, tile], a_lo[:, k, tile]),
                                      (wf_hi[:, k, :], wf_lo[:, k, :]), k == 0, k == KT - 1)
                    ins.then_inc(bank_full[6 + t], 1)
            def head_norm():
                with n.rounds(pe, "qknorm"):
                    pe.wait_ge(qsq_ready, n.after("qsq", 1))
                    for p in range(2):
                        into(6 + p, 0)
                        pe.matmul(bank[6 + p][:, :], ones[:, :], qsq[:, 2 * p:2 * p + 2, :], start=True, stop=True)\
                            .then_inc(bank_full[6 + p], 1)

            def first_four(*only):
                feature_major((0, 1, 2, 3), tokens, 0, 4, 4, 0, only=only)

            for r in range(2):
                with n.rounds(pe, "pin"):
                    first_four(0)
                    head_norm()
                    first_four(1, 2)
                    head_norm()
                    first_four(3)

            def cumulative():
                with n.rounds(pe, "cum"):
                    pe.wait_ge(logf_ready, 1)
                    into(6, 0)
                    first, second = fg[:, 5, 0:HEADS], fg[:, 5, HEADS:2 * HEADS]
                    pe.matmul(bank[6][:, 0:HEADS], tri_ones[:, 0:128], first, start=True, stop=True)
                    pe.matmul(bank[6][:, HEADS:2 * HEADS], ones[:, :], first, start=True, stop=False)
                    pe.matmul(bank[6][:, HEADS:2 * HEADS], tri_ones[:, 0:128], second, start=False, stop=True).then_inc(bank_full[6], 1)
                    lfb_done = n.after("lfb", 1)
                return lfb_done

            def scores(r):
                with n.rounds(pe, "score"):
                    for e in range(2):
                        h = 2 * r + e
                        into(e, 0)
                        pe.matmul(bank[e][:, 0:256], lfb[:, 0, h, :], tri_ones[:, :], start=True, stop=False)
                        pe.matmul(bank[e][:, 128:256], lfb[:, 1, h, :], tri_ones[:, 0:128], start=False, stop=True).then_inc(bank_full[e], 1)
                        into(2 + e, 0)
                        pe.matmul(bank[2 + e][:, 0:128], qk[:, h, 0:128], qk[:, HEADS + h, 0:128], start=True, stop=True)
                        pe.matmul(bank[2 + e][:, 128:384], qk[:, h, 128:256], qk[:, HEADS + h, :], start=True, stop=True)\
                            .then_inc(bank_full[2 + e], 1)

            for r in range(2):
                with n.rounds(pe, "v"):
                    for c in range(4):
                        token_major((4, 5), (c,))
                        if 4 * r + c == 0:
                            lfb_done = cumulative()
                        elif 2 <= 4 * r + c < 6:
                            if 4 * r + c == 2:
                                pe.wait_ge(lfb_ready, lfb_done)
                                pe.wait_ge(qkn_ready, n.after("qkn", 0))
                            scores(4 * r + c - 2)
            n.past("softmax")

            def pooled(half):
                for j in range(4 * half, 4 * half + 4):
                    b, g = 4 + j % 4, j // 2
                    pe.wait_ge(mixed_ready, n.after("mixed", g + 1))
                    into(b, half)
                    for ci in range(2):
                        ins = pe.matmul(bank[b][:, 0:T], group_sb[:, g, ci, (j % 2) * 128:(j % 2 + 1) * 128], mixed[:, 2 * g + ci, :],
                                        start=ci == 0, stop=ci == 1)
                    ins.then_inc(bank_full[b], 1)

            def gates_1(only=None):
                feature_major((4, 5, 6, 7), tokens, 0, 4, 4, 0, only=only)

            def branches():
                feature_major((0, 1, 2, 3), lambda k: (at_hi[:, k, :], at_lo[:, k, :]), 0, 2, 4, 0)
                feature_major((4, 5, 6, 7), lambda k: (po_hi[:, k, :], po_lo[:, k, :]), 2, 2, 4, 0)

            with n.rounds(pe, "gates_0"):
                with n.rounds(pe, "pool"):
                    first_four(0, 1)
                    pooled(0)
                    first_four(2, 3)
                    pooled(1)
            pe.wait_ge(prob_ready, 2)
            with n.rounds(pe, "gates_1"):
                for r in range(HEADS // 2):
                    with n.rounds(pe, "heads"):
                        for e in range(2):
                            h = 2 * r + e
                            into(e, 0)
                            pe.transpose(bank[e][:, 0:128], lg0[:, h, :], ident[:, :])
                            pe.transpose(bank[e][:, 128:256], lg1[:, h, 0:128], ident[:, :])
                            pe.transpose(bank[e][:, 256:384], lg1[:, h, 128:256], ident[:, :]).then_inc(bank_full[e], 1)
                        gates_1((r,))
                        for e in range(2):
                            h = 2 * r + e
                            head = slice(h * HD, (h + 1) * HD)
                            into(e, 1)
                            into(2 + e, 0)
                            pe.matmul(bank[2 + e][:, 0:T], vrow[:, 0, head], pts[:, e, 0:256], start=True, stop=False)
                            pe.matmul(bank[2 + e][:, 128:256], vrow[:, 1, head], pts[:, e, 256:384], start=False, stop=True)\
                                .then_inc(bank_full[2 + e], 1)
            into(3, 0)
            with n.rounds(pe, "branches"):
                branches()
            with n.rounds(pe, "merge", 3):
                with n.rounds(pe, "gates_0"):
                    first_four(0, 1, 2, 3)
                with n.rounds(pe, "gates_1"):
                    gates_1()
                with n.rounds(pe, "branches"):
                    branches()
            n.past("merged")
            with n.rounds(pe, "w_out_2", 4):
                token_major((0, 1), ready=lambda c: pe.wait_ge(act_ready, 4 + c + 1))
            with n.rounds(pe, "post_2"):
                transposes(xn, xn_ready, "xn")
            ready = [n.after(f"empty{b}", 0) for b in range(4, 8)]

            def key_scores(t, two, b):
                into(b, 0)
                for hh in range(4 * two, 4 * two + 4):
                    q = hh % 4
                    ins = pe.matmul(bank[b][:, q * 128:(q + 1) * 128], qp[:, hh, t * 128:(t + 1) * 128], keys_sb[:, hh, :],
                                    start=True, stop=True)
                ins.then_inc(bank_full[b], 1)

            pe.wait_ge(late_loaded, 32)
            with n.rounds(pe, "query", 2):
                feature_major((0, 1, 2, 3), tokens, 0, 4, 4, 0, ready=ready)
            with n.rounds(pe, "keys_0"):
                key_scores(0, 0, 4)
            with n.rounds(pe, "query", 2):
                feature_major((0, 1, 2, 3), tokens, 0, 4, 4, 0)
            into(3, 0)
            with n.rounds(pe, "keys"):
                for t in range(TT):
                    for two in range(4):
                        if t or two:
                            key_scores(t, two, 4 * t + two)

            def nothing(t, start):
                for c in range(4):
                    ins = pe.matmul(bank[4 * t + c][:, :], zeros[:, :], xn[:, 0, 0:512], start=start, stop=not start)
                return ins

            def adds(t):
                for e in range(2):
                    for s in range(TOPK):
                        pe.wait_ge(diag_ready, n.after("diag", e * TOPK + s + 1))
                        pe.wait_ge(v_loaded[s % NV], n.after("v_rows", e * 2 + s // NV + 1) * 16)
                        for c in range(4):
                            ins = pe.matmul(bank[4 * t + c][:, :], diag[s % NDIAG][:, :], v_slot[s % NV][:, c * 512:(c + 1) * 512],
                                            start=False, stop=False)
                        ins.then_inc(v_used, 1)

            pe.wait_ge(zeros_ready, 1)
            for b in range(8):
                into(b, 0)
            for t in range(TT):
                nothing(t, True)
                with n.rounds(pe, "pair"):
                    adds(t)
                with n.rounds(pe, "pair", PH // 2 - 1):
                    adds(t)
                nothing(t, False).then_inc(acc_done, 1)


INPUTS = ("stream", "columns", "x", "meta", "b_out", "g_mix_post", "g_ffn_post", "g_norm2", "w_forget",
          "forget_bias", "group_w", "keys", "expert_u", "expert_v")


def laid_out(a):
    def wide(w):
        k, m = w.shape
        return w.reshape(k // 512, 4, 128, m // 512, 512).transpose(3, 0, 2, 1, 4).reshape(m // 512, k // 512, 128, 2048)

    def narrow(w):
        blocks = w.shape[1] // 256
        return w.reshape(2, 8, 128, blocks, 256).transpose(3, 0, 2, 1, 4).reshape(blocks, 2, 128, 2048)

    def column(v):
        return v.reshape(-1, 128).T

    w_in = narrow(a["conv_w_in"][0])
    first = np.concatenate([w_in[0:D // 256], w_in[D // 256:]], 1).reshape(-1, 128, 2048)
    gate_up = np.stack([narrow(a["ffn_w_gate"][0]), narrow(a["ffn_w_up"][0])], 1)
    ffn = np.concatenate([gate_up.reshape(FF // 512, 8, 128, 2048), a["ffn_w_down"][0].reshape(FF // 512, 4, 128, 2048)], 1)
    fox, w2 = HEADS * HD, a["w_in_2"][0]
    edges = [2 * fox, 3 * fox, 3 * fox + HEADS, 3 * fox + HEADS + POOL_W]
    w_qk, w_v, w_f, w_p, w_g = (w2[:, i:j] for i, j in zip([0] + edges, edges + [w2.shape[1]]))
    gates = wide(w_g)
    merge = np.concatenate([gates[0:4], gates[4:8], wide(a["w_branch_attn_2"][0]), wide(a["w_branch_pool_2"][0])], 1)
    flat = [w.reshape(-1, 128, 2048) for w in (wide(a["conv_w_out"][0]), ffn, wide(w_qk), wide(w_p), wide(w_v), merge,
                                               wide(a["w_out_2"][0]), wide(a["peer_w_query_2"][0]))]
    b_in = a["conv_b_in"][0]
    table = {"g_mix": column(a["norm_mix_pre"][0]), "b_a": column(b_in[:D]), "b_g": column(b_in[D:]),
             "w_dw": a["conv_w_dw"][0].reshape(TAPS, KT, 128).transpose(2, 1, 0).reshape(128, KT * TAPS),
             "b_dw": column(a["conv_b_dw"][0]), "ln_g": column(a["conv_ln_g"][0]), "ln_b": column(a["conv_ln_b"][0]),
             "g_ffn": column(a["norm_ffn_pre"][0]), "g_norm1": column(a["norm1_g_2"][0]),
             "g_q": column(a["q_norm_g_2"][0]), "g_k": column(a["k_norm_g_2"][0]), "pool_scale": column(a["pool_scale_2"][0])}
    keys = np.stack([a["peer_sub_keys_1_2"][0], a["peer_sub_keys_2_2"][0]], 1)
    return {
        "stream": np.concatenate([first] + flat, 0),
        "columns": np.concatenate([table[name] for name, _ in COLUMNS], 1),
        "x": a["x"][0], "meta": a["meta_tokens"], "b_out": a["conv_b_out"][0],
        "g_mix_post": a["norm_mix_post"][0], "g_ffn_post": a["norm_ffn_post"][0], "g_norm2": a["norm2_g_2"][0],
        "w_forget": w_f.reshape(KT, 128, HEADS).transpose(1, 0, 2),
        "forget_bias": a["forget_bias_2"][0],
        "group_w": a["pool_group_w_2"][0].reshape(4, 2, 128, 256).transpose(2, 0, 1, 3),
        "keys": keys.transpose(3, 0, 1, 2).reshape(128, 2 * PH, NKEYS),
        "expert_u": a["peer_expert_u_2"][0], "expert_v": a["peer_expert_v_2"][0],
    }


def kernel(**inputs):
    import concourse.bacc as bacc
    from concourse.bass_utils import run_bass_kernel_spmd

    nc = bacc.Bacc("TRN2", target_bir_lowering=False, num_devices=1)
    laid = laid_out({name: np.asarray(a) for name, a in inputs.items()})
    arrays, args = {}, []
    for name in INPUTS:
        a = np.ascontiguousarray(laid[name])
        arrays[f"in_{name}"] = a
        args.append(nc.dram_tensor(f"in_{name}", a.shape, mybir.dt.from_np(a.dtype), kind="ExternalInput").ap())
    args.append(nc.dram_tensor("out_0", (T, D), mybir.dt.float32, kind="ExternalOutput").ap())
    two_layers(nc, *args)
    r = run_bass_kernel_spmd(nc, [arrays], core_ids=[0])
    return r.results[0]["out_0"].reshape(1, T, D)
```
